# Optimizing a Trainium2 kernel written in Bass

```python
import functools
import jax, jax.numpy as jnp
from jax import lax
import numpy as np

D_MODEL = 1024
BATCH = 1
SEQ = 256
DEPTH = 1
DEC_BATCH = 8
DEC_SEQ = 1
PAST_LEN = 1024
PAGE_SIZE = 128

N_HEADS = 16
N_KV_HEADS = 2
HEAD_DIM = 64
GROUP = N_HEADS // N_KV_HEADS
WINDOW = 128
ATTN_W = N_HEADS * HEAD_DIM
KV_W = N_KV_HEADS * HEAD_DIM
D_RNN = 1280
N_RNN_BLOCKS = 10
RNN_BLOCK = D_RNN // N_RNN_BLOCKS
CONV_W = 4
LRU_C = 8.0
N_EXPERTS = 32
TOP_K = 4
D_FF = 1024
SWIGLU_LIMIT = 7.0
SWIGLU_ALPHA = 1.702
MOE_BLOCK = 128
LN_EPS = 1e-5
DEEPNORM_ALPHA = (2 * DEPTH) ** 0.25
DEEPNORM_BETA = (8 * DEPTH) ** -0.25
PROJ_SPLITS = [ATTN_W, KV_W, KV_W, D_RNN, D_RNN, D_MODEL, D_MODEL]
PROJ_W = sum(PROJ_SPLITS)

kernel_name = "hybrid_swa_rglru_moe_deepnorm_step"

def layer_norm(x, g, b):
    xf = x.astype(jnp.float32)
    mu = jnp.mean(xf, axis=-1, keepdims=True)
    var = jnp.mean(jnp.square(xf - mu), axis=-1, keepdims=True)
    return ((xf - mu) * lax.rsqrt(var + LN_EPS) * g + b).astype(x.dtype)

def alibi_slopes():
    h = jnp.arange(1, N_HEADS + 1, dtype=jnp.float32)
    return (2.0 ** (-8.0 * h / N_HEADS)).reshape(N_KV_HEADS, GROUP)

def window_attention(q, k, v, q_pos, k_pos, sinks):
    scale = HEAD_DIM ** -0.5
    scores = jnp.einsum('bnqhgd,bnshd->bnhgqs', q, k,
                        preferred_element_type=jnp.float32) * scale
    dist = (q_pos[:, :, None] - k_pos[:, None, :])
    valid = (dist >= 0) & (dist < WINDOW) & (k_pos[:, None, :] >= 0)
    slopes = alibi_slopes()[None, None, :, :, None, None]
    logits = scores - slopes * dist.astype(jnp.float32)[None, :, None, None]
    logits = jnp.where(valid[None, :, None, None], logits, -jnp.inf)
    sink = sinks.astype(jnp.float32).reshape(N_KV_HEADS, GROUP)[None, None, :, :, None, None]
    m = jnp.maximum(jnp.max(logits, axis=-1, keepdims=True), sink)
    p = jnp.exp(logits - m)
    denom = jnp.sum(p, axis=-1, keepdims=True) + jnp.exp(sink - m)
    probs = (p / denom).astype(v.dtype)
    return jnp.einsum('bnhgqs,bnshd->bnqhgd', probs, v)

def prompt_attend(q, k, v, sinks, cache_len):
    B, S = q.shape[:2]
    nb = S // WINDOW
    qb = q.reshape(B, nb, WINDOW, N_KV_HEADS, GROUP, HEAD_DIM)

    def band(t):
        tb = t.reshape(B, nb, WINDOW, N_KV_HEADS, HEAD_DIM)
        prev = jnp.pad(tb[:, :-1], ((0, 0), (1, 0), (0, 0), (0, 0), (0, 0)))
        return jnp.concatenate([prev, tb], axis=2)

    pos = jnp.arange(S, dtype=jnp.int32).reshape(nb, WINDOW)
    kpos = jnp.concatenate([pos - WINDOW, pos], axis=1)
    o = window_attention(qb, band(k), band(v), pos, kpos, sinks)
    return o.reshape(B, S, ATTN_W), k[:, S - cache_len:], v[:, S - cache_len:]

def sample_attend(q, k, v, sinks, ck, cv):
    B, T = q.shape[:2]
    cw = ck.shape[1]
    keys = jnp.concatenate([ck.astype(k.dtype), k], axis=1)
    vals = jnp.concatenate([cv.astype(v.dtype), v], axis=1)
    qpos = PAST_LEN + jnp.arange(T, dtype=jnp.int32)
    kpos = PAST_LEN - cw + jnp.arange(cw + T, dtype=jnp.int32)
    o = window_attention(q.reshape(B, 1, T, N_KV_HEADS, GROUP, HEAD_DIM),
                         keys[:, None], vals[:, None], qpos[None], kpos[None], sinks)
    return o.reshape(B, T, ATTN_W), keys[:, -cw:], vals[:, -cw:]

def rglru_branch(xr, conv_buf, h0, conv_w, conv_b, wa, ba, wx, bx, lam):
    B, T, _ = xr.shape
    xp = jnp.concatenate([conv_buf.astype(xr.dtype), xr], axis=1)
    xc = conv_b + xp[:, 0:T] * conv_w[0]
    for j in range(1, CONV_W):
        xc = xc + xp[:, j:j + T] * conv_w[j]
    new_buf = xp[:, T:]
    xcb = xc.reshape(B, T, N_RNN_BLOCKS, RNN_BLOCK)
    r = jax.nn.sigmoid(jnp.einsum('btnc,ncd->btnd', xcb, wa).reshape(B, T, D_RNN) + ba)
    i = jax.nn.sigmoid(jnp.einsum('btnc,ncd->btnd', xcb, wx).reshape(B, T, D_RNN) + bx)
    log_a = (-LRU_C * jax.nn.softplus(-lam.astype(jnp.float32))) * r.astype(jnp.float32)
    a = jnp.exp(log_a)
    b = jnp.sqrt(-jnp.expm1(2.0 * log_a)) * (i * xc).astype(jnp.float32)

    def step(h, ab):
        a_t, b_t = ab
        h = a_t * h + b_t
        return h, h

    h_last, hs = lax.scan(step, h0.astype(jnp.float32), (a.swapaxes(0, 1), b.swapaxes(0, 1)))
    return hs.swapaxes(0, 1).astype(xr.dtype), new_buf, h_last

def temporal_block(x, p, attend, conv_buf, h0):
    B, T, _ = x.shape
    proj = x @ p['w_in']
    offs = list(np.cumsum(PROJ_SPLITS)[:-1])
    q, k, v, xr, yr, ga, gb = jnp.split(proj, offs, axis=-1)
    q = q.reshape(B, T, N_HEADS, HEAD_DIM)
    k = k.reshape(B, T, N_KV_HEADS, HEAD_DIM)
    v = v.reshape(B, T, N_KV_HEADS, HEAD_DIM)
    o_attn, nk, nv = attend(q, k, v, p['attn_sinks'])
    y_rnn, new_buf, h_last = rglru_branch(xr, conv_buf, h0, p['conv_w'], p['conv_b'],
                                          p['rg_wa'], p['rg_ba'], p['rg_wx'], p['rg_bx'],
                                          p['rg_lambda'])
    y_rnn = y_rnn * jax.nn.gelu(yr)
    merged = (jax.nn.sigmoid(ga) * (o_attn @ p['w_attn_out'])
              + jax.nn.sigmoid(gb) * (y_rnn @ p['w_rnn_out']))
    return merged @ p['w_out'], nk, nv, new_buf, h_last

def moe(x, w_router, b_router, w_up, b_up, w_down, b_down):
    B, T, D = x.shape
    xt = x.reshape(-1, D)
    n_tok = xt.shape[0]
    logits = (xt @ w_router + b_router).astype(jnp.float32)
    top_v, top_i = lax.top_k(logits, TOP_K)
    gate = jax.nn.softmax(top_v, axis=-1)
    n = n_tok * TOP_K
    flat_e = top_i.reshape(-1).astype(jnp.int32)
    flat_tok = jnp.arange(n, dtype=jnp.int32) // TOP_K
    flat_g = gate.reshape(-1)
    order = jnp.argsort(flat_e)
    se = flat_e[order]
    counts = jnp.zeros((N_EXPERTS,), jnp.int32).at[flat_e].add(1)
    padded = (counts + MOE_BLOCK - 1) // MOE_BLOCK * MOE_BLOCK
    pad_end = jnp.cumsum(padded)
    pad_start = pad_end - padded
    start = jnp.cumsum(counts) - counts
    dest = pad_start[se] + jnp.arange(n, dtype=jnp.int32) - start[se]
    nb = -(-(n + N_EXPERTS * (MOE_BLOCK - 1)) // MOE_BLOCK)
    rows = nb * MOE_BLOCK
    row_tok = jnp.full((rows,), n_tok, jnp.int32).at[dest].set(flat_tok[order])
    row_g = jnp.zeros((rows,), jnp.float32).at[dest].set(flat_g[order])
    block_e = jnp.minimum(
        jnp.searchsorted(pad_end, jnp.arange(nb, dtype=jnp.int32) * MOE_BLOCK, side='right'),
        N_EXPERTS - 1).astype(jnp.int32)
    x_pad = jnp.concatenate([xt, jnp.zeros((1, D), xt.dtype)], axis=0)
    xb = x_pad[row_tok].reshape(nb, MOE_BLOCK, D)

    def expert_block(args):
        xblk, e = args
        h = xblk @ w_up[e] + b_up[e]
        glu, lin = h[:, :D_FF], h[:, D_FF:]
        glu = jnp.minimum(glu, SWIGLU_LIMIT)
        lin = jnp.clip(lin, -SWIGLU_LIMIT, SWIGLU_LIMIT)
        act = glu * jax.nn.sigmoid(SWIGLU_ALPHA * glu) * (lin + 1.0)
        return act @ w_down[e] + b_down[e]

    yb = lax.map(expert_block, (xb, block_e)).reshape(rows, D)
    y = jnp.zeros((n_tok + 1, D), jnp.float32).at[row_tok].add(
        yb.astype(jnp.float32) * row_g[:, None])[:n_tok]
    return y.astype(x.dtype).reshape(B, T, D)

def setup_inputs(seed: int = 0) -> dict:
    key = jax.random.key(seed)
    ks = jax.random.split(key, 28)
    f32 = jnp.float32

    def nrm(k, shape, s):
        return jax.random.normal(k, shape, f32) * s

    cw = min(WINDOW, PAST_LEN)
    beta = DEEPNORM_BETA
    col_scale = jnp.concatenate([
        jnp.ones((ATTN_W + KV_W,), f32), jnp.full((KV_W,), beta, f32),
        jnp.ones((2 * D_RNN + 2 * D_MODEL,), f32)])
    u = jax.random.uniform(ks[14], (DEPTH, D_RNN), f32, 0.9, 0.999)
    s = u ** (1.0 / LRU_C)
    return {
        "x_prompt": nrm(ks[0], (BATCH, SEQ, D_MODEL), 1.0),
        "x_sample": nrm(ks[1], (DEC_BATCH, DEC_SEQ, D_MODEL), 1.0),
        "cache_k": nrm(ks[2], (DEPTH, DEC_BATCH, cw, N_KV_HEADS, HEAD_DIM), 1.0),
        "cache_v": nrm(ks[3], (DEPTH, DEC_BATCH, cw, N_KV_HEADS, HEAD_DIM), beta),
        "state_conv": nrm(ks[4], (DEPTH, DEC_BATCH, CONV_W - 1, D_RNN), 1.0),
        "state_h": nrm(ks[5], (DEPTH, DEC_BATCH, D_RNN), 0.5),
        "w_in": nrm(ks[6], (DEPTH, D_MODEL, PROJ_W), D_MODEL ** -0.5) * col_scale,
        "attn_sinks": nrm(ks[7], (DEPTH, N_HEADS), 0.5),
        "conv_w": nrm(ks[8], (DEPTH, CONV_W, D_RNN), CONV_W ** -0.5),
        "conv_b": nrm(ks[9], (DEPTH, D_RNN), 0.02),
        "rg_wa": nrm(ks[10], (DEPTH, N_RNN_BLOCKS, RNN_BLOCK, RNN_BLOCK), RNN_BLOCK ** -0.5),
        "rg_ba": nrm(ks[11], (DEPTH, D_RNN), 0.02),
        "rg_wx": nrm(ks[12], (DEPTH, N_RNN_BLOCKS, RNN_BLOCK, RNN_BLOCK), RNN_BLOCK ** -0.5),
        "rg_bx": nrm(ks[13], (DEPTH, D_RNN), 0.02),
        "rg_lambda": jnp.log(s) - jnp.log1p(-s),
        "w_attn_out": nrm(ks[15], (DEPTH, ATTN_W, D_MODEL), beta * ATTN_W ** -0.5),
        "w_rnn_out": nrm(ks[16], (DEPTH, D_RNN, D_MODEL), beta * D_RNN ** -0.5),
        "w_out": nrm(ks[17], (DEPTH, D_MODEL, D_MODEL), beta * D_MODEL ** -0.5),
        "ln1_g": 1.0 + nrm(ks[18], (DEPTH, D_MODEL), 0.02),
        "ln1_b": nrm(ks[19], (DEPTH, D_MODEL), 0.02),
        "w_router": nrm(ks[20], (DEPTH, D_MODEL, N_EXPERTS), D_MODEL ** -0.5),
        "b_router": nrm(ks[21], (DEPTH, N_EXPERTS), 0.01),
        "w_up": nrm(ks[22], (DEPTH, N_EXPERTS, D_MODEL, 2 * D_FF), beta * D_MODEL ** -0.5),
        "b_up": nrm(ks[23], (DEPTH, N_EXPERTS, 2 * D_FF), 0.02),
        "w_down": nrm(ks[24], (DEPTH, N_EXPERTS, D_FF, D_MODEL), beta * D_FF ** -0.5),
        "b_down": nrm(ks[25], (DEPTH, N_EXPERTS, D_MODEL), 0.02),
        "ln2_g": 1.0 + nrm(ks[26], (DEPTH, D_MODEL), 0.02),
        "ln2_b": nrm(ks[27], (DEPTH, D_MODEL), 0.02),
    }

def reference(x_prompt, x_sample, cache_k, cache_v, state_conv, state_h,
              w_in, attn_sinks, conv_w, conv_b, rg_wa, rg_ba, rg_wx, rg_bx, rg_lambda,
              w_attn_out, w_rnn_out, w_out, ln1_g, ln1_b,
              w_router, b_router, w_up, b_up, w_down, b_down, ln2_g, ln2_b):
    cw = cache_k.shape[2]
    xp, xs = x_prompt, x_sample
    Bp, Bs = xp.shape[0], xs.shape[0]
    nk_p, nv_p, nc_p, nh_p = [], [], [], []
    nk_s, nv_s, nc_s, nh_s = [], [], [], []
    for l in range(DEPTH):
        p = {
            'w_in': w_in[l], 'attn_sinks': attn_sinks[l], 'conv_w': conv_w[l], 'conv_b': conv_b[l],
            'rg_wa': rg_wa[l], 'rg_ba': rg_ba[l], 'rg_wx': rg_wx[l], 'rg_bx': rg_bx[l],
            'rg_lambda': rg_lambda[l], 'w_attn_out': w_attn_out[l], 'w_rnn_out': w_rnn_out[l],
            'w_out': w_out[l],
        }
        moe_l = functools.partial(moe, w_router=w_router[l], b_router=b_router[l], w_up=w_up[l],
                                  b_up=b_up[l], w_down=w_down[l], b_down=b_down[l])
        mix_p, k_p, v_p, c_p, h_p = temporal_block(
            xp, p, functools.partial(prompt_attend, cache_len=cw),
            jnp.zeros((Bp, CONV_W - 1, D_RNN), xp.dtype), jnp.zeros((Bp, D_RNN), jnp.float32))
        xp = layer_norm(DEEPNORM_ALPHA * xp + mix_p, ln1_g[l], ln1_b[l])
        xp = layer_norm(DEEPNORM_ALPHA * xp + moe_l(xp), ln2_g[l], ln2_b[l])
        mix_s, k_s, v_s, c_s, h_s = temporal_block(
            xs, p, functools.partial(sample_attend, ck=cache_k[l], cv=cache_v[l]),
            state_conv[l], state_h[l])
        xs = layer_norm(DEEPNORM_ALPHA * xs + mix_s, ln1_g[l], ln1_b[l])
        xs = layer_norm(DEEPNORM_ALPHA * xs + moe_l(xs), ln2_g[l], ln2_b[l])
        nk_p.append(k_p); nv_p.append(v_p); nc_p.append(c_p); nh_p.append(h_p)
        nk_s.append(k_s); nv_s.append(v_s); nc_s.append(c_s); nh_s.append(h_s)
    return (xp, xs,
            jnp.stack(nk_p), jnp.stack(nv_p), jnp.stack(nc_p), jnp.stack(nh_p),
            jnp.stack(nk_s), jnp.stack(nv_s), jnp.stack(nc_s), jnp.stack(nh_s))


_drawn_inputs = setup_inputs


def setup_inputs(seed=0):
    import zlib

    import numpy as np

    out = dict(_drawn_inputs(seed))
    spreads = {}
    factors = {'attn_sinks': 27.454,
     'rg_ba': 8.0,
     'rg_bx': 7.831,
     'b_router': 22.554,
     'b_up': 8.0,
     'b_down': 6.308,
     'ln2_g': 7.78,
     'ln2_b': 8.695}
    for name, (base, spread) in spreads.items():
        noise = np.random.default_rng([zlib.crc32(name.encode()), seed]).standard_normal(out[name].shape)
        drawn = base * np.exp(spread * noise) if base else spread * noise
        out[name] = __import__('jax').numpy.asarray(drawn.astype(out[name].dtype))
    for name, factor in factors.items():
        out[name] = (out[name] * factor).astype(out[name].dtype)
    return out
```

```python
from contextlib import ExitStack

import numpy as np

import concourse.bass as bass
from concourse import mybir

F32 = mybir.dt.float32
F32R = mybir.dt.float32r
I32 = mybir.dt.int32
ALU = mybir.AluOpType
ACT = mybir.ActivationFunctionType
AX = mybir.AxisListType

P = 128
D = 1024
SEQ, DECB = 256, 8
T = SEQ + DECB
KD = D // P
TILES = [(0, 128), (128, 128), (256, 8)]
NH, NKV, HD = 16, 2, 64
GROUP = NH // NKV
WIN = 128
KVW = NKV * HD
DR = 1280
RT = DR // P
CONV = 4
NE, TOPK, DFF = 32, 4, 1024
FT = 2 * DFF // P
LIMIT, SALPHA = 7.0, 1.702
ALPHA = 2.0 ** 0.25
EPS = 1e-5
PROJ = D + 2 * KVW + 2 * DR + 2 * D
CAP = 64
N_OUT = 11
CHAIN = 3
MAXOVER = 16
NB = NE + MAXOVER
NCOL = NB + 2
BIG = 4096.0
INVALID = 1e30

RING = 6
SLOT = 2048
SPLITS = 3

C_ID, C_STACK, C_TRI, C_IOTA, C_DIST = 0, 128, 192, 320, 448
C_TDIST = C_DIST + 512
C_SLOPE = C_TDIST + 128
C_OV = C_SLOPE + 1
C_EIDX = C_OV + MAXOVER
C_W = C_EIDX + 1


def constants():
    c = np.zeros((P, C_W), np.float32)
    p = np.arange(P)[:, None]
    j = np.arange(P)[None, :]
    c[:, C_ID:C_ID + P] = p == j
    c[:, C_STACK:C_STACK + CAP] = (p % CAP) == np.arange(CAP)[None, :]
    c[:, C_TRI:C_TRI + P] = p < j
    c[:, C_IOTA:C_IOTA + P] = j % CAP
    for blk in range(2):
        prev = p + WIN - j
        cur = p - j
        c[:, C_DIST + 256 * blk:C_DIST + 256 * blk + 128] = np.where((prev < WIN) & (blk > 0), prev, INVALID)
        c[:, C_DIST + 256 * blk + 128:C_DIST + 256 * blk + 256] = np.where(cur >= 0, cur, INVALID)
    c[:, C_TDIST:C_TDIST + P] = WIN - 1 - j
    c[:NH, C_SLOPE] = [-slope(h) for h in range(NH)]
    c[:, C_OV:C_OV + MAXOVER] = np.arange(MAXOVER)[None, :]
    c[:, C_EIDX] = np.arange(P)
    return c


def slope(h):
    return float(np.float32(2.0) ** np.float32(-8.0 * (h + 1) / NH))


def plan():
    def cols(base, width):
        return [("win", base + 256 * i) for i in range(width // 256)]
    off_k, off_xr = D, D + 2 * KVW
    off_yr, off_ga, off_gb = off_xr + DR, off_xr + 2 * DR, off_xr + 2 * DR + D
    chunks, tiles = [], []

    def section(names, base, width):
        for i, c in enumerate(cols(base, width)):
            chunks.append(c)
            for half in range(2):
                tiles.append((names, 2 * i + half, len(chunks) - 1, half))

    section("kv", off_k, 2 * KVW)
    section("q", 0, D)
    section("xr", off_xr, DR)
    section("yr", off_yr, DR)
    for name, what in (("r", "wa"), ("i", "wx")):
        chunks.append((what, 0))
        tiles.extend((name, n, len(chunks) - 1, 0) for n in range(RT))
    section("ga", off_ga, D)
    section("gb", off_gb, D)
    order = []
    step = 0
    for n, (name, idx, _, _) in enumerate(tiles):
        order.append(("tile", n))
        if n == 3:
            order.append(("kvturn", 0))
        if name == "yr" or (name in ("ga", "gb") and step < NH + 2):
            order.append(("step", step))
            step += 1
        if name == "gb" and idx in (2, 3, 5, 7):
            order.append(("sample", (2, 3, 5, 7).index(idx)))
    assert step == NH + 2
    n_tiles_chunks = len(chunks)
    chunks += [("wao", 256 * i) for i in range(4)] + [("wro", P * i) for i in range(8)]
    chunks += [("wout", 2 * i) for i in range(4)] + [("ln1", 0), ("bup", 0)]
    return chunks, tiles, order, n_tiles_chunks


def build(nc, a):
    chunks, tiles, order, NPC = plan()
    NCH = len(chunks)
    CH_AO, CH_RO, CH_OUT, CH_LN, CH_BUP = NPC, NPC + 4, NPC + 12, NPC + 16, NPC + 17
    NT1 = len(tiles)

    def flat(name):
        ap = a[name]
        return ap[0]

    with ExitStack() as whole:
        def sb(name, shape, dt=F32, scope=whole):
            return scope.enter_context(nc.sbuf_tensor(name, shape, dt))

        def sem(name):
            return whole.enter_context(nc.semaphore(name))

        bank = [whole.enter_context(nc.psum_tensor(f"bank{i}", [P, 512], F32)) for i in range(8)]

        const = sb("const", [P, C_W])
        ident = const[:, C_ID:C_ID + P]
        stack = const[:, C_STACK:C_STACK + CAP]
        iota = const[:, C_IOTA:C_IOTA + P]
        raw = sb("raw", [P, RING, SLOT])
        xtok = sb("xtok", [P, 3, D])
        bdown = raw[0:NE, 1, 0:D]
        gateT = sb("gateT", [NE, T])
        posb = sb("posb", [P, NCOL, 3])
        gateb = sb("gateb", [P, NCOL, 3])
        bup = sb("bup", [P, FT, NB])
        tablei = sb("tablei", [1, NB + 2], I32)
        ones = sb("ones", [P, P])
        stats = sb("stats", [P, 3, 12])
        mv = sb("mv", [P, 3, 2])
        sd = sb("sd", [P, 3])
        rstd = sb("rstd", [P, 3])
        zero1 = sb("zero1", [P, 1])
        epsc = sb("epsc", [P, 1])

        early = ExitStack()
        xT = sb("xT", [P, KD, T], scope=early)
        first = ExitStack()
        parr = sb("parr", [80, P], scope=first)
        statr = sb("statr", [32, DR], scope=first)
        first.close()
        lg = sb("lg", [P, 2, 2, 256], scope=early)
        rmax = sb("rmax", [P, 2, 2], scope=early)
        spare = sb("spare", [P, 384], scope=early)
        par = sb("par", [P, 80], scope=early)
        stat = sb("stat", [P, RT, 32], scope=early)
        sink = sb("sink", [P, NH], scope=early)
        sinkc = sb("sinkc", [NH, 1], scope=early)
        wr = sb("wr", [P, KD, NE], scope=early)
        brb = sb("brb", [P, NE], scope=early)
        kT = sb("kT", [P, T], scope=early)
        vT = sb("vT", [P, T], scope=early)
        kz = sb("kz", [P, 4, 384], scope=early)
        vtok = sb("vtok", [P, 2, P], scope=early)
        ktok = sb("ktok", [P, P], scope=early)
        kv8 = sb("kv8", [DECB, 2, P], scope=early)
        qT = sb("qT", [P, KD, T], scope=early)
        pT = sb("pT", [P, 2, 384], scope=early)
        negm = sb("negm", [P, 2, NH], scope=early)
        rsum = sb("rsum", [P, 2, NH], scope=early)
        esk = sb("esk", [P, 2, NH], scope=early)
        otok = sb("otok", [P, 2, D], scope=early)
        oT = qT
        kc = sb("kc", [P, DECB, KVW], scope=early)
        vc = sb("vc", [P, DECB, KVW], scope=early)
        xrp = sb("xrp", [P, RT, T], scope=early)
        xrs = sb("xrs", [P, RT, DECB], scope=early)
        xc = sb("xc", [P, RT, T], scope=early)
        yr = sb("yr", [P, RT, T], scope=early)
        rg = sb("rg", [P, RT, T], scope=early)
        ig = sb("ig", [P, RT, T], scope=early)
        ga = sb("ga", [P, KD, T], scope=early)
        gb = sb("gb", [P, KD, T], scope=early)
        sg = sb("sg", [P, RT, T], scope=early)
        den = xrp
        hrec = xc
        sgf = sg[:, :, :].rearrange("p a b -> p (a b)")
        kcT = sgf[:, 0:1024].rearrange("p (b k) -> p b k", b=DECB)
        slog = sgf[0:NH, 1024:2048].rearrange("p (b k) -> p b k", b=DECB)
        qz = sgf[:, 2048:2176].rearrange("p (b h) -> p b h", b=DECB)
        pTs = sgf[:, 2176:2304].rearrange("p (b h) -> p b h", b=DECB)
        srow = sb("srow", [NH, 4, DECB], scope=early)
        pack = sb("pack", [P, RT, 20], scope=early)
        lamt = sb("lamt", [P, 8, RT], scope=early)
        rgf = rg[:, :, :].rearrange("p a b -> p (a b)")
        rt = rgf[:, 0:768].rearrange("p (i t e) -> p i t e", i=8, t=3)
        lgt = rgf[:, 768:864].rearrange("p (t e) -> p t e", t=3)
        m8 = rgf[:, 864:888].rearrange("p (t e) -> p t e", t=3)
        rsm = rgf[:, 888:900].rearrange("p (i t) -> p i t", i=4)
        posmT = rgf[0:NE, 900:900 + T]
        ov = rgf[0:NE, 1164:1172]
        selm = rgf[0:NE, 1172:1172 + NB]
        negj = rgf[0:NE, 1220:1220 + NB]
        ohw = rgf[0:NE, 1268:1268 + 3 * MAXOVER].rearrange("p (i o) -> p i o", i=3)
        rows = otok[0:20, :, :].rearrange("p a b -> p (a b)")[:, 0:DR]
        early.close()

        late = ExitStack()
        hi = sb("hi", [P, SPLITS, SLOT], F32R, scope=late)
        lo = sb("lo", [P, SPLITS, SLOT], F32R, scope=late)
        xg = sb("xg", [P, KD, P], F32R, scope=late)
        at = sb("at", [P, KD, P], F32R, scope=late)
        hsb = sb("hsb", [P, 2 * DFF], scope=late)
        ysb = sb("ysb", [P, D], scope=late)
        gt = sb("gt", [P, T], scope=late)
        onehot = sb("onehot", [P, 3, CAP], scope=late)
        gated = sb("gated", [P, 3, P], scope=late)
        glu = sb("glu", [P, KD, CAP], scope=late)
        lin = sb("lin", [P, KD, CAP], scope=late)
        sig = sb("sig", [P, KD, CAP], scope=late)
        act_ = sb("act_", [P, KD, CAP], scope=late)
        yT = sb("yT", [P, KD, T], scope=late)
        late.close()

        s_const = sem("s_const")
        s_x = sem("s_x")
        s_par = sem("s_par")
        s_misc = sem("s_misc")
        s_cache = sem("s_cache")
        s_new = sem("s_new")
        s_bd = sem("s_bd")
        s_out = sem("s_out")
        y_out = sem("y_out")
        loaded = [sem(f"loaded{i}") for i in range(RING)]
        ones_ready = sem("ones_ready")
        x_turned = sem("x_turned")
        xT_ready = sem("xT_ready")
        par_turned = sem("par_turned")
        par_ready = sem("par_ready")
        tile_done = sem("tile_done")
        tile_evac = sem("tile_evac")
        kv_turned = sem("kv_turned")
        kv_ready = sem("kv_ready")
        kz_ready = sem("kz_ready")
        scored = sem("scored")
        scores_taken = sem("scores_taken")
        max_ready = sem("max_ready")
        probs_ready = sem("probs_ready")
        probs_turned = sem("probs_turned")
        pT_ready = sem("pT_ready")
        pv_done = sem("pv_done")
        o_ready = sem("o_ready")
        den_in = sem("den_in")
        sinkexp = sem("sinkexp")
        o_norm = sem("o_norm")
        o_turned = sem("o_turned")
        oT_ready = sem("oT_ready")
        conv_ready = sem("conv_ready")
        lam_in = sem("lam_in")
        lam_exp = sem("lam_exp")
        lam_ready = sem("lam_ready")
        gates_done = sem("gates_done")
        tanh_done = sem("tanh_done")
        ratio_ready = sem("ratio_ready")
        root_done = sem("root_done")
        decay_done = sem("decay_done")
        gelu_done = sem("gelu_done")
        y_rnn_ready = sem("y_rnn_ready")
        s_kt = sem("s_kt")
        s_kte = sem("s_kte")
        s_qz = sem("s_qz")
        s_sc = sem("s_sc")
        s_sm = sem("s_sm")
        s_ex = sem("s_ex")
        s_pn = sem("s_pn")
        s_ptt = sem("s_ptt")
        s_pte = sem("s_pte")
        s_pv = sem("s_pv")
        s_os = sem("s_os")
        out_done = sem("out_done")
        out_evac = sem("out_evac")
        merged_ready = sem("merged_ready")
        mix_done = sem("mix_done")
        pack_ready = sem("pack_ready")
        pack_turned = sem("pack_turned")
        rows_ready = sem("rows_ready")
        var_ready = sem("var_ready")
        sd_ready = sem("sd_ready")
        x1_ready = sem("x1_ready")
        x1_turned = sem("x1_turned")
        x1T_ready = sem("x1T_ready")
        logits_done = sem("logits_done")
        top_ready = sem("top_ready")
        exp_ready = sem("exp_ready")
        mask_ready = sem("mask_ready")
        count_done = sem("count_done")
        over_ready = sem("over_ready")
        start_done = sem("start_done")
        route_ready = sem("route_ready")
        route_turned = sem("route_turned")
        routeT_ready = sem("routeT_ready")
        table_done = sem("table_done")
        table_ready = sem("table_ready")
        v = sem("v")
        vm = sem("vm")
        onehot_ready = sem("onehot_ready")
        gated_ready = sem("gated_ready")
        gathered = sem("gathered")
        gated_turned = sem("gated_turned")
        gt_ready = sem("gt_ready")
        xg_high = sem("xg_high")
        xg_ready = sem("xg_ready")
        split_free = sem("split_free")
        hi_ready = sem("hi_ready")
        lo_ready = sem("lo_ready")
        up_taken = sem("up_taken")
        hT_done = sem("hT_done")
        hT_taken = sem("hT_taken")
        glu_ready = sem("glu_ready")
        sig_ready = sem("sig_ready")
        act_ready = sem("act_ready")
        at_high = sem("at_high")
        at_ready = sem("at_ready")
        y_ready = sem("y_ready")
        combined = sem("combined")
        added = sem("added")
        y_cleared = sem("y_cleared")
        final_done = sem("final_done")
        var2_ready = sem("var2_ready")
        sd2_ready = sem("sd2_ready")
        ln2_loaded = sem("ln2_loaded")
        fin_ready = sem("fin_ready")

        def slot(c):
            return raw[:, c % RING, :]

        def loads(c):
            return sum(2 if chunks[x][0] == "ln1" else 1 for x in range(c % RING, min(c + 1, NCH), RING)) \
                + len([x for x in range(NCH, c + 1) if x % RING == c % RING])

        def chunk_ready(e, c):
            e.wait_ge(loaded[c % RING], 16 * loads(c))

        LOADED0 = [16 * loads(NCH + i) for i in range(12)]

        block = whole.enter_context(nc.Block())

        @block.sync
        def _(sp):
            win = flat("w_in").rearrange("(k p) n -> p k n", p=P)
            wao = flat("w_attn_out").rearrange("(k p) n -> p k n", p=P)
            wro = flat("w_rnn_out").rearrange("(k p) n -> p k n", p=P)
            wout = flat("w_out").rearrange("(k p) n -> p k n", p=P)
            w_up = a["w_up"].rearrange("l e d n -> (l e d) n")
            w_down = a["w_down"].rearrange("l e d n -> (l e d) n")

            def used(c):
                if c < NPC:
                    sp.wait_ge(tile_done, max(n for n in range(NT1) if tiles[n][2] == c) + 1)
                elif c < CH_RO:
                    sp.wait_ge(out_done, 2 * (c - CH_AO) + 2)
                elif c < CH_OUT:
                    sp.wait_ge(out_done, 8 + c - CH_RO + 1)
                elif c < CH_LN:
                    sp.wait_ge(mix_done, c - CH_OUT + 1)
                elif c == CH_LN:
                    sp.wait_ge(x1_ready, 3)
                else:
                    sp.wait_ge(table_done, 1)

            for c, (kind, at0) in enumerate(chunks):
                if c >= RING:
                    used(c - RING)
                if kind == "win":
                    pieces = [(slot(c).rearrange("p (k n) -> p k n", k=KD), win[:, :, at0:at0 + 256])]
                elif kind in ("wa", "wx"):
                    pieces = [(slot(c)[:, 0:DR].rearrange("p (n d) -> p n d", n=RT),
                               flat("rg_" + kind).rearrange("n c d -> c n d"))]
                elif kind == "wao":
                    pieces = [(slot(c).rearrange("p (k n) -> p k n", k=KD), wao[:, :, at0:at0 + 256])]
                elif kind == "wro":
                    pieces = [(slot(c)[:, 0:DR].rearrange("p (k n) -> p k n", k=RT), wro[:, :, at0:at0 + P])]
                elif kind == "wout":
                    pieces = [(slot(c).rearrange("p (k n) -> p k n", k=2), wout[:, at0:at0 + 2, :])]
                elif kind == "ln1":
                    pieces = [(slot(c)[:, 0:D], a["ln1_g"].partition_broadcast(P)),
                              (slot(c)[:, D:2 * D], a["ln1_b"].partition_broadcast(P))]
                else:
                    pieces = [(slot(c)[0:NE, :], flat("b_up"))]
                for dst, src in pieces:
                    sp.dma_start(dst, src).then_inc(loaded[c % RING], 16)

            def moe_chunk(i, row0):
                c = NCH + i
                if i < 8:
                    src = w_up[bass.ds(row0 + i * P, P), :]
                    dst = slot(c)
                else:
                    src = w_down[bass.ds(row0 + (i - 8) * 256, 256), :].rearrange("(k p) n -> p k n", p=P)
                    dst = slot(c).rearrange("p (k n) -> p k n", k=2)
                sp.dma_start(dst, src).then_inc(loaded[c % RING], 16)

            for i in range(12):
                if i < RING:
                    used(NCH + i - RING)
                else:
                    sp.wait_ge(lo_ready, i - RING + 1)
                moe_chunk(i, 0)
            sp.wait_ge(table_ready, 1)
            blocks = sp.value_load(tablei[0:1, NB:NB + 1], min_val=NE, max_val=NB)
            with sp.Fori(1, blocks) as b:
                e = sp.value_load(tablei[0:1, bass.ds(b, 1)], min_val=0, max_val=NE - 1)
                row0 = e * D
                for i in range(12):
                    sp.wait_ge(lo_ready, b * 12 + (i - RING + 1))
                    moe_chunk(i, row0)
            sp.wait_ge(lo_ready, blocks * 12)
            sp.dma_start(raw[:, 0, 0:D], a["ln2_g"].partition_broadcast(P)).then_inc(ln2_loaded, 16)
            sp.dma_start(raw[:, 0, D:2 * D], a["ln2_b"].partition_broadcast(P)).then_inc(ln2_loaded, 16)
            sp.dma_start(bdown, flat("b_down")).then_inc(ln2_loaded, 16)
            for t, (t0, n) in enumerate(TILES):
                sp.wait_ge(fin_ready, t + 1)
                dst = a["o_yp"][0, t0:t0 + n, :] if t < 2 else a["o_ys"][:, 0, :]
                sp.dma_start(dst, xtok[0:n, t, :]).then_inc(y_out, 16)
            sp.wait_ge(y_out, 48)

        @block.gpsimd
        def _(pool):
            pool.dma_start(a["o_ks"][0, :, 0:WIN - 1], a["cache_k"][0, :, 1:WIN]).then_inc(s_out, 16)
            pool.dma_start(a["o_vs"][0, :, 0:WIN - 1], a["cache_v"][0, :, 1:WIN]).then_inc(s_out, 16)
            pool.dma_start(a["o_cs"][0, :, 0:2], a["state_conv"][0, :, 1:3]).then_inc(s_out, 16)
            pool.wait_ge(kv_ready, 3)
            pool.wait_ge(s_cache, 32)
            pool.dma_start(kc[P - 1:P, :, :], kv8[:, 0:1, :]).then_inc(s_new, 16)
            pool.dma_start(vc[P - 1:P, :, :], kv8[:, 1:2, :]).then_inc(s_new, 16)
            kvo = lambda name: a[name][0, :, WIN - 1, :, :].rearrange("b g d -> b (g d)")
            pool.dma_start(kvo("o_ks"), kv8[:, 0, :]).then_inc(s_out, 16)
            pool.dma_start(kvo("o_vs"), kv8[:, 1, :]).then_inc(s_out, 16)
            pool.dma_start(a["o_kp"][0, 0].rearrange("s g d -> s (g d)"), ktok[:, :]).then_inc(s_out, 16)
            pool.dma_start(a["o_vp"][0, 0].rearrange("s g d -> s (g d)"), vtok[:, 1, :]).then_inc(s_out, 16)
            pool.wait_ge(rows_ready, 3)
            pool.dma_start(a["o_cp"][0, 0], rows[0:3, :]).then_inc(s_out, 16)
            pool.dma_start(a["o_hp"][0], rows[3:4, :]).then_inc(s_out, 16)
            pool.dma_start(a["o_cs"][0, :, 2, :], rows[4:12, :]).then_inc(s_out, 16)
            pool.dma_start(a["o_hs"][0], rows[12:20, :]).then_inc(s_out, 16)
            pool.wait_ge(s_out, 16 * N_OUT)

        @block.scalar
        def _(act):
            act.dma_start(const[:, :], a["consts"]).then_inc(s_const, 16)
            for t in range(2):
                act.dma_start(xtok[:, t, :], a["x_prompt"][0, t * P:(t + 1) * P, :]).then_inc(s_x, 16)
            act.dma_start(xtok[0:DECB, 2, :], a["x_sample"][:, 0, :]).then_inc(s_x, 16)
            r0 = 0
            for name in ("conv_w", "conv_b", "rg_ba", "rg_bx", "rg_lambda"):
                src = a[name][0].rearrange("j (t p) -> (j t) p", p=P) if name == "conv_w" \
                    else a[name][0].rearrange("(t p) -> t p", p=P)
                n = 40 if name == "conv_w" else RT
                act.dma_start(parr[r0:r0 + n, :], src).then_inc(s_par, 16)
                r0 += n
            act.dma_start(statr[0:24, :], a["state_conv"][0].rearrange("b j c -> (b j) c")).then_inc(s_par, 16)
            act.dma_start(statr[24:32, :], a["state_h"][0]).then_inc(s_par, 16)
            act.dma_start(sink[:, :], a["attn_sinks"].partition_broadcast(P)).then_inc(s_misc, 16)
            act.dma_start(sinkc[:, :], a["attn_sinks"].rearrange("l h -> h l")).then_inc(s_misc, 16)
            act.dma_start(kc[0:P - 1, :, :], a["cache_k"][0, :, 1:WIN].rearrange("b w g d -> w b (g d)"))\
                .then_inc(s_cache, 16)
            act.dma_start(vc[0:P - 1, :, :], a["cache_v"][0, :, 1:WIN].rearrange("b w g d -> w b (g d)"))\
                .then_inc(s_cache, 16)
            act.dma_start(wr[:, :, :], flat("w_router").rearrange("(k p) e -> p k e", p=P)).then_inc(s_bd, 16)
            act.dma_start(brb[:, :], a["b_router"].partition_broadcast(P)).then_inc(s_bd, 16)

            def turned_x(ready, done):
                for g in range(5):
                    act.wait_ge(ready, g + 1)
                    if g < 4:
                        t, d0 = g // 2, 4 * (g % 2)
                        act.activation(xT[:, d0:d0 + 4, t * P:(t + 1) * P],
                                       bank[g][:, :].rearrange("p (d n) -> p d n", d=4), ACT.Copy).then_inc(done, 1)
                    else:
                        act.activation(xT[:, :, SEQ:T], bank[4][:, 0:64].rearrange("p (d n) -> p d n", d=KD),
                                       ACT.Copy).then_inc(done, 1)

            turned_x(x_turned, xT_ready)
            act.wait_ge(lam_in, 1)
            act.activation(lamt[:, 2, :], lamt[:, 1, :], ACT.Exp, scale=-1.0).then_inc(lam_exp, 1)

            def exps(h):
                act.wait_ge(max_ready, h + 1)
                for blk in range(2):
                    last = act.activation(lg[:, h % 2, blk, :], lg[:, h % 2, blk, :], ACT.Exp,
                                          bias=negm[:, blk, h:h + 1], accum_out=rsum[:, blk, h:h + 1])
                last.then_inc(probs_ready, 1)

            for what, n in order:
                if what == "tile":
                    name, idx, _, _ = tiles[n]
                    ps = bank[n % 4][:, 0:T]
                    act.wait_ge(tile_done, n + 1)
                    if name == "kv":
                        ins = act.activation((kT if idx == 0 else vT)[:, :], ps, ACT.Copy)
                    elif name == "q":
                        ins = act.activation(qT[:, idx, :], ps, ACT.Copy, scale=HD ** -0.5)
                    elif name == "xr":
                        act.activation(xrp[:, idx, 3:3 + SEQ], ps[:, 0:SEQ], ACT.Copy)
                        ins = act.activation(xrs[:, idx, :], ps[:, SEQ:T], ACT.Copy)
                    elif name in ("r", "i"):
                        if name == "r" and idx == 0:
                            act.wait_ge(par_ready, 2)
                        col = (50 if name == "r" else 60) + idx
                        ins = act.activation((rg if name == "r" else ig)[:, idx, :], ps, ACT.Identity,
                                             bias=par[:, col:col + 1])
                    else:
                        ins = act.activation({"yr": yr, "ga": ga, "gb": gb}[name][:, idx, :], ps, ACT.Copy)
                    ins.then_inc(tile_evac, 1)
                elif what == "kvturn":
                    act.wait_ge(kv_turned, 1)
                    act.activation(vtok[:, :, :], bank[6][:, 0:256].rearrange("p (b n) -> p b n", b=2), ACT.Copy)\
                        .then_inc(kv_ready, 1)
                    act.activation(ktok[:, :], bank[6][:, 256:384], ACT.Copy).then_inc(kv_ready, 1)
                    act.activation(kv8[:, :, :], bank[7][0:DECB, 0:256].rearrange("p (b n) -> p b n", b=2), ACT.Copy)\
                        .then_inc(kv_ready, 1)
                elif what == "step":
                    h = n - 1
                    if 0 <= h < NH:
                        if h >= 2:
                            act.wait_ge(pv_done, h - 1)
                        act.wait_ge(probs_turned, h + 1)
                        act.activation(pT[:, h % 2, :], bank[6][:, 0:384], ACT.Copy).then_inc(pT_ready, 1)
                    h = n - 2
                    if 0 <= h < NH:
                        act.wait_ge(pv_done, h + 1)
                        act.activation(otok[:, :, h * HD:(h + 1) * HD],
                                       bank[7][:, (h % 4) * P:(h % 4 + 1) * P].rearrange("p (b n) -> p b n", b=2),
                                       ACT.Copy).then_inc(o_ready, 1)
                    if n < NH:
                        exps(n)
                    if n == NH + 1:
                        act.wait_ge(den_in, 1)
                        act.activation(esk[:, :, :], esk[:, :, :], ACT.Exp).then_inc(sinkexp, 1)
                else:
                    if n == 0:
                        for j in range(2):
                            act.wait_ge(s_kt, j + 1)
                            act.activation(kcT[:, 4 * j:4 * j + 4, :],
                                           bank[4 + j][:, :].rearrange("p (b n) -> p b n", b=4), ACT.Copy)\
                                .then_inc(s_kte, 1)
                    elif n == 1:
                        act.wait_ge(s_sm, 1)
                        act.activation(slog, slog, ACT.Exp).then_inc(s_ex, 1)
                        act.activation(srow[:, 1, :], srow[:, 1, :], ACT.Exp).then_inc(s_ex, 1)
                    elif n == 2:
                        act.wait_ge(s_ptt, 1)
                        act.activation(pTs, bank[4][:, 0:P].rearrange("p (b h) -> p b h", b=DECB), ACT.Copy)\
                            .then_inc(s_pte, 1)

            for g in range(4):
                act.wait_ge(o_turned, g + 1)
                if g == 0:
                    act.wait_ge(s_qz, 1)
                blk, d0 = g // 2, 4 * (g % 2)
                act.activation(oT[:, d0:d0 + 4, blk * P:(blk + 1) * P],
                               bank[4 + g][:, :].rearrange("p (d n) -> p d n", d=4), ACT.Copy).then_inc(oT_ready, 1)

            act.wait_ge(tile_evac, NT1)
            act.activation(rg[:, :, :], rg[:, :, :], ACT.Sigmoid).then_inc(gates_done, 1)
            act.wait_ge(gates_done, 1)
            act.wait_ge(lam_ready, 1)
            act.wait_ge(s_os, 1)
            for n in range(RT):
                act.activation(sg[:, n, :], rg[:, n, :], ACT.Tanh, scale=lamt[:, 7, n:n + 1]).then_inc(tanh_done, 1)
            act.activation(ig[:, :, :], ig[:, :, :], ACT.Sigmoid).then_inc(gates_done, 1)
            act.activation(ga[:, :, :], ga[:, :, :], ACT.Sigmoid).then_inc(gates_done, 1)
            act.activation(gb[:, :, :], gb[:, :, :], ACT.Sigmoid).then_inc(gates_done, 1)
            act.wait_ge(tanh_done, RT)
            for n in range(RT):
                act.activation(rg[:, n, :], rg[:, n, :], ACT.Exp, scale=lamt[:, 6, n:n + 1]).then_inc(decay_done, 1)
            act.activation(yr[:, :, :], yr[:, :, :], ACT.Gelu_apprx_tanh).then_inc(gelu_done, 1)
            act.wait_ge(ratio_ready, 1)
            act.activation(sg[:, :, :], sg[:, :, :], ACT.Sqrt, scale=2.0).then_inc(root_done, 1)

            for g, (c0, w) in enumerate(((0, 512), (512, 512), (1024, 256))):
                act.wait_ge(pack_turned, g + 1)
                act.activation(rows[:, c0:c0 + w], bank[5 + g][0:20, 0:w], ACT.Copy).then_inc(rows_ready, 1)

            def roots(ready, done):
                for t, (_, n) in enumerate(TILES):
                    act.wait_ge(ready, t + 1)
                    act.activation(sd[0:n, t:t + 1], mv[0:n, t, 1:2], ACT.Sqrt, bias=epsc[0:n, :]).then_inc(done, 1)

            roots(var_ready, sd_ready)
            turned_x(x1_turned, x1T_ready)
            for t, (_, n) in enumerate(TILES):
                act.wait_ge(top_ready, t + 1)
                act.activation(rt[0:n, 5, t, :], lgt[0:n, t, :], ACT.Exp, bias=rsm[0:n, 0, t:t + 1])\
                    .then_inc(exp_ready, 1)

            act.wait_ge(table_ready, 1)
            blocks = act.value_load(tablei[0:1, NB:NB + 1], min_val=NE, max_val=NB)

            def take_gather(count):
                act.wait_ge(gathered, count)
                act.activation(xg[:, :, 0:CAP], bank[6][:, :].rearrange("p (d n) -> p d n", d=KD), ACT.Copy)\
                    .then_inc(xg_high, 1)

            def take_gt(count):
                act.wait_ge(gated_turned, count)
                act.activation(gt[:, :], bank[7][:, 0:T], ACT.Copy).then_inc(gt_ready, 1)

            def take_y(before):
                act.wait_ge(split_free, before * 12 + SPLITS)
                for j in range(2):
                    act.activation(ysb[:, j * 512:(j + 1) * 512], bank[4 + j][:, :], ACT.Copy).then_inc(y_ready, 1)

            take_gather(1)
            with act.Fori(0, blocks) as b:
                def split(i):
                    c = NCH + i
                    act.wait_ge(split_free, b * 12 + (i + 1))
                    act.wait_ge(loaded[c % RING], b * 32 + LOADED0[i])
                    act.activation(hi[:, i % SPLITS, :], slot(c), ACT.Copy).then_inc(hi_ready, 1)
                for i in range(3):
                    split(i)
                take_y(b)
                for i in range(3, 10):
                    split(i)
                act.wait_ge(split_free, b * 12 + (SPLITS + 8))
                for j in range(4):
                    act.activation(hsb[:, j * 512:(j + 1) * 512], bank[j][:, :], ACT.Copy).then_inc(up_taken, 1)
                take_gather(b + 2)
                take_gt(b + 2)
                split(10)
                act.wait_ge(glu_ready, b + 1)
                act.activation(sig[:, :, :], glu[:, :, :], ACT.Sigmoid, scale=SALPHA).then_inc(sig_ready, 1)
                act.wait_ge(act_ready, b + 1)
                act.activation(at[:, :, 0:CAP], act_[:, :, :], ACT.Copy).then_inc(at_high, 1)
                split(11)
            take_y(blocks)
            take_gt(blocks + 2)
            roots(var2_ready, sd2_ready)

        @block.tensor
        def _(pe):
            pe.wait_ge(s_const, 16)
            pe.wait_ge(s_x, 48)

            def turn_x(done, first_wait=None):
                for g in range(4):
                    t, d0 = g // 2, 4 * (g % 2)
                    for j in range(4):
                        last = pe.transpose(bank[g][:, j * P:(j + 1) * P], xtok[:, t, (d0 + j) * P:(d0 + j + 1) * P],
                                            ident)
                    last.then_inc(done, 1)
                for d in range(KD):
                    last = pe.transpose(bank[4][:, d * 8:d * 8 + 8], xtok[0:DECB, 2, d * P:(d + 1) * P],
                                        ident[0:DECB, 0:DECB])
                last.then_inc(done, 1)

            turn_x(x_turned)
            pe.wait_ge(s_par, 16 * 7)
            pe.transpose(bank[5][:, 0:80], parr[:, :], ident[0:80, 0:80]).then_inc(par_turned, 1)
            for n in range(RT):
                last = pe.transpose(bank[6][:, n * 32:(n + 1) * 32], statr[:, n * P:(n + 1) * P], ident[0:32, 0:32])
            last.then_inc(par_turned, 1)
            pe.wait_ge(xT_ready, 5)

            def scores(h):
                g, par_ = h // GROUP, h % 2
                if h == 0:
                    pe.wait_ge(kz_ready, 1)
                    pe.wait_ge(tile_evac, 10)
                if h >= 2:
                    pe.wait_ge(scores_taken, h - 1)
                for blk in range(2):
                    last = pe.matmul(bank[4 + h % 2][:, blk * 256:(blk + 1) * 256],
                                     qT[:, h // 2, blk * P:(blk + 1) * P],
                                     kz[:, 2 * g + par_, blk * P:blk * P + 256], start=True, stop=True)
                last.then_inc(scored, 1)

            def turn_probs(h):
                pe.wait_ge(probs_ready, h + 1)
                if h >= 1:
                    pe.wait_ge(pT_ready, h)
                for j, (blk, part) in enumerate(((0, 1), (1, 0), (1, 1))):
                    last = pe.transpose(bank[6][:, j * P:(j + 1) * P], lg[:, h % 2, blk, part * P:(part + 1) * P],
                                        ident)
                last.then_inc(probs_turned, 1)

            def weigh(h):
                g = h // GROUP
                pe.wait_ge(pT_ready, h + 1)
                if h >= 1:
                    pe.wait_ge(o_ready, h)
                o = bank[7][:, (h % 4) * P:(h % 4 + 1) * P]
                vv = lambda blk: vtok[:, blk, g * HD:(g + 1) * HD]
                pe.matmul(o[:, 0:HD], pT[:, h % 2, 0:P], vv(0), start=True, stop=True)
                pe.matmul(o[:, HD:P], pT[:, h % 2, P:2 * P], vv(0), start=True, stop=False)
                pe.matmul(o[:, HD:P], pT[:, h % 2, 2 * P:3 * P], vv(1), start=False, stop=True).then_inc(pv_done, 1)

            seen = set()
            for what, n in order:
                if what == "tile":
                    name, idx, c, half = tiles[n]
                    if c not in seen:
                        chunk_ready(pe, c)
                        seen.add(c)
                    if n >= 4:
                        pe.wait_ge(tile_evac, n - 3)
                    if name in ("r", "i"):
                        pe.wait_ge(conv_ready, idx + 1 if name == "r" else RT)
                        last = pe.matmul(bank[n % 4][:, 0:T], slot(c)[:, idx * P:(idx + 1) * P], xc[:, idx, :],
                                         start=True, stop=True)
                    else:
                        w = slot(c).rearrange("p (k n) -> p k n", k=KD)
                        for k in range(KD):
                            last = pe.matmul(bank[n % 4][:, 0:T], w[:, k, half * P:(half + 1) * P], xT[:, k, :],
                                             start=k == 0, stop=k == KD - 1)
                    last.then_inc(tile_done, 1)
                elif what == "kvturn":
                    pe.wait_ge(tile_evac, 2)
                    pe.wait_ge(par_ready, 2)
                    for blk in range(2):
                        pe.transpose(bank[6][:, blk * P:(blk + 1) * P], vT[:, blk * P:(blk + 1) * P], ident)
                    pe.transpose(bank[6][:, 256:384], kT[:, P:2 * P], ident)
                    pe.transpose(bank[7][0:DECB, 0:P], kT[:, SEQ:T], ident)
                    pe.transpose(bank[7][0:DECB, P:2 * P], vT[:, SEQ:T], ident).then_inc(kv_turned, 1)
                elif what == "step":
                    if n == 0:
                        pe.wait_ge(kv_ready, 3)
                    if n < NH:
                        scores(n)
                    if 0 <= n - 1 < NH:
                        turn_probs(n - 1)
                    if 0 <= n - 2 < NH:
                        weigh(n - 2)
                else:
                    if n == 0:
                        pe.wait_ge(s_new, 32)
                        pe.wait_ge(scores_taken, NH)
                        for j in range(2):
                            for b in range(4):
                                last = pe.transpose(bank[4 + j][:, b * P:(b + 1) * P], kc[:, 4 * j + b, :], ident)
                            last.then_inc(s_kt, 1)
                    elif n == 1:
                        pe.wait_ge(s_kte, 2)
                        pe.wait_ge(s_qz, 1)
                        pe.wait_ge(o_ready, NH)
                        for b in range(DECB):
                            last = pe.matmul(bank[6 + b // 4][0:NH, (b % 4) * P:(b % 4 + 1) * P], qz[:, b, :],
                                             kcT[:, b, :], start=True, stop=True)
                        last.then_inc(s_sc, 1)
                    elif n == 2:
                        pe.wait_ge(s_pn, 1)
                        for b in range(DECB):
                            last = pe.transpose(bank[4][:, b * NH:(b + 1) * NH], slog[:, b, :], ident[0:NH, 0:NH])
                        last.then_inc(s_ptt, 1)
                    else:
                        pe.wait_ge(s_pte, 1)
                        for b in range(DECB):
                            last = pe.matmul(bank[5][:, b * NH:(b + 1) * NH], vc[:, b, :], pTs[:, b, :],
                                             start=True, stop=True)
                        last.then_inc(s_pv, 1)

            pe.wait_ge(o_norm, 2)
            pe.wait_ge(s_os, 1)
            for g in range(4):
                blk, d0 = g // 2, 4 * (g % 2)
                for j in range(4):
                    last = pe.transpose(bank[4 + g][:, j * P:(j + 1) * P], otok[:, blk, (d0 + j) * P:(d0 + j + 1) * P],
                                        ident)
                last.then_inc(o_turned, 1)

            pe.wait_ge(oT_ready, 4)
            for m in range(16):
                if m < 4:
                    pe.wait_ge(tile_evac, NT1)
                else:
                    pe.wait_ge(out_evac, m - 3)
                if m < 8:
                    c, half = CH_AO + m // 2, m % 2
                    w, src, kk = slot(c).rearrange("p (k n) -> p k n", k=KD), oT, KD
                else:
                    c, half = CH_RO + m - 8, 0
                    w, src, kk = slot(c)[:, 0:DR].rearrange("p (k n) -> p k n", k=RT), yr, RT
                    pe.wait_ge(y_rnn_ready, 1)
                chunk_ready(pe, c)
                for k in range(kk):
                    last = pe.matmul(bank[m % 4][:, 0:T], w[:, k, half * P:(half + 1) * P], src[:, k, :],
                                     start=k == 0, stop=k == kk - 1)
                last.then_inc(out_done, 1)
            pe.wait_ge(pack_ready, 1)
            pe.wait_ge(oT_ready, 4)
            for g, (n0, n1) in enumerate(((0, 4), (4, 8), (8, 10))):
                for n in range(n0, n1):
                    last = pe.transpose(bank[5 + g][0:20, (n - n0) * P:(n - n0 + 1) * P], pack[:, n, :], ident)
                last.then_inc(pack_turned, 1)
            mix = [(bank[4], bank[5]), (bank[6], bank[7]), (bank[0], bank[1])]
            pe.wait_ge(merged_ready, 8)
            pe.wait_ge(rows_ready, 3)
            for cc in range(4):
                chunk_ready(pe, CH_OUT + cc)
                w = slot(CH_OUT + cc).rearrange("p (k n) -> p k n", k=2)
                for kk in range(2):
                    k = 2 * cc + kk
                    for t, (t0, n) in enumerate(TILES):
                        for h in range(2):
                            last = pe.matmul(mix[t][h][0:n, :], ga[:, k, t0:t0 + n], w[:, kk, h * 512:(h + 1) * 512],
                                             start=k == 0, stop=k == KD - 1)
                last.then_inc(mix_done, 1)

            pe.wait_ge(x1_ready, 3)
            turn_x(x1_turned)
            pe.wait_ge(x1T_ready, 5)
            pe.wait_ge(s_bd, 32)
            for t, (t0, n) in enumerate(TILES):
                for k in range(KD):
                    last = pe.matmul(bank[5][0:n, t * NE:(t + 1) * NE], xT[:, k, t0:t0 + n], wr[:, k, :],
                                     start=k == 0, stop=k == KD - 1)
            last.then_inc(logits_done, 1)
            pe.wait_ge(mask_ready, 3)
            mask = lambda t, n: rt[0:n, 4, t, :]
            for t, (t0, n) in enumerate(TILES):
                for u in range(t):
                    pe.matmul(bank[6][0:n, t * NE:(t + 1) * NE], ones[:, 0:n], mask(u, P), start=u == 0, stop=False)
                pe.matmul(bank[6][0:n, t * NE:(t + 1) * NE], const[0:n, C_TRI:C_TRI + n], mask(t, n),
                          start=t == 0, stop=True)
            for t, (t0, n) in enumerate(TILES):
                last = pe.matmul(bank[7][0:NE, 0:1], mask(t, n), ones[0:n, 0:1], start=t == 0, stop=t == 2)
            last.then_inc(count_done, 1)
            pe.wait_ge(over_ready, 1)
            pe.matmul(bank[7][0:NE, 8:9], const[0:NE, C_TRI:C_TRI + NE], ov[:, 1:2], start=True, stop=True)
            pe.matmul(bank[7][0:1, 16:17], ov[:, 1:2], ones[0:NE, 0:1], start=True, stop=True).then_inc(start_done, 1)
            pe.wait_ge(route_ready, 3)
            for t, (t0, n) in enumerate(TILES):
                pe.transpose(bank[0][0:NE, t0:t0 + n], rt[0:n, 6, t, :], ident[0:n, 0:n])
                last = pe.transpose(bank[1][0:NE, t0:t0 + n], rt[0:n, 7, t, :], ident[0:n, 0:n])
            last.then_inc(route_turned, 1)
            pe.wait_ge(routeT_ready, 1)
            for t, (t0, n) in enumerate(TILES):
                pe.matmul(bank[2][0:n, t * NB:(t + 1) * NB], posmT[:, t0:t0 + n], selm[:, :], start=True, stop=False)
                pe.matmul(bank[2][0:n, t * NB:(t + 1) * NB], ones[0:NE, 0:n], negj[:, :], start=False, stop=True)
                pe.matmul(bank[3][0:n, t * NB:(t + 1) * NB], gateT[:, t0:t0 + n], selm[:, :], start=True, stop=True)
            pe.matmul(bank[7][0:1, 32:32 + NB], const[0:NE, C_EIDX:C_EIDX + 1], selm[:, :], start=True, stop=True)
            chunk_ready(pe, CH_BUP)
            for f in range(FT):
                bk, o = (5, f * NB) if f < 8 else (6, (f - 8) * NB)
                last = pe.matmul(bank[bk][:, o:o + NB], slot(CH_BUP)[0:NE, f * P:(f + 1) * P], selm[:, :],
                                 start=True, stop=True)
            last.then_inc(table_done, 1)

            pe.wait_ge(table_ready, 1)
            blocks = pe.value_load(tablei[0:1, NB:NB + 1], min_val=NE, max_val=NB)

            def gather():
                for d in range(KD):
                    for t, (t0, n) in enumerate(TILES):
                        last = pe.matmul(bank[6][:, d * CAP:(d + 1) * CAP], xtok[0:n, t, d * P:(d + 1) * P],
                                         onehot[0:n, t, :], start=t == 0, stop=t == 2)
                last.then_inc(gathered, 1)

            def turn_gates():
                for t, (t0, n) in enumerate(TILES):
                    last = pe.transpose(bank[7][:, t0:t0 + n], gated[0:n, t, :], ident[0:n, 0:n])
                last.then_inc(gated_turned, 1)

            def combine(added_before):
                for d in range(KD):
                    if d >= 2:
                        pe.wait_ge(added, added_before + (d - 1))
                    pe.matmul(bank[6 + d % 2][:, 0:T], ysb[:, d * P:(d + 1) * P], gt[:, :], start=True, stop=True)\
                        .then_inc(combined, 1)

            pe.wait_ge(onehot_ready, 1)
            gather()
            pe.sem_inc(split_free, SPLITS)
            pe.sem_inc(gated_turned, 1)
            pe.wait_ge(y_cleared, 1)
            with pe.Fori(0, blocks) as b:
                pe.wait_ge(xg_ready, b + 1)
                pe.wait_ge(hT_taken, b + 1)
                for k in range(KD):
                    pe.wait_ge(hi_ready, b * 12 + (k + 1))
                    for n in range(4):
                        pe.matmul(bank[n][:, :], xg[:, k, :], hi[:, k % SPLITS, n * 512:(n + 1) * 512],
                                  start=k == 0, stop=False)
                    pe.wait_ge(lo_ready, b * 12 + (k + 1))
                    for n in range(4):
                        last = pe.matmul(bank[n][:, :], xg[:, k, :], lo[:, k % SPLITS, n * 512:(n + 1) * 512],
                                         start=False, stop=k == KD - 1)
                    last.then_inc(split_free, 1)
                pe.wait_ge(onehot_ready, b + 2)
                pe.wait_ge(added, b * 8 + 1)
                gather()
                pe.wait_ge(gated_ready, b + 1)
                turn_gates()
                pe.wait_ge(up_taken, b * 4 + 4)
                for f in range(FT):
                    last = pe.matmul(bank[f // 8][:, (f % 8) * CAP:(f % 8 + 1) * CAP], hsb[:, f * P:(f + 1) * P],
                                     stack, start=True, stop=True)
                    if f % 8 == 7:
                        last.then_inc(hT_done, 1)
                pe.wait_ge(gt_ready, b + 1)
                pe.wait_ge(y_ready, b * 2 + 2)
                pe.wait_ge(xg_ready, b + 2)
                combine(b * 8 + 1)
                pe.wait_ge(at_ready, b + 1)
                for i in range(8, 12):
                    h_, l_ = hi[:, i % SPLITS, :], lo[:, i % SPLITS, :]
                    for part, ready, src in ((0, hi_ready, h_), (1, lo_ready, l_)):
                        pe.wait_ge(ready, b * 12 + (i + 1))
                        for kk in range(2):
                            k = 2 * (i - 8) + kk
                            for n in range(2):
                                last = pe.matmul(bank[4 + n][:, :], at[:, k, :],
                                                 src[:, kk * D + n * 512:kk * D + (n + 1) * 512],
                                                 start=part == 0 and k == 0, stop=part == 1 and k == KD - 1)
                    last.then_inc(split_free, 1)

            pe.wait_ge(gated_ready, blocks + 1)
            pe.wait_ge(added, blocks * 8 + 1)
            turn_gates()
            pe.wait_ge(gt_ready, blocks + 1)
            pe.wait_ge(y_ready, blocks * 2 + 2)
            combine(blocks * 8 + 1)
            pe.wait_ge(ln2_loaded, 48)
            pe.wait_ge(added, blocks * 8 + 9)
            for t, (t0, n) in enumerate(TILES):
                for h in range(2):
                    o = bank[2 * t + h][0:n, :]
                    pe.matmul(o, gateT[:, t0:t0 + n], bdown[:, h * 512:(h + 1) * 512], start=True, stop=False)
                    for j in range(4):
                        last = pe.matmul(o[:, j * P:(j + 1) * P], yT[:, 4 * h + j, t0:t0 + n], ident,
                                         start=False, stop=j == 3)
                last.then_inc(final_done, 1)

        @block.vector
        def _(dve):
            steps = [0]

            def link(ins):
                steps[0] += 1
                ins.then_inc(v, 1)
                dve.wait_ge(v, steps[0])

            link(dve.memset(zero1[:, :], 0.0))
            link(dve.memset(epsc[:, :], EPS))
            link(dve.memset(kz[:, :, :], 0.0))
            link(dve.memset(xrp[:, :, 0:3], 0.0))
            link(dve.memset(posb[:, :, :], -1.0))
            link(dve.memset(gateb[:, :, :], 0.0))
            dve.memset(ones[:, :], 1.0).then_inc(ones_ready, 1)
            dve.wait_ge(par_turned, 2)
            dve.tensor_copy(par[:, :], bank[5][:, 0:80]).then_inc(par_ready, 1)
            dve.tensor_copy(stat[:, :, :], bank[6][:, 0:320].rearrange("p (n c) -> p n c", n=RT)).then_inc(par_ready, 1)
            dve.wait_ge(par_ready, 2)
            lam = par[:, 70:80]
            L = lambda i: lamt[:, i, :]
            link(dve.tensor_scalar(L(0), lam, -1.0, None, ALU.mult))
            dve.tensor_tensor(L(1), lam, L(0), ALU.max).then_inc(lam_in, 1)
            dve.wait_ge(lam_exp, 1)
            link(dve.tensor_scalar(L(3), L(2), 2.0, None, ALU.add))
            link(dve.reciprocal(L(3), L(3)))
            link(dve.tensor_tensor(L(3), L(2), L(3), ALU.mult))
            link(dve.tensor_tensor(L(4), L(3), L(3), ALU.mult))
            link(dve.memset(L(5), 1.0 / 19.0))
            for k in range(17, 0, -2):
                link(dve.tensor_tensor(L(5), L(5), L(4), ALU.mult))
                link(dve.tensor_scalar(L(5), L(5), 1.0 / k, None, ALU.add))
            link(dve.tensor_tensor(L(5), L(5), L(3), ALU.mult))
            link(dve.tensor_scalar(L(0), L(0), 0.0, None, ALU.max))
            link(dve.scalar_tensor_tensor(out=L(5), in0=L(5), scalar=2.0, in1=L(0), op0=ALU.mult, op1=ALU.add))
            link(dve.tensor_scalar(L(6), L(5), -8.0, None, ALU.mult))
            dve.tensor_scalar(L(7), L(5), 8.0, None, ALU.mult).then_inc(lam_ready, 1)

            dve.wait_ge(tile_evac, 2)
            for g in range(2):
                for q in range(2):
                    last = dve.tensor_copy(kz[q * 64:q * 64 + 64, 2 * g + q, P:P + SEQ], kT[g * 64:g * 64 + 64, 0:SEQ])
            last.then_inc(kz_ready, 1)
            dve.wait_ge(s_misc, 32)

            def softmax_head(h):
                dve.wait_ge(scored, h + 1)
                if h >= 2:
                    dve.wait_ge(probs_turned, h - 1)
                link(dve.scalar_tensor_tensor(out=lg[:, h % 2, :, :].rearrange("p b n -> p (b n)"),
                                              in0=const[:, C_DIST:C_DIST + 512], scalar=-slope(h),
                                              in1=bank[4 + h % 2][:, :], op0=ALU.mult, op1=ALU.add)
                     )
                dve.tensor_reduce(rmax[:, h % 2, :], lg[:, h % 2, :, :], AX.X, ALU.max).then_inc(scores_taken, 1)
                dve.wait_ge(scores_taken, h + 1)
                dve.tensor_scalar(negm[:, :, h], rmax[:, h % 2, :], sink[:, h:h + 1], -1.0, ALU.max, ALU.mult)\
                    .then_inc(max_ready, 1)

            def conv(n):
                xr_tile = 10 + n
                dve.wait_ge(tile_evac, xr_tile + 1)
                w = lambda j: par[:, j * RT + n:j * RT + n + 1]
                cb = par[:, 40 + n:41 + n]
                o, os_ = xc[:, n, 0:SEQ], xc[:, n, SEQ:T]
                dve.tensor_scalar(o, xrp[:, n, 0:SEQ], w(0), cb, ALU.mult, ALU.add)
                link(dve.tensor_scalar(os_, stat[:, n, 0:24:3], w(0), cb, ALU.mult, ALU.add))
                for j in range(1, CONV):
                    dve.scalar_tensor_tensor(out=o, in0=xrp[:, n, j:j + SEQ], scalar=w(j), in1=o,
                                             op0=ALU.mult, op1=ALU.add)
                    src = stat[:, n, j:24:3] if j < 3 else xrs[:, n, :]
                    ins = dve.scalar_tensor_tensor(out=os_, in0=src, scalar=w(j), in1=os_, op0=ALU.mult, op1=ALU.add)
                    if j < CONV - 1:
                        link(ins)
                    else:
                        ins.then_inc(conv_ready, 1)

            for what, n in order:
                if what == "step" and n < NH:
                    softmax_head(n)
                    if n < RT:
                        conv(n)
                elif what == "sample" and n == 0:
                    link(dve.memset(qz, 0.0))
                    for g in range(2):
                        for q in range(2):
                            src = qT[q * 64:q * 64 + 64, 4 * g:4 * g + 4, SEQ:T].rearrange("p f b -> p b f")
                            last = dve.tensor_copy(qz[g * 64:g * 64 + 64, :, 8 * g + q:8 * g + 8:2], src)
                    last.then_inc(s_qz, 1)
                elif what == "sample" and n == 1:
                    dve.wait_ge(s_sc, 1)
                    dist = const[0:NH, C_TDIST:C_TDIST + P].unsqueeze(1).broadcast_to([NH, 4, P])
                    for j in range(2):
                        ins = dve.scalar_tensor_tensor(out=slog[:, 4 * j:4 * j + 4, :], in0=dist,
                                                       scalar=const[0:NH, C_SLOPE:C_SLOPE + 1],
                                                       in1=bank[6 + j][0:NH, :].rearrange("p (b n) -> p b n", b=4),
                                                       op0=ALU.mult, op1=ALU.add)
                    link(ins)
                    link(dve.tensor_reduce(srow[:, 0, :], slog, AX.X, ALU.max))
                    link(dve.tensor_scalar(srow[:, 0, :], srow[:, 0, :], sinkc[:, 0:1], None, ALU.max))
                    dve.tensor_scalar(srow[:, 1, :], srow[:, 0, :], -1.0, sinkc[:, 0:1], ALU.mult, ALU.add)
                    dve.tensor_tensor(slog, slog, srow[:, 0, :].unsqueeze(2).broadcast_to([NH, DECB, P]),
                                      ALU.subtract).then_inc(s_sm, 1)
                    dve.wait_ge(s_ex, 2)
                    link(dve.tensor_reduce(srow[:, 2, :], slog, AX.X, ALU.add))
                    link(dve.tensor_tensor(srow[:, 2, :], srow[:, 2, :], srow[:, 1, :], ALU.add))
                    link(dve.reciprocal(srow[:, 3, :], srow[:, 2, :]))
                    dve.tensor_tensor(slog, slog, srow[:, 3, :].unsqueeze(2).broadcast_to([NH, DECB, P]),
                                      ALU.mult).then_inc(s_pn, 1)
                elif what == "sample" and n == 3:
                    dve.wait_ge(s_pv, 1)
                    ps = bank[5][:, 0:P].rearrange("p (b h) -> p b h", b=DECB)
                    for g in range(2):
                        for q in range(2):
                            dst = oT[q * 64:q * 64 + 64, 4 * g:4 * g + 4, SEQ:T].rearrange("p f b -> p b f")
                            last = dve.tensor_copy(dst, ps[g * 64:g * 64 + 64, :, 8 * g + q:8 * g + 8:2])
                    last.then_inc(s_os, 1)
                if what == "step" and n == NH + 1:
                    dve.wait_ge(probs_ready, NH)
                    dve.wait_ge(max_ready, NH)
                    dve.tensor_tensor(esk[:, :, :], negm[:, :, :],
                                      sink[:, :].unsqueeze(1).broadcast_to([P, 2, NH]), ALU.add).then_inc(den_in, 1)
                    dve.wait_ge(sinkexp, 1)
                    link(dve.tensor_tensor(esk[:, :, :], esk[:, :, :], rsum[:, :, :], ALU.add))
                    link(dve.reciprocal(esk[:, :, :], esk[:, :, :]))
                    dve.wait_ge(o_ready, NH)
                    for blk in range(2):
                        o = otok[:, blk, :].rearrange("p (h d) -> p h d", h=NH)
                        dve.tensor_tensor(o, o, esk[:, blk, :].unsqueeze(2).broadcast_to([P, NH, HD]), ALU.mult)\
                            .then_inc(o_norm, 1)

            dve.wait_ge(tanh_done, RT)
            link(dve.tensor_copy(pack[:, :, 0:3], xrp[:, :, SEQ:SEQ + 3]))
            link(dve.tensor_scalar(den[:, :, :], sg[:, :, :], 1.0, None, ALU.add))
            link(dve.reciprocal(den[:, :, :], den[:, :, :]))
            dve.tensor_tensor(sg[:, :, :], sg[:, :, :], den[:, :, :], ALU.mult).then_inc(ratio_ready, 1)
            dve.wait_ge(gates_done, 2)
            link(dve.tensor_tensor(ig[:, :, :], ig[:, :, :], xc[:, :, :], ALU.mult))
            dve.wait_ge(root_done, 1)
            link(dve.tensor_tensor(ig[:, :, :], ig[:, :, :], sg[:, :, :], ALU.mult))
            dve.wait_ge(decay_done, RT)
            for n in range(RT):
                dve.tensor_tensor_scan(hrec[:, n, 0:SEQ], rg[:, n, 0:SEQ], ig[:, n, 0:SEQ], 0.0, ALU.mult, ALU.add)
            link(dve.tensor_tensor(hrec[:, :, SEQ:T], rg[:, :, SEQ:T], stat[:, :, 24:32], ALU.mult))
            link(dve.tensor_tensor(hrec[:, :, SEQ:T], hrec[:, :, SEQ:T], ig[:, :, SEQ:T], ALU.add))
            dve.wait_ge(gelu_done, 1)
            dve.tensor_tensor(yr[:, :, :], yr[:, :, :], hrec[:, :, :], ALU.mult).then_inc(y_rnn_ready, 1)
            dve.tensor_copy(pack[:, :, 3:4], hrec[:, :, SEQ - 1:SEQ])
            dve.tensor_copy(pack[:, :, 4:12], xrs[:, :, :])
            dve.tensor_copy(pack[:, :, 12:20], hrec[:, :, SEQ:T]).then_inc(pack_ready, 1)

            dve.wait_ge(gates_done, 4)
            for m in range(16):
                dve.wait_ge(out_done, m + 1)
                ps = bank[m % 4][:, 0:T]
                if m < 8:
                    dve.tensor_tensor(ga[:, m, :], ga[:, m, :], ps, ALU.mult).then_inc(out_evac, 1)
                else:
                    f = m - 8
                    dve.tensor_tensor(gb[:, f, :], gb[:, f, :], ps, ALU.mult).then_inc(out_evac, 1)
                    dve.wait_ge(out_evac, m + 1)
                    dve.tensor_tensor(ga[:, f, :], ga[:, f, :], gb[:, f, :], ALU.add).then_inc(merged_ready, 1)

            def norm(psums, var_sem, sd_sem, g_row, b_row, done):
                for t, (_, n) in enumerate(TILES):
                    for h in range(2):
                        x = xtok[0:n, t, h * 512:(h + 1) * 512]
                        link(dve.scalar_tensor_tensor(out=x, in0=x, scalar=ALPHA, in1=psums[t][h][0:n, :],
                                                      op0=ALU.mult, op1=ALU.add))
                        link(dve.bn_stats(stats[0:n, t, h * 6:h * 6 + 6], x))
                    dve.bn_aggr(mv[0:n, t, :], stats[0:n, t, :]).then_inc(var_sem, 1)
                for t, (_, n) in enumerate(TILES):
                    x = xtok[0:n, t, :]
                    dve.wait_ge(sd_sem, t + 1)
                    link(dve.reciprocal(rstd[0:n, t:t + 1], sd[0:n, t:t + 1]))
                    link(dve.tensor_scalar(x, x, mv[0:n, t, 0:1], rstd[0:n, t:t + 1], ALU.subtract, ALU.mult))
                    link(dve.tensor_tensor(x, x, g_row[0:n, :], ALU.mult))
                    dve.tensor_tensor(x, x, b_row[0:n, :], ALU.add).then_inc(done, 1)

            dve.wait_ge(mix_done, 4)
            chunk_ready(dve, CH_LN)
            norm([(bank[4], bank[5]), (bank[6], bank[7]), (bank[0], bank[1])], var_ready, sd_ready,
                 slot(CH_LN)[:, 0:D], slot(CH_LN)[:, D:2 * D], x1_ready)

            dve.wait_ge(logits_done, 1)
            dve.wait_ge(s_bd, 32)
            R = lambda i, t, n: rt[0:n, i, t, :]
            for t, (_, n) in enumerate(TILES):
                l = lgt[0:n, t, :]
                v4 = m8[0:n, t, TOPK - 1:TOPK]
                link(dve.tensor_tensor(l, bank[5][0:n, t * NE:(t + 1) * NE], brb[0:n, :], ALU.add))
                link(dve.max(m8[0:n, t, :], l))
                dve.tensor_scalar(rsm[0:n, 0, t:t + 1], m8[0:n, t, 0:1], -1.0, None, ALU.mult).then_inc(top_ready, 1)
                dve.tensor_scalar(R(1, t, n), l, v4, None, ALU.is_equal)
                link(dve.tensor_scalar(R(0, t, n), l, v4, None, ALU.is_gt))
                link(dve.tensor_reduce(rsm[0:n, 1, t:t + 1], R(0, t, n), AX.X, ALU.add))
                link(dve.tensor_scalar(rsm[0:n, 1, t:t + 1], rsm[0:n, 1, t:t + 1], -1.0, float(TOPK),
                                       ALU.mult, ALU.add))
                link(dve.tensor_tensor_scan(R(2, t, n), ones[0:n, 0:NE], R(1, t, n), 0.0, ALU.mult, ALU.add))
                link(dve.scalar_tensor_tensor(out=R(3, t, n), in0=R(2, t, n), scalar=rsm[0:n, 1, t:t + 1],
                                              in1=R(1, t, n), op0=ALU.is_le, op1=ALU.mult))
                dve.tensor_tensor(R(4, t, n), R(0, t, n), R(3, t, n), ALU.add).then_inc(mask_ready, 1)
            dve.wait_ge(mask_ready, 3)
            for t, (_, n) in enumerate(TILES):
                dve.wait_ge(exp_ready, t + 1)
                link(dve.tensor_tensor(R(5, t, n), R(5, t, n), R(4, t, n), ALU.mult))
                link(dve.tensor_reduce(rsm[0:n, 2, t:t + 1], R(5, t, n), AX.X, ALU.add))
                link(dve.reciprocal(rsm[0:n, 3, t:t + 1], rsm[0:n, 2, t:t + 1]))
                link(dve.tensor_scalar(R(7, t, n), R(5, t, n), rsm[0:n, 3, t:t + 1], None, ALU.mult))
            dve.wait_ge(count_done, 1)
            for t, (_, n) in enumerate(TILES):
                link(dve.scalar_tensor_tensor(out=R(6, t, n), in0=bank[6][0:n, t * NE:(t + 1) * NE], scalar=BIG,
                                              in1=R(4, t, n), op0=ALU.add, op1=ALU.mult))
                dve.tensor_scalar(R(6, t, n), R(6, t, n), BIG, None, ALU.subtract).then_inc(route_ready, 1)
            count = bank[7][0:NE, 0:1]
            link(dve.tensor_scalar(ov[:, 2:3], count, float(CAP), None, ALU.is_gt))
            for j in range(2, 5):
                src, dst = (j, j + 1) if j < 4 else (4, 1)
                ins = dve.scalar_tensor_tensor(out=ov[:, dst:dst + 1], in0=count, scalar=float(j * CAP),
                                               in1=ov[:, src:src + 1], op0=ALU.is_gt, op1=ALU.add)
                if j < 4:
                    link(ins)
                else:
                    ins.then_inc(over_ready, 1)
            dve.wait_ge(start_done, 1)
            dve.wait_ge(over_ready, 1)
            oi = const[0:NE, C_OV:C_OV + MAXOVER]
            link(dve.tensor_copy(ov[:, 5:6], bank[7][0:NE, 8:9]))
            link(dve.tensor_tensor(ov[:, 6:7], ov[:, 5:6], ov[:, 1:2], ALU.add))
            link(dve.tensor_scalar(ohw[:, 0, :], oi, ov[:, 5:6], None, ALU.is_ge))
            link(dve.scalar_tensor_tensor(out=ohw[:, 1, :], in0=oi, scalar=ov[:, 6:7], in1=ohw[:, 0, :],
                                          op0=ALU.is_lt, op1=ALU.mult))
            link(dve.tensor_scalar(ohw[:, 2, :], oi, ov[:, 5:6], None, ALU.subtract))
            link(dve.tensor_scalar(ohw[:, 2, :], ohw[:, 2, :], -float(CAP), -float(CAP), ALU.mult, ALU.add))
            dve.memset(negj[:, 0:NE], 0.0)
            dve.tensor_tensor(negj[:, NE:NB], ohw[:, 2, :], ohw[:, 1, :], ALU.mult)
            dve.tensor_copy(selm[:, 0:NE], ident[0:NE, 0:NE])
            dve.tensor_copy(selm[:, NE:NB], ohw[:, 1, :])
            dve.wait_ge(route_turned, 1)
            dve.tensor_copy(posmT[:, :], bank[0][0:NE, 0:T])
            dve.tensor_copy(gateT[:, :], bank[1][0:NE, 0:T]).then_inc(routeT_ready, 1)
            dve.wait_ge(table_done, 1)
            for t, (_, n) in enumerate(TILES):
                dve.tensor_copy(posb[0:n, 1:1 + NB, t], bank[2][0:n, t * NB:(t + 1) * NB])
                dve.tensor_copy(gateb[0:n, 1:1 + NB, t], bank[3][0:n, t * NB:(t + 1) * NB])
            for half in range(2):
                dve.tensor_copy(bup[:, 8 * half:8 * half + 8, :],
                                bank[5 + half][:, 0:8 * NB].rearrange("p (f n) -> p f n", f=8))
            dve.tensor_copy(tablei[0:1, 0:NB], bank[7][0:1, 32:32 + NB])
            link(dve.tensor_scalar(tablei[0:1, NB:NB + 1], bank[7][0:1, 16:17], float(NE), None, ALU.add))
            dve.wait_ge(s_out, 16 * N_OUT)
            link(dve.memset(yT[:, :, :], 0.0))
            link(dve.memset(bank[4][:, :], 0.0))
            dve.memset(bank[5][:, :], 0.0).then_inc(y_cleared, 1)
            dve.wait_ge(y_cleared, 1)

            def one_hot(col, done):
                for t, (_, n) in enumerate(TILES):
                    ins = dve.tensor_scalar(onehot[0:n, t, :], iota[0:n, 0:CAP], posb[0:n, col, t], None, ALU.is_equal)
                ins.then_inc(done, 1)

            def gates(col, done):
                for t, (_, n) in enumerate(TILES):
                    ins = dve.tensor_scalar(gated[0:n, t, :], iota[0:n, :], posb[0:n, col, t], gateb[0:n, col, t],
                                            ALU.is_equal, ALU.mult)
                ins.then_inc(done, 1)

            def xg_low(count):
                dve.wait_ge(xg_high, count)
                dve.tensor_tensor(xg[:, :, CAP:P], bank[6][:, :].rearrange("p (d n) -> p d n", d=KD),
                                  xg[:, :, 0:CAP].bitcast(F32), ALU.subtract).then_inc(xg_ready, 1)

            def add(d, count):
                dve.wait_ge(combined, count)
                dve.tensor_tensor(yT[:, d, :], yT[:, d, :], bank[6 + d % 2][:, 0:T], ALU.add).then_inc(added, 1)

            one_hot(bass.ds(1, 1), onehot_ready)
            dve.sem_inc(hT_taken, 1)
            dve.sem_inc(added, 1)
            dve.sem_inc(table_ready, 1)
            blocks = dve.value_load(tablei[0:1, NB:NB + 1], min_val=NE, max_val=NB)
            xg_low(1)
            with dve.Fori(0, blocks) as b:
                inner = [0]

                def chain(ins):
                    inner[0] += 1
                    ins.then_inc(vm, 1)
                    dve.wait_ge(vm, b * CHAIN + inner[0])

                def split(i):
                    dve.wait_ge(hi_ready, b * 12 + (i + 1))
                    dve.tensor_tensor(lo[:, i % SPLITS, :], slot(NCH + i), hi[:, i % SPLITS, :].bitcast(F32),
                                      ALU.subtract).then_inc(lo_ready, 1)

                dve.wait_ge(gathered, b + 1)
                one_hot(bass.ds(b + 2, 1), onehot_ready)
                dve.wait_ge(gated_turned, b + 1)
                gates(bass.ds(b, 1), gated_ready)
                for i in range(10):
                    split(i)
                xg_low(b + 2)
                dve.wait_ge(hT_done, b * 2 + 1)
                chain(dve.tensor_tensor(glu[:, :, :], bank[0][:, :].rearrange("p (f n) -> p f n", f=KD),
                                        bup[:, 0:KD, bass.ds(b, 1)].broadcast_to([P, KD, CAP]), ALU.add))
                dve.tensor_scalar(glu[:, :, :], glu[:, :, :], LIMIT, None, ALU.min).then_inc(glu_ready, 1)
                dve.wait_ge(hT_done, b * 2 + 2)
                dve.tensor_tensor(lin[:, :, :], bank[1][:, :].rearrange("p (f n) -> p f n", f=KD),
                                  bup[:, KD:FT, bass.ds(b, 1)].broadcast_to([P, KD, CAP]), ALU.add)\
                    .then_inc(hT_taken, 1)
                dve.wait_ge(hT_taken, b + 2)
                chain(dve.tensor_scalar(lin[:, :, :], lin[:, :, :], LIMIT, -LIMIT, ALU.min, ALU.max))
                split(10)
                dve.wait_ge(sig_ready, b + 1)
                chain(dve.tensor_tensor(act_[:, :, :], glu[:, :, :], sig[:, :, :], ALU.mult))
                dve.scalar_tensor_tensor(out=act_[:, :, :], in0=lin[:, :, :], scalar=1.0, in1=act_[:, :, :],
                                         op0=ALU.add, op1=ALU.mult).then_inc(act_ready, 1)
                dve.wait_ge(at_high, b + 1)
                dve.tensor_tensor(at[:, :, CAP:P], act_[:, :, :], at[:, :, 0:CAP].bitcast(F32), ALU.subtract)\
                    .then_inc(at_ready, 1)
                for d in range(KD):
                    add(d, b * 8 + (d + 1))
                split(11)
                assert inner[0] == CHAIN
            dve.wait_ge(gated_turned, blocks + 1)
            gates(bass.ds(blocks, 1), gated_ready)
            for d in range(KD):
                add(d, blocks * 8 + (d + 1))
            dve.wait_ge(final_done, 3)
            dve.wait_ge(ln2_loaded, 48)
            norm([(bank[0], bank[1]), (bank[2], bank[3]), (bank[4], bank[5])], var2_ready, sd2_ready,
                 raw[:, 0, 0:D], raw[:, 0, D:2 * D], fin_ready)


INS = ["x_prompt", "x_sample", "cache_k", "cache_v", "state_conv", "state_h", "w_in", "attn_sinks", "conv_w", "conv_b",
       "rg_wa", "rg_ba", "rg_wx", "rg_bx", "rg_lambda", "w_attn_out", "w_rnn_out", "w_out", "ln1_g", "ln1_b",
       "w_router", "b_router", "w_up", "b_up", "w_down", "b_down", "ln2_g", "ln2_b"]
OUTS = [("o_yp", (1, SEQ, D)), ("o_ys", (DECB, 1, D)), ("o_kp", (1, 1, WIN, NKV, HD)), ("o_vp", (1, 1, WIN, NKV, HD)),
        ("o_cp", (1, 1, CONV - 1, DR)), ("o_hp", (1, 1, DR)), ("o_ks", (1, DECB, WIN, NKV, HD)),
        ("o_vs", (1, DECB, WIN, NKV, HD)), ("o_cs", (1, DECB, CONV - 1, DR)), ("o_hs", (1, DECB, DR))]


def kernel(**inputs):
    import concourse.bacc as bacc
    from concourse.bass_utils import run_bass_kernel_spmd

    nc = bacc.Bacc("TRN2", target_bir_lowering=False, num_devices=1)
    arrays, aps = {}, {}
    for name in INS + ["consts"]:
        x = constants() if name == "consts" else np.ascontiguousarray(inputs[name])
        arrays["in_" + name] = x
        aps[name] = nc.dram_tensor("in_" + name, x.shape, mybir.dt.from_np(x.dtype), kind="ExternalInput").ap()
    for name, shape in OUTS:
        aps[name] = nc.dram_tensor("out_" + name, shape, F32, kind="ExternalOutput").ap()
    build(nc, aps)
    r = run_bass_kernel_spmd(nc, [arrays], core_ids=[0])
    return tuple(r.results[0]["out_" + name] for name, _ in OUTS)
```

```python
from contextlib import ExitStack

import numpy as np

import concourse.bass as bass
from concourse import mybir

F32 = mybir.dt.float32
F32R = mybir.dt.float32r
I32 = mybir.dt.int32
ALU = mybir.AluOpType
ACT = mybir.ActivationFunctionType
AX = mybir.AxisListType

P = 128
D = 1024
SEQ, DECB = 256, 8
T = SEQ + DECB
KD = D // P
TILES = [(0, 128), (128, 128), (256, 8)]
NH, NKV, HD = 16, 2, 64
GROUP = NH // NKV
WIN = 128
KVW = NKV * HD
DR = 1280
RT = DR // P
CONV = 4
NE, TOPK, DFF = 32, 4, 1024
FT = 2 * DFF // P
LIMIT, SALPHA = 7.0, 1.702
ALPHA = 2.0 ** 0.25
EPS = 1e-5
PROJ = D + 2 * KVW + 2 * DR + 2 * D
CAP = 64
N_OUT = 11
CHAIN = 16
MAXOVER = 16
NB = NE + MAXOVER
NCOL = NB + 2
BIG = 4096.0
INVALID = 1e30

RING = 6
SLOT = 2048
SPLITS = 4
UPC = 8
NG = 4
ON_POOL = (2, 6, 10)
ON_DVE = tuple(i for i in range(12) if i not in ON_POOL)

C_ID, C_STACK, C_TRI, C_IOTA, C_DIST = 0, 128, 192, 320, 448
C_TDIST = C_DIST + 512
C_SLOPE = C_TDIST + 128
C_OV = C_SLOPE + 1
C_EIDX = C_OV + MAXOVER
C_W = C_EIDX + 1


def constants():
    c = np.zeros((P, C_W), np.float32)
    p = np.arange(P)[:, None]
    j = np.arange(P)[None, :]
    c[:, C_ID:C_ID + P] = p == j
    c[:, C_STACK:C_STACK + CAP] = (p % CAP) == np.arange(CAP)[None, :]
    c[:, C_TRI:C_TRI + P] = p < j
    c[:, C_IOTA:C_IOTA + P] = j % CAP
    for blk in range(2):
        prev = p + WIN - j
        cur = p - j
        c[:, C_DIST + 256 * blk:C_DIST + 256 * blk + 128] = np.where((prev < WIN) & (blk > 0), prev, INVALID)
        c[:, C_DIST + 256 * blk + 128:C_DIST + 256 * blk + 256] = np.where(cur >= 0, cur, INVALID)
    c[:, C_TDIST:C_TDIST + P] = WIN - 1 - j
    c[:NH, C_SLOPE] = [-slope(h) for h in range(NH)]
    c[:, C_OV:C_OV + MAXOVER] = np.arange(MAXOVER)[None, :]
    c[:, C_EIDX] = np.arange(P)
    return c


def slope(h):
    return float(np.float32(2.0) ** np.float32(-8.0 * (h + 1) / NH))


def plan():
    def cols(base, width):
        return [("win", base + 256 * i) for i in range(width // 256)]
    off_k, off_xr = D, D + 2 * KVW
    off_yr, off_ga, off_gb = off_xr + DR, off_xr + 2 * DR, off_xr + 2 * DR + D
    chunks, tiles = [], []

    def section(names, base, width):
        for i, c in enumerate(cols(base, width)):
            chunks.append(c)
            for half in range(2):
                tiles.append((names, 2 * i + half, len(chunks) - 1, half))

    section("kv", off_k, 2 * KVW)
    section("q", 0, D)
    section("xr", off_xr, DR)
    section("yr", off_yr, DR)
    for name, what in (("r", "wa"), ("i", "wx")):
        chunks.append((what, 0))
        tiles.extend((name, n, len(chunks) - 1, 0) for n in range(RT))
    section("ga", off_ga, D)
    section("gb", off_gb, D)
    order = []
    step = 0
    for n, (name, idx, _, _) in enumerate(tiles):
        order.append(("tile", n))
        if n == 3:
            order.append(("kvturn", 0))
        if name == "yr" or (name in ("ga", "gb") and step < NH + 2):
            order.append(("step", step))
            step += 1
        if name == "gb" and idx in (2, 3, 5, 7):
            order.append(("sample", (2, 3, 5, 7).index(idx)))
    assert step == NH + 2
    n_tiles_chunks = len(chunks)
    chunks += [("wao", 256 * i) for i in range(4)] + [("wro", P * i) for i in range(8)]
    chunks += [("wout", 2 * i) for i in range(4)] + [("ln1", 0), ("bup", 0)]
    return chunks, tiles, order, n_tiles_chunks


def build(nc, a):
    chunks, tiles, order, NPC = plan()
    NCH = len(chunks)
    CH_AO, CH_RO, CH_OUT, CH_LN, CH_BUP = NPC, NPC + 4, NPC + 12, NPC + 16, NPC + 17
    NT1 = len(tiles)

    def flat(name):
        ap = a[name]
        return ap[0]

    with ExitStack() as whole:
        def sb(name, shape, dt=F32, scope=whole):
            return scope.enter_context(nc.sbuf_tensor(name, shape, dt))

        def sem(name):
            return whole.enter_context(nc.semaphore(name))

        bank = [whole.enter_context(nc.psum_tensor(f"bank{i}", [P, 512], F32)) for i in range(8)]

        const = sb("const", [P, C_W])
        ident = const[:, C_ID:C_ID + P]
        stack = const[:, C_STACK:C_STACK + CAP]
        iota = const[:, C_IOTA:C_IOTA + P]
        raw = sb("raw", [P, RING, SLOT])
        xtok = sb("xtok", [P, 3, D])
        bdown = raw[0:NE, 1, 0:D]
        gateT = sb("gateT", [NE, T])
        posb = sb("posb", [P, NCOL, 3])
        gateb = sb("gateb", [P, NCOL, 3])
        bup = sb("bup", [P, FT, NB])
        tablei = sb("tablei", [1, NB + 2], I32)
        ones = sb("ones", [P, P])
        stats = sb("stats", [P, 3, 12])
        mv = sb("mv", [P, 3, 2])
        sd = sb("sd", [P, 3])
        rstd = sb("rstd", [P, 3])
        warm = sb("warm", [P, 1])
        epsc = sb("epsc", [P, 1])

        early = ExitStack()
        xT = sb("xT", [P, KD, T], scope=early)
        first = ExitStack()
        parr = sb("parr", [80, P], scope=first)
        statr = sb("statr", [32, DR], scope=first)
        first.close()
        lg = sb("lg", [P, 2, 2, 256], scope=early)
        rmax = sb("rmax", [P, 2, 2], scope=early)
        spare = sb("spare", [P, 384], scope=early)
        par = sb("par", [P, 80], scope=early)
        stat = sb("stat", [P, RT, 32], scope=early)
        sink = sb("sink", [P, NH], scope=early)
        sinkc = sb("sinkc", [NH, 1], scope=early)
        wr = sb("wr", [P, KD, NE], scope=early)
        brb = sb("brb", [P, NE], scope=early)
        kT = sb("kT", [P, T], scope=early)
        vT = sb("vT", [P, T], scope=early)
        kz = sb("kz", [P, 4, 384], scope=early)
        vtok = sb("vtok", [P, 2, P], scope=early)
        ktok = sb("ktok", [P, P], scope=early)
        kv8 = sb("kv8", [DECB, 2, P], scope=early)
        qT = sb("qT", [P, KD, T], scope=early)
        pT = sb("pT", [P, 2, 384], scope=early)
        negm = sb("negm", [P, 2, NH], scope=early)
        rsum = sb("rsum", [P, 2, NH], scope=early)
        esk = sb("esk", [P, 2, NH], scope=early)
        otok = sb("otok", [P, 2, D], scope=early)
        oT = qT
        kc = sb("kc", [P, DECB, KVW], scope=early)
        vc = sb("vc", [P, DECB, KVW], scope=early)
        xrp = sb("xrp", [P, RT, T], scope=early)
        xrs = sb("xrs", [P, RT, DECB], scope=early)
        xc = sb("xc", [P, RT, T], scope=early)
        yr = sb("yr", [P, RT, T], scope=early)
        rg = sb("rg", [P, RT, T], scope=early)
        ig = sb("ig", [P, RT, T], scope=early)
        ga = sb("ga", [P, KD, T], scope=early)
        gb = sb("gb", [P, KD, T], scope=early)
        sg = sb("sg", [P, RT, T], scope=early)
        den = xrp
        hrec = xc
        sgf = sg[:, :, :].rearrange("p a b -> p (a b)")
        kcT = sgf[:, 0:1024].rearrange("p (b k) -> p b k", b=DECB)
        slog = sgf[0:NH, 1024:2048].rearrange("p (b k) -> p b k", b=DECB)
        qz = sgf[:, 2048:2176].rearrange("p (b h) -> p b h", b=DECB)
        pTs = sgf[:, 2176:2304].rearrange("p (b h) -> p b h", b=DECB)
        srow = sb("srow", [NH, 4, DECB], scope=early)
        pack = sb("pack", [P, RT, 20], scope=early)
        lamt = sb("lamt", [P, 8, RT], scope=early)
        rgf = rg[:, :, :].rearrange("p a b -> p (a b)")
        rt = rgf[:, 0:768].rearrange("p (i t e) -> p i t e", i=8, t=3)
        lgt = rgf[:, 768:864].rearrange("p (t e) -> p t e", t=3)
        m8 = rgf[:, 864:888].rearrange("p (t e) -> p t e", t=3)
        rsm = rgf[:, 888:900].rearrange("p (i t) -> p i t", i=4)
        posmT = rgf[0:NE, 900:900 + T]
        ov = rgf[0:NE, 1164:1172]
        selm = rgf[0:NE, 1172:1172 + NB]
        negj = rgf[0:NE, 1220:1220 + NB]
        ohw = rgf[0:NE, 1268:1268 + 3 * MAXOVER].rearrange("p (i o) -> p i o", i=3)
        rows = otok[0:20, :, :].rearrange("p a b -> p (a b)")[:, 0:DR]
        early.close()

        late = ExitStack()
        hi = sb("hi", [P, SPLITS, SLOT], F32R, scope=late)
        lo = sb("lo", [P, SPLITS, SLOT], F32R, scope=late)
        xg = sb("xg", [P, KD, P], F32R, scope=late)
        at = sb("at", [P, KD, P], F32R, scope=late)
        hsb = sb("hsb", [P, 2, 512], scope=late)
        xh = sb("xh", [P, 3, D], F32R, scope=late)
        xl = sb("xl", [P, 3, D], F32R, scope=late)
        ysb = sb("ysb", [P, D], scope=late)
        gt = sb("gt", [P, T], scope=late)
        onehot = sb("onehot", [P, 3, 3 * CAP], F32R, scope=late)
        gx = sb("gx", [P, D], scope=late)
        gated = sb("gated", [P, 3, P], scope=late)
        glin = sb("glin", [P, 2, 4, CAP], scope=late)
        sig = sb("sig", [P, 2, 2, CAP], scope=late)
        act_ = sb("act_", [P, 2, 2, CAP], scope=late)
        yT = sb("yT", [P, KD, T], scope=late)
        late.close()

        s_const = sem("s_const")
        s_x = sem("s_x")
        s_par = sem("s_par")
        s_misc = sem("s_misc")
        s_cache = sem("s_cache")
        s_new = sem("s_new")
        s_bd = sem("s_bd")
        s_out = sem("s_out")
        y_out = sem("y_out")
        loaded = [sem(f"loaded{i}") for i in range(RING)]
        ones_ready = sem("ones_ready")
        x_turned = sem("x_turned")
        xT_ready = sem("xT_ready")
        par_turned = sem("par_turned")
        par_ready = sem("par_ready")
        tile_done = sem("tile_done")
        tile_evac = sem("tile_evac")
        kv_turned = sem("kv_turned")
        kv_ready = sem("kv_ready")
        kz_ready = sem("kz_ready")
        scored = sem("scored")
        scores_taken = sem("scores_taken")
        max_ready = sem("max_ready")
        probs_ready = sem("probs_ready")
        probs_turned = sem("probs_turned")
        pT_ready = sem("pT_ready")
        pv_done = sem("pv_done")
        o_ready = sem("o_ready")
        den_in = sem("den_in")
        sinkexp = sem("sinkexp")
        o_norm = sem("o_norm")
        o_turned = sem("o_turned")
        oT_ready = sem("oT_ready")
        conv_ready = sem("conv_ready")
        lam_in = sem("lam_in")
        lam_exp = sem("lam_exp")
        lam_ready = sem("lam_ready")
        gates_done = sem("gates_done")
        tanh_done = sem("tanh_done")
        ratio_ready = sem("ratio_ready")
        root_done = sem("root_done")
        decay_done = sem("decay_done")
        gelu_done = sem("gelu_done")
        y_rnn_ready = sem("y_rnn_ready")
        s_kt = sem("s_kt")
        s_kte = sem("s_kte")
        s_qz = sem("s_qz")
        s_sc = sem("s_sc")
        s_sm = sem("s_sm")
        s_ex = sem("s_ex")
        s_pn = sem("s_pn")
        s_ptt = sem("s_ptt")
        s_pte = sem("s_pte")
        s_pv = sem("s_pv")
        s_os = sem("s_os")
        out_done = sem("out_done")
        out_evac = sem("out_evac")
        merged_ready = sem("merged_ready")
        mix_done = sem("mix_done")
        pack_ready = sem("pack_ready")
        pack_turned = sem("pack_turned")
        rows_ready = sem("rows_ready")
        var_ready = sem("var_ready")
        sd_ready = sem("sd_ready")
        x1_ready = sem("x1_ready")
        x1_turned = sem("x1_turned")
        x1T_ready = sem("x1T_ready")
        logits_done = sem("logits_done")
        top_ready = sem("top_ready")
        exp_ready = sem("exp_ready")
        mask_ready = sem("mask_ready")
        count_done = sem("count_done")
        over_ready = sem("over_ready")
        start_done = sem("start_done")
        route_ready = sem("route_ready")
        route_turned = sem("route_turned")
        routeT_ready = sem("routeT_ready")
        table_done = sem("table_done")
        table_ready = sem("table_ready")
        v = sem("v")
        vm = sem("vm")
        onehot_ready = sem("onehot_ready")
        gated_ready = sem("gated_ready")
        gathered = sem("gathered")
        gx_ready = sem("gx_ready")
        gx_turned = sem("gx_turned")
        gated_turned = sem("gated_turned")
        gt_ready = sem("gt_ready")
        xh_ready = sem("xh_ready")
        xl_ready = sem("xl_ready")
        xg_ready = sem("xg_ready")
        split_free = sem("split_free")
        hi_ready = sem("hi_ready")
        lo_ready = sem("lo_ready")
        lo_pool_ready = sem("lo_pool_ready")
        up_taken = sem("up_taken")
        hT_done = sem("hT_done")
        hT_taken = sem("hT_taken")
        glu_ready = sem("glu_ready")
        lin_ready = sem("lin_ready")
        sig_ready = sem("sig_ready")
        at_ready = sem("at_ready")
        y_ready = sem("y_ready")
        combined = sem("combined")
        added = sem("added")
        y_cleared = sem("y_cleared")
        final_done = sem("final_done")
        var2_ready = sem("var2_ready")
        sd2_ready = sem("sd2_ready")
        ln2_loaded = sem("ln2_loaded")
        fin_ready = sem("fin_ready")

        def slot(c):
            return raw[:, c % RING, :]

        def loads(c):
            return sum(2 if chunks[x][0] == "ln1" else 1 for x in range(c % RING, min(c + 1, NCH), RING)) \
                + sum(2 if (x - NCH) % 12 < UPC else 1 for x in range(NCH, c + 1) if x % RING == c % RING)

        def chunk_ready(e, c):
            e.wait_ge(loaded[c % RING], 16 * loads(c))

        def low_ready(e, i, b):
            if i in ON_POOL:
                e.wait_ge(lo_pool_ready, b * len(ON_POOL) + (ON_POOL.index(i) + 1))
            else:
                e.wait_ge(lo_ready, b * len(ON_DVE) + (ON_DVE.index(i) + 1))

        CBANK = (6, 7)
        LOADED0 = [16 * loads(NCH + i) for i in range(12)]
        PER_BLOCK = [16 * (loads(NCH + i + 12) - loads(NCH + i)) for i in range(12)]

        block = whole.enter_context(nc.Block())

        @block.sync
        def _(sp):
            win = flat("w_in").rearrange("(k p) n -> p k n", p=P)
            wao = flat("w_attn_out").rearrange("(k p) n -> p k n", p=P)
            wro = flat("w_rnn_out").rearrange("(k p) n -> p k n", p=P)
            wout = flat("w_out").rearrange("(k p) n -> p k n", p=P)
            w_up = a["w_up"].rearrange("l e d (h j n) -> (l e d) h j n", h=2, j=NG)
            w_down = a["w_down"].rearrange("l e d n -> (l e d) n")

            def used(c):
                if c < NPC:
                    sp.wait_ge(tile_done, max(n for n in range(NT1) if tiles[n][2] == c) + 1)
                elif c < CH_RO:
                    sp.wait_ge(out_done, 2 * (c - CH_AO) + 2)
                elif c < CH_OUT:
                    sp.wait_ge(out_done, 8 + c - CH_RO + 1)
                elif c < CH_LN:
                    sp.wait_ge(mix_done, c - CH_OUT + 1)
                elif c == CH_LN:
                    sp.wait_ge(x1_ready, 3)
                else:
                    sp.wait_ge(table_done, 1)

            for c, (kind, at0) in enumerate(chunks):
                if c >= RING:
                    used(c - RING)
                if kind == "win":
                    pieces = [(slot(c).rearrange("p (k n) -> p k n", k=KD), win[:, :, at0:at0 + 256])]
                elif kind in ("wa", "wx"):
                    pieces = [(slot(c)[:, 0:DR].rearrange("p (n d) -> p n d", n=RT),
                               flat("rg_" + kind).rearrange("n c d -> c n d"))]
                elif kind == "wao":
                    pieces = [(slot(c).rearrange("p (k n) -> p k n", k=KD), wao[:, :, at0:at0 + 256])]
                elif kind == "wro":
                    pieces = [(slot(c)[:, 0:DR].rearrange("p (k n) -> p k n", k=RT), wro[:, :, at0:at0 + P])]
                elif kind == "wout":
                    pieces = [(slot(c).rearrange("p (k n) -> p k n", k=2), wout[:, at0:at0 + 2, :])]
                elif kind == "ln1":
                    pieces = [(slot(c)[:, 0:D], a["ln1_g"].partition_broadcast(P)),
                              (slot(c)[:, D:2 * D], a["ln1_b"].partition_broadcast(P))]
                else:
                    pieces = [(slot(c)[0:NE, :], flat("b_up"))]
                for dst, src in pieces:
                    sp.dma_start(dst, src).then_inc(loaded[c % RING], 16)

            def moe_chunk(i, row0):
                c = NCH + i
                if i < UPC:
                    j, half = i // 2, i % 2
                    for h in range(2):
                        src = w_up[bass.ds(row0 + half * 512, 512), h, j, :].rearrange("(k p) n -> p k n", p=P)
                        dst = slot(c).rearrange("p (k h n) -> p k h n", k=4, h=2)[:, :, h, :]
                        sp.dma_start(dst, src).then_inc(loaded[c % RING], 16)
                    return
                src = w_down[bass.ds(row0 + (i - UPC) * 256, 256), :].rearrange("(k p) n -> p k n", p=P)
                dst = slot(c).rearrange("p (k n) -> p k n", k=2)
                sp.dma_start(dst, src).then_inc(loaded[c % RING], 16)

            for i in range(12):
                if i < RING:
                    used(NCH + i - RING)
                else:
                    low_ready(sp, i - RING, 0)
                moe_chunk(i, 0)
            sp.wait_ge(table_ready, 1)
            blocks = sp.value_load(tablei[0:1, NB:NB + 1], min_val=NE, max_val=NB)
            with sp.Fori(1, blocks) as b:
                e = sp.value_load(tablei[0:1, bass.ds(b, 1)], min_val=0, max_val=NE - 1)
                row0 = e * D
                before = b - 1
                for i in range(12):
                    if i < RING:
                        low_ready(sp, 12 + i - RING, before)
                    else:
                        low_ready(sp, i - RING, b)
                    moe_chunk(i, row0)
            sp.wait_ge(split_free, blocks * 12 + SPLITS)
            sp.dma_start(raw[:, 0, 0:D], a["ln2_g"].partition_broadcast(P)).then_inc(ln2_loaded, 16)
            sp.dma_start(raw[:, 0, D:2 * D], a["ln2_b"].partition_broadcast(P)).then_inc(ln2_loaded, 16)
            sp.dma_start(bdown, flat("b_down")).then_inc(ln2_loaded, 16)
            for t, (t0, n) in enumerate(TILES):
                sp.wait_ge(fin_ready, t + 1)
                dst = a["o_yp"][0, t0:t0 + n, :] if t < 2 else a["o_ys"][:, 0, :]
                sp.dma_start(dst, xtok[0:n, t, :]).then_inc(y_out, 16)
            sp.wait_ge(y_out, 48)

        @block.gpsimd
        def _(pool):
            pool.dma_start(a["o_ks"][0, :, 0:WIN - 1], a["cache_k"][0, :, 1:WIN]).then_inc(s_out, 16)
            pool.dma_start(a["o_vs"][0, :, 0:WIN - 1], a["cache_v"][0, :, 1:WIN]).then_inc(s_out, 16)
            pool.dma_start(a["o_cs"][0, :, 0:2], a["state_conv"][0, :, 1:3]).then_inc(s_out, 16)
            pool.wait_ge(kv_ready, 3)
            pool.wait_ge(s_cache, 32)
            pool.dma_start(kc[P - 1:P, :, :], kv8[:, 0:1, :]).then_inc(s_new, 16)
            pool.dma_start(vc[P - 1:P, :, :], kv8[:, 1:2, :]).then_inc(s_new, 16)
            kvo = lambda name: a[name][0, :, WIN - 1, :, :].rearrange("b g d -> b (g d)")
            pool.dma_start(kvo("o_ks"), kv8[:, 0, :]).then_inc(s_out, 16)
            pool.dma_start(kvo("o_vs"), kv8[:, 1, :]).then_inc(s_out, 16)
            pool.dma_start(a["o_kp"][0, 0].rearrange("s g d -> s (g d)"), ktok[:, :]).then_inc(s_out, 16)
            pool.dma_start(a["o_vp"][0, 0].rearrange("s g d -> s (g d)"), vtok[:, 1, :]).then_inc(s_out, 16)
            pool.wait_ge(rows_ready, 3)
            pool.dma_start(a["o_cp"][0, 0], rows[0:3, :]).then_inc(s_out, 16)
            pool.dma_start(a["o_hp"][0], rows[3:4, :]).then_inc(s_out, 16)
            pool.dma_start(a["o_cs"][0, :, 2, :], rows[4:12, :]).then_inc(s_out, 16)
            pool.dma_start(a["o_hs"][0], rows[12:20, :]).then_inc(s_out, 16)
            pool.wait_ge(s_out, 16 * N_OUT)
            pool.wait_ge(table_ready, 1)
            blocks = pool.value_load(tablei[0:1, NB:NB + 1], min_val=NE, max_val=NB)
            with pool.Fori(0, blocks) as b:
                for i in ON_POOL:
                    pool.wait_ge(hi_ready, b * 12 + (i + 1))
                    pool.tensor_tensor(lo[:, i % SPLITS, :], slot(NCH + i), hi[:, i % SPLITS, :].bitcast(F32),
                                       ALU.subtract).then_inc(lo_pool_ready, 1)

        @block.scalar
        def _(act):
            act.dma_start(const[:, :], a["consts"]).then_inc(s_const, 16)
            for t in range(2):
                act.dma_start(xtok[:, t, :], a["x_prompt"][0, t * P:(t + 1) * P, :]).then_inc(s_x, 16)
            act.dma_start(xtok[0:DECB, 2, :], a["x_sample"][:, 0, :]).then_inc(s_x, 16)
            r0 = 0
            for name in ("conv_w", "conv_b", "rg_ba", "rg_bx", "rg_lambda"):
                src = a[name][0].rearrange("j (t p) -> (j t) p", p=P) if name == "conv_w" \
                    else a[name][0].rearrange("(t p) -> t p", p=P)
                n = 40 if name == "conv_w" else RT
                act.dma_start(parr[r0:r0 + n, :], src).then_inc(s_par, 16)
                r0 += n
            act.dma_start(statr[0:24, :], a["state_conv"][0].rearrange("b j c -> (b j) c")).then_inc(s_par, 16)
            act.dma_start(statr[24:32, :], a["state_h"][0]).then_inc(s_par, 16)
            act.dma_start(sink[:, :], a["attn_sinks"].partition_broadcast(P)).then_inc(s_misc, 16)
            act.dma_start(sinkc[:, :], a["attn_sinks"].rearrange("l h -> h l")).then_inc(s_misc, 16)
            act.dma_start(kc[0:P - 1, :, :], a["cache_k"][0, :, 1:WIN].rearrange("b w g d -> w b (g d)"))\
                .then_inc(s_cache, 16)
            act.dma_start(vc[0:P - 1, :, :], a["cache_v"][0, :, 1:WIN].rearrange("b w g d -> w b (g d)"))\
                .then_inc(s_cache, 16)
            act.dma_start(wr[:, :, :], flat("w_router").rearrange("(k p) e -> p k e", p=P)).then_inc(s_bd, 16)
            act.dma_start(brb[:, :], a["b_router"].partition_broadcast(P)).then_inc(s_bd, 16)

            def turned_x(ready, done):
                for g in range(5):
                    act.wait_ge(ready, g + 1)
                    if g < 4:
                        t, d0 = g // 2, 4 * (g % 2)
                        act.activation(xT[:, d0:d0 + 4, t * P:(t + 1) * P],
                                       bank[g][:, :].rearrange("p (d n) -> p d n", d=4), ACT.Copy).then_inc(done, 1)
                    else:
                        act.activation(xT[:, :, SEQ:T], bank[4][:, 0:64].rearrange("p (d n) -> p d n", d=KD),
                                       ACT.Copy).then_inc(done, 1)

            turned_x(x_turned, xT_ready)
            act.wait_ge(lam_in, 1)
            act.activation(lamt[:, 2, :], lamt[:, 1, :], ACT.Exp, scale=-1.0).then_inc(lam_exp, 1)

            def exps(h):
                act.wait_ge(max_ready, h + 1)
                for blk in range(2):
                    last = act.activation(lg[:, h % 2, blk, :], lg[:, h % 2, blk, :], ACT.Exp,
                                          bias=negm[:, blk, h:h + 1], accum_out=rsum[:, blk, h:h + 1])
                last.then_inc(probs_ready, 1)

            for what, n in order:
                if what == "tile":
                    name, idx, _, _ = tiles[n]
                    ps = bank[n % 4][:, 0:T]
                    act.wait_ge(tile_done, n + 1)
                    if name == "kv":
                        ins = act.activation((kT if idx == 0 else vT)[:, :], ps, ACT.Copy)
                    elif name == "q":
                        ins = act.activation(qT[:, idx, :], ps, ACT.Copy, scale=HD ** -0.5)
                    elif name == "xr":
                        act.activation(xrp[:, idx, 3:3 + SEQ], ps[:, 0:SEQ], ACT.Copy)
                        ins = act.activation(xrs[:, idx, :], ps[:, SEQ:T], ACT.Copy)
                    elif name in ("r", "i"):
                        if name == "r" and idx == 0:
                            act.wait_ge(par_ready, 2)
                        col = (50 if name == "r" else 60) + idx
                        ins = act.activation((rg if name == "r" else ig)[:, idx, :], ps, ACT.Identity,
                                             bias=par[:, col:col + 1])
                    else:
                        ins = act.activation({"yr": yr, "ga": ga, "gb": gb}[name][:, idx, :], ps, ACT.Copy)
                    ins.then_inc(tile_evac, 1)
                elif what == "kvturn":
                    act.wait_ge(kv_turned, 1)
                    act.activation(vtok[:, :, :], bank[6][:, 0:256].rearrange("p (b n) -> p b n", b=2), ACT.Copy)\
                        .then_inc(kv_ready, 1)
                    act.activation(ktok[:, :], bank[6][:, 256:384], ACT.Copy).then_inc(kv_ready, 1)
                    act.activation(kv8[:, :, :], bank[7][0:DECB, 0:256].rearrange("p (b n) -> p b n", b=2), ACT.Copy)\
                        .then_inc(kv_ready, 1)
                elif what == "step":
                    h = n - 1
                    if 0 <= h < NH:
                        if h >= 2:
                            act.wait_ge(pv_done, h - 1)
                        act.wait_ge(probs_turned, h + 1)
                        act.activation(pT[:, h % 2, :], bank[6][:, 0:384], ACT.Copy).then_inc(pT_ready, 1)
                    h = n - 2
                    if 0 <= h < NH:
                        act.wait_ge(pv_done, h + 1)
                        act.activation(otok[:, :, h * HD:(h + 1) * HD],
                                       bank[7][:, (h % 4) * P:(h % 4 + 1) * P].rearrange("p (b n) -> p b n", b=2),
                                       ACT.Copy).then_inc(o_ready, 1)
                    if n < NH:
                        exps(n)
                    if n == NH + 1:
                        act.wait_ge(den_in, 1)
                        act.activation(esk[:, :, :], esk[:, :, :], ACT.Exp).then_inc(sinkexp, 1)
                else:
                    if n == 0:
                        for j in range(2):
                            act.wait_ge(s_kt, j + 1)
                            act.activation(kcT[:, 4 * j:4 * j + 4, :],
                                           bank[4 + j][:, :].rearrange("p (b n) -> p b n", b=4), ACT.Copy)\
                                .then_inc(s_kte, 1)
                    elif n == 1:
                        act.wait_ge(s_sm, 1)
                        act.activation(slog, slog, ACT.Exp).then_inc(s_ex, 1)
                        act.activation(srow[:, 1, :], srow[:, 1, :], ACT.Exp).then_inc(s_ex, 1)
                    elif n == 2:
                        act.wait_ge(s_ptt, 1)
                        act.activation(pTs, bank[4][:, 0:P].rearrange("p (b h) -> p b h", b=DECB), ACT.Copy)\
                            .then_inc(s_pte, 1)

            for g in range(4):
                act.wait_ge(o_turned, g + 1)
                if g == 0:
                    act.wait_ge(s_qz, 1)
                blk, d0 = g // 2, 4 * (g % 2)
                act.activation(oT[:, d0:d0 + 4, blk * P:(blk + 1) * P],
                               bank[4 + g][:, :].rearrange("p (d n) -> p d n", d=4), ACT.Copy).then_inc(oT_ready, 1)

            act.wait_ge(tile_evac, NT1)
            act.activation(rg[:, :, :], rg[:, :, :], ACT.Sigmoid).then_inc(gates_done, 1)
            act.wait_ge(gates_done, 1)
            act.wait_ge(lam_ready, 1)
            act.wait_ge(s_os, 1)
            for n in range(RT):
                act.activation(sg[:, n, :], rg[:, n, :], ACT.Tanh, scale=lamt[:, 7, n:n + 1]).then_inc(tanh_done, 1)
            act.activation(ig[:, :, :], ig[:, :, :], ACT.Sigmoid).then_inc(gates_done, 1)
            act.activation(ga[:, :, :], ga[:, :, :], ACT.Sigmoid).then_inc(gates_done, 1)
            act.activation(gb[:, :, :], gb[:, :, :], ACT.Sigmoid).then_inc(gates_done, 1)
            act.wait_ge(tanh_done, RT)
            for n in range(RT):
                act.activation(rg[:, n, :], rg[:, n, :], ACT.Exp, scale=lamt[:, 6, n:n + 1]).then_inc(decay_done, 1)
            act.activation(yr[:, :, :], yr[:, :, :], ACT.Gelu_apprx_tanh).then_inc(gelu_done, 1)
            act.wait_ge(ratio_ready, 1)
            act.activation(sg[:, :, :], sg[:, :, :], ACT.Sqrt, scale=2.0).then_inc(root_done, 1)

            for g, (c0, w) in enumerate(((0, 512), (512, 512), (1024, 256))):
                act.wait_ge(pack_turned, g + 1)
                act.activation(rows[:, c0:c0 + w], bank[5 + g][0:20, 0:w], ACT.Copy).then_inc(rows_ready, 1)

            def roots(ready, done):
                for t, (_, n) in enumerate(TILES):
                    act.wait_ge(ready, t + 1)
                    act.activation(sd[0:n, t:t + 1], mv[0:n, t, 1:2], ACT.Sqrt, bias=epsc[0:n, :]).then_inc(done, 1)

            roots(var_ready, sd_ready)
            turned_x(x1_turned, x1T_ready)
            for t, (_, n) in enumerate(TILES):
                act.wait_ge(top_ready, t + 1)
                act.activation(rt[0:n, 5, t, :], lgt[0:n, t, :], ACT.Exp, bias=rsm[0:n, 0, t:t + 1])\
                    .then_inc(exp_ready, 1)

            act.wait_ge(table_ready, 1)
            blocks = act.value_load(tablei[0:1, NB:NB + 1], min_val=NE, max_val=NB)

            for t, (_, n) in enumerate(TILES):
                act.activation(xh[0:n, t, :], xtok[0:n, t, :], ACT.Copy).then_inc(xh_ready, 1)

            def take_gather(count):
                act.wait_ge(gathered, count)
                for h in range(2):
                    ins = act.activation(gx[:, h * 512:(h + 1) * 512], bank[6 + h][:, :], ACT.Copy)
                ins.then_inc(gx_ready, 1)

            def take_turned(count):
                act.wait_ge(gx_turned, count)
                for h in range(2):
                    ins = act.activation(xg[:, 4 * h:4 * h + 4, :],
                                         bank[6 + h][:, :].rearrange("p (d n) -> p d n", d=4), ACT.Copy)
                ins.then_inc(xg_ready, 1)

            def take_gt(count):
                act.wait_ge(gated_turned, count)
                act.activation(gt[:, :], bank[7][:, 0:T], ACT.Copy).then_inc(gt_ready, 1)

            def take_y(before):
                act.wait_ge(split_free, before * 12 + SPLITS)
                for j in range(2):
                    act.activation(ysb[:, j * 512:(j + 1) * 512], bank[4 + j][:, :], ACT.Copy).then_inc(y_ready, 1)

            take_gather(1)
            take_turned(1)
            with act.Fori(0, blocks) as b:
                def split(i):
                    c = NCH + i
                    act.wait_ge(split_free, b * 12 + (i + 1))
                    act.wait_ge(loaded[c % RING], b * PER_BLOCK[i] + LOADED0[i])
                    act.activation(hi[:, i % SPLITS, :], slot(c), ACT.Copy).then_inc(hi_ready, 1)

                def take_up(j):
                    act.wait_ge(split_free, b * 12 + (SPLITS + 2 * j + 2))
                    if j >= 2:
                        act.wait_ge(hT_done, b * NG + (j - 1))
                    act.activation(hsb[:, j % 2, :], bank[j % 2][:, :], ACT.Copy).then_inc(up_taken, 1)

                def sigmoid(j):
                    act.wait_ge(glu_ready, b * NG + (j + 1))
                    act.activation(sig[:, j % 2, :, :], glin[:, j % 2, 0:2, :], ACT.Sigmoid, scale=SALPHA)\
                        .then_inc(sig_ready, 1)

                act.activation(warm[:, :], warm[:, :], ACT.Sigmoid)
                split(0)
                split(1)
                split(2)
                take_y(b)
                split(3)
                split(4)
                take_up(0)
                split(5)
                take_gt(b + 2)
                split(6)
                take_up(1)
                split(7)
                sigmoid(0)
                split(8)
                take_up(2)
                split(9)
                sigmoid(1)
                split(10)
                sigmoid(2)
                take_up(3)
                split(11)
                take_gather(b + 2)
                sigmoid(3)
                take_turned(b + 2)
            take_y(blocks)
            take_gt(blocks + 2)
            roots(var2_ready, sd2_ready)

        @block.tensor
        def _(pe):
            pe.wait_ge(s_const, 16)
            pe.wait_ge(s_x, 48)

            def turn_x(done, first_wait=None):
                for g in range(4):
                    t, d0 = g // 2, 4 * (g % 2)
                    for j in range(4):
                        last = pe.transpose(bank[g][:, j * P:(j + 1) * P], xtok[:, t, (d0 + j) * P:(d0 + j + 1) * P],
                                            ident)
                    last.then_inc(done, 1)
                for d in range(KD):
                    last = pe.transpose(bank[4][:, d * 8:d * 8 + 8], xtok[0:DECB, 2, d * P:(d + 1) * P],
                                        ident[0:DECB, 0:DECB])
                last.then_inc(done, 1)

            turn_x(x_turned)
            pe.wait_ge(s_par, 16 * 7)
            pe.transpose(bank[5][:, 0:80], parr[:, :], ident[0:80, 0:80]).then_inc(par_turned, 1)
            for n in range(RT):
                last = pe.transpose(bank[6][:, n * 32:(n + 1) * 32], statr[:, n * P:(n + 1) * P], ident[0:32, 0:32])
            last.then_inc(par_turned, 1)
            pe.wait_ge(xT_ready, 5)

            def scores(h):
                g, par_ = h // GROUP, h % 2
                if h == 0:
                    pe.wait_ge(kz_ready, 1)
                    pe.wait_ge(tile_evac, 10)
                if h >= 2:
                    pe.wait_ge(scores_taken, h - 1)
                for blk in range(2):
                    last = pe.matmul(bank[4 + h % 2][:, blk * 256:(blk + 1) * 256],
                                     qT[:, h // 2, blk * P:(blk + 1) * P],
                                     kz[:, 2 * g + par_, blk * P:blk * P + 256], start=True, stop=True)
                last.then_inc(scored, 1)

            def turn_probs(h):
                pe.wait_ge(probs_ready, h + 1)
                if h >= 1:
                    pe.wait_ge(pT_ready, h)
                for j, (blk, part) in enumerate(((0, 1), (1, 0), (1, 1))):
                    last = pe.transpose(bank[6][:, j * P:(j + 1) * P], lg[:, h % 2, blk, part * P:(part + 1) * P],
                                        ident)
                last.then_inc(probs_turned, 1)

            def weigh(h):
                g = h // GROUP
                pe.wait_ge(pT_ready, h + 1)
                if h >= 1:
                    pe.wait_ge(o_ready, h)
                o = bank[7][:, (h % 4) * P:(h % 4 + 1) * P]
                vv = lambda blk: vtok[:, blk, g * HD:(g + 1) * HD]
                pe.matmul(o[:, 0:HD], pT[:, h % 2, 0:P], vv(0), start=True, stop=True)
                pe.matmul(o[:, HD:P], pT[:, h % 2, P:2 * P], vv(0), start=True, stop=False)
                pe.matmul(o[:, HD:P], pT[:, h % 2, 2 * P:3 * P], vv(1), start=False, stop=True).then_inc(pv_done, 1)

            seen = set()
            for what, n in order:
                if what == "tile":
                    name, idx, c, half = tiles[n]
                    if c not in seen:
                        chunk_ready(pe, c)
                        seen.add(c)
                    if n >= 4:
                        pe.wait_ge(tile_evac, n - 3)
                    if name in ("r", "i"):
                        pe.wait_ge(conv_ready, idx + 1 if name == "r" else RT)
                        last = pe.matmul(bank[n % 4][:, 0:T], slot(c)[:, idx * P:(idx + 1) * P], xc[:, idx, :],
                                         start=True, stop=True)
                    else:
                        w = slot(c).rearrange("p (k n) -> p k n", k=KD)
                        for k in range(KD):
                            last = pe.matmul(bank[n % 4][:, 0:T], w[:, k, half * P:(half + 1) * P], xT[:, k, :],
                                             start=k == 0, stop=k == KD - 1)
                    last.then_inc(tile_done, 1)
                elif what == "kvturn":
                    pe.wait_ge(tile_evac, 2)
                    pe.wait_ge(par_ready, 2)
                    for blk in range(2):
                        pe.transpose(bank[6][:, blk * P:(blk + 1) * P], vT[:, blk * P:(blk + 1) * P], ident)
                    pe.transpose(bank[6][:, 256:384], kT[:, P:2 * P], ident)
                    pe.transpose(bank[7][0:DECB, 0:P], kT[:, SEQ:T], ident)
                    pe.transpose(bank[7][0:DECB, P:2 * P], vT[:, SEQ:T], ident).then_inc(kv_turned, 1)
                elif what == "step":
                    if n == 0:
                        pe.wait_ge(kv_ready, 3)
                    if n < NH:
                        scores(n)
                    if 0 <= n - 1 < NH:
                        turn_probs(n - 1)
                    if 0 <= n - 2 < NH:
                        weigh(n - 2)
                else:
                    if n == 0:
                        pe.wait_ge(s_new, 32)
                        pe.wait_ge(scores_taken, NH)
                        for j in range(2):
                            for b in range(4):
                                last = pe.transpose(bank[4 + j][:, b * P:(b + 1) * P], kc[:, 4 * j + b, :], ident)
                            last.then_inc(s_kt, 1)
                    elif n == 1:
                        pe.wait_ge(s_kte, 2)
                        pe.wait_ge(s_qz, 1)
                        pe.wait_ge(o_ready, NH)
                        for b in range(DECB):
                            last = pe.matmul(bank[6 + b // 4][0:NH, (b % 4) * P:(b % 4 + 1) * P], qz[:, b, :],
                                             kcT[:, b, :], start=True, stop=True)
                        last.then_inc(s_sc, 1)
                    elif n == 2:
                        pe.wait_ge(s_pn, 1)
                        for b in range(DECB):
                            last = pe.transpose(bank[4][:, b * NH:(b + 1) * NH], slog[:, b, :], ident[0:NH, 0:NH])
                        last.then_inc(s_ptt, 1)
                    else:
                        pe.wait_ge(s_pte, 1)
                        for b in range(DECB):
                            last = pe.matmul(bank[5][:, b * NH:(b + 1) * NH], vc[:, b, :], pTs[:, b, :],
                                             start=True, stop=True)
                        last.then_inc(s_pv, 1)

            pe.wait_ge(o_norm, 2)
            pe.wait_ge(s_os, 1)
            for g in range(4):
                blk, d0 = g // 2, 4 * (g % 2)
                for j in range(4):
                    last = pe.transpose(bank[4 + g][:, j * P:(j + 1) * P], otok[:, blk, (d0 + j) * P:(d0 + j + 1) * P],
                                        ident)
                last.then_inc(o_turned, 1)

            pe.wait_ge(oT_ready, 4)
            for m in range(16):
                if m < 4:
                    pe.wait_ge(tile_evac, NT1)
                else:
                    pe.wait_ge(out_evac, m - 3)
                if m < 8:
                    c, half = CH_AO + m // 2, m % 2
                    w, src, kk = slot(c).rearrange("p (k n) -> p k n", k=KD), oT, KD
                else:
                    c, half = CH_RO + m - 8, 0
                    w, src, kk = slot(c)[:, 0:DR].rearrange("p (k n) -> p k n", k=RT), yr, RT
                    pe.wait_ge(y_rnn_ready, 1)
                chunk_ready(pe, c)
                for k in range(kk):
                    last = pe.matmul(bank[m % 4][:, 0:T], w[:, k, half * P:(half + 1) * P], src[:, k, :],
                                     start=k == 0, stop=k == kk - 1)
                last.then_inc(out_done, 1)
            pe.wait_ge(pack_ready, 1)
            pe.wait_ge(oT_ready, 4)
            for g, (n0, n1) in enumerate(((0, 4), (4, 8), (8, 10))):
                for n in range(n0, n1):
                    last = pe.transpose(bank[5 + g][0:20, (n - n0) * P:(n - n0 + 1) * P], pack[:, n, :], ident)
                last.then_inc(pack_turned, 1)
            mix = [(bank[4], bank[5]), (bank[6], bank[7]), (bank[0], bank[1])]
            pe.wait_ge(merged_ready, 8)
            pe.wait_ge(rows_ready, 3)
            for cc in range(4):
                chunk_ready(pe, CH_OUT + cc)
                w = slot(CH_OUT + cc).rearrange("p (k n) -> p k n", k=2)
                for kk in range(2):
                    k = 2 * cc + kk
                    for t, (t0, n) in enumerate(TILES):
                        for h in range(2):
                            last = pe.matmul(mix[t][h][0:n, :], ga[:, k, t0:t0 + n], w[:, kk, h * 512:(h + 1) * 512],
                                             start=k == 0, stop=k == KD - 1)
                last.then_inc(mix_done, 1)

            pe.wait_ge(x1_ready, 3)
            turn_x(x1_turned)
            pe.wait_ge(x1T_ready, 5)
            pe.wait_ge(s_bd, 32)
            for t, (t0, n) in enumerate(TILES):
                for k in range(KD):
                    last = pe.matmul(bank[5][0:n, t * NE:(t + 1) * NE], xT[:, k, t0:t0 + n], wr[:, k, :],
                                     start=k == 0, stop=k == KD - 1)
            last.then_inc(logits_done, 1)
            pe.wait_ge(mask_ready, 3)
            mask = lambda t, n: rt[0:n, 4, t, :]
            for t, (t0, n) in enumerate(TILES):
                for u in range(t):
                    pe.matmul(bank[6][0:n, t * NE:(t + 1) * NE], ones[:, 0:n], mask(u, P), start=u == 0, stop=False)
                pe.matmul(bank[6][0:n, t * NE:(t + 1) * NE], const[0:n, C_TRI:C_TRI + n], mask(t, n),
                          start=t == 0, stop=True)
            for t, (t0, n) in enumerate(TILES):
                last = pe.matmul(bank[7][0:NE, 0:1], mask(t, n), ones[0:n, 0:1], start=t == 0, stop=t == 2)
            last.then_inc(count_done, 1)
            pe.wait_ge(over_ready, 1)
            pe.matmul(bank[7][0:NE, 8:9], const[0:NE, C_TRI:C_TRI + NE], ov[:, 1:2], start=True, stop=True)
            pe.matmul(bank[7][0:1, 16:17], ov[:, 1:2], ones[0:NE, 0:1], start=True, stop=True).then_inc(start_done, 1)
            pe.wait_ge(route_ready, 3)
            for t, (t0, n) in enumerate(TILES):
                pe.transpose(bank[0][0:NE, t0:t0 + n], rt[0:n, 6, t, :], ident[0:n, 0:n])
                last = pe.transpose(bank[1][0:NE, t0:t0 + n], rt[0:n, 7, t, :], ident[0:n, 0:n])
            last.then_inc(route_turned, 1)
            pe.wait_ge(routeT_ready, 1)
            for t, (t0, n) in enumerate(TILES):
                pe.matmul(bank[2][0:n, t * NB:(t + 1) * NB], posmT[:, t0:t0 + n], selm[:, :], start=True, stop=False)
                pe.matmul(bank[2][0:n, t * NB:(t + 1) * NB], ones[0:NE, 0:n], negj[:, :], start=False, stop=True)
                pe.matmul(bank[3][0:n, t * NB:(t + 1) * NB], gateT[:, t0:t0 + n], selm[:, :], start=True, stop=True)
            pe.matmul(bank[7][0:1, 32:32 + NB], const[0:NE, C_EIDX:C_EIDX + 1], selm[:, :], start=True, stop=True)
            chunk_ready(pe, CH_BUP)
            for f in range(FT):
                bk, o = (5, f * NB) if f < 8 else (6, (f - 8) * NB)
                last = pe.matmul(bank[bk][:, o:o + NB], slot(CH_BUP)[0:NE, f * P:(f + 1) * P], selm[:, :],
                                 start=True, stop=True)
            last.then_inc(table_done, 1)

            pe.wait_ge(table_ready, 1)
            blocks = pe.value_load(tablei[0:1, NB:NB + 1], min_val=NE, max_val=NB)

            def gather(h):
                for part, x in ((0, xh), (1, xl)):
                    for t, (_, n) in enumerate(TILES):
                        last = pe.matmul(bank[6 + h][:, :],
                                         onehot[0:n, t, (1 - part) * CAP:(1 - part) * CAP + P],
                                         x[0:n, t, h * 512:(h + 1) * 512],
                                         start=part == 0 and t == 0, stop=part == 1 and t == 2)
                if h == 1:
                    last.then_inc(gathered, 1)

            def turn_gathered(count):
                pe.wait_ge(gx_ready, count)
                for d in range(KD):
                    last = pe.transpose(bank[6 + d // 4][:, (d % 4) * P:(d % 4 + 1) * P], gx[:, d * P:(d + 1) * P],
                                        ident)
                last.then_inc(gx_turned, 1)

            def turn_gates():
                for t, (t0, n) in enumerate(TILES):
                    last = pe.transpose(bank[7][:, t0:t0 + n], gated[0:n, t, :], ident[0:n, 0:n])
                last.then_inc(gated_turned, 1)

            def combine(tiles_, added_before):
                for d in tiles_:
                    if d >= 2:
                        pe.wait_ge(added, added_before + (d - 1))
                    pe.matmul(bank[CBANK[d % 2]][:, 0:T], ysb[:, d * P:(d + 1) * P], gt[:, :], start=True, stop=True)\
                        .then_inc(combined, 1)

            pe.wait_ge(onehot_ready, 1)
            pe.wait_ge(xh_ready, 3)
            pe.wait_ge(xl_ready, 3)
            gather(0)
            gather(1)
            turn_gathered(1)
            pe.sem_inc(split_free, SPLITS)
            pe.sem_inc(gated_turned, 1)
            pe.wait_ge(y_cleared, 1)
            with pe.Fori(0, blocks) as b:
                def up(i):
                    j, half = i // 2, i % 2
                    if j >= 2 and half == 0:
                        pe.wait_ge(up_taken, b * NG + (j - 1))
                    h_ = hi[:, i % SPLITS, :].rearrange("p (k n) -> p k n", k=4)
                    l_ = lo[:, i % SPLITS, :].rearrange("p (k n) -> p k n", k=4)
                    pe.wait_ge(hi_ready, b * 12 + (i + 1))
                    for k in range(4):
                        pe.matmul(bank[j % 2][:, :], xg[:, 4 * half + k, :], h_[:, k, :],
                                  start=half == 0 and k == 0, stop=False)
                    low_ready(pe, i, b)
                    for k in range(4):
                        last = pe.matmul(bank[j % 2][:, :], xg[:, 4 * half + k, :], l_[:, k, :],
                                         start=False, stop=half == 1 and k == 3)
                    last.then_inc(split_free, 1)

                def down(i):
                    pe.wait_ge(at_ready, b * NG + (i - UPC + 1))
                    for part, src in ((0, hi), (1, lo)):
                        if part == 0:
                            pe.wait_ge(hi_ready, b * 12 + (i + 1))
                        else:
                            low_ready(pe, i, b)
                        for kk in range(2):
                            k = 2 * (i - UPC) + kk
                            for n in range(2):
                                last = pe.matmul(bank[4 + n][:, :], at[:, k, :],
                                                 src[:, i % SPLITS, kk * D + n * 512:kk * D + (n + 1) * 512],
                                                 start=part == 0 and k == 0, stop=part == 1 and k == KD - 1)
                    last.then_inc(split_free, 1)

                def turn_up(j):
                    pe.wait_ge(up_taken, b * NG + (j + 1))
                    pe.wait_ge(hT_taken, b * NG + (j + 1))
                    for f in range(4):
                        last = pe.transpose(bank[2 + j % 2][:, f * P:(f + 1) * P], hsb[:, j % 2, f * P:(f + 1) * P],
                                            ident)
                    last.then_inc(hT_done, 1)

                pe.wait_ge(xg_ready, b + 1)
                up(0)
                up(1)
                pe.wait_ge(gated_ready, b + 1)
                turn_gates()
                up(2)
                turn_up(0)
                pe.wait_ge(gt_ready, b + 1)
                pe.wait_ge(y_ready, b * 2 + 2)
                combine((0, 1), b * 8)
                up(3)
                combine((2,), b * 8)
                up(4)
                turn_up(1)
                combine((3, 4), b * 8)
                up(5)
                combine((5, 6), b * 8)
                up(6)
                turn_up(2)
                combine((7,), b * 8)
                pe.wait_ge(onehot_ready, b + 2)
                pe.wait_ge(added, b * 8 + 7)
                gather(0)
                up(7)
                pe.wait_ge(added, b * 8 + 8)
                gather(1)
                turn_up(3)
                down(8)
                turn_gathered(b + 2)
                down(9)
                down(10)
                down(11)

            pe.wait_ge(gated_ready, blocks + 1)
            pe.wait_ge(xg_ready, blocks + 1)
            turn_gates()
            pe.wait_ge(gt_ready, blocks + 1)
            pe.wait_ge(y_ready, blocks * 2 + 2)
            combine(range(KD), blocks * 8)
            pe.wait_ge(ln2_loaded, 48)
            pe.wait_ge(added, blocks * 8 + 8)
            for t, (t0, n) in enumerate(TILES):
                for h in range(2):
                    o = bank[2 * t + h][0:n, :]
                    pe.matmul(o, gateT[:, t0:t0 + n], bdown[:, h * 512:(h + 1) * 512], start=True, stop=False)
                    for j in range(4):
                        last = pe.matmul(o[:, j * P:(j + 1) * P], yT[:, 4 * h + j, t0:t0 + n], ident,
                                         start=False, stop=j == 3)
                last.then_inc(final_done, 1)

        @block.vector
        def _(dve):
            steps = [0]

            def link(ins):
                steps[0] += 1
                ins.then_inc(v, 1)
                dve.wait_ge(v, steps[0])

            link(dve.memset(warm[:, :], 0.0))
            link(dve.memset(epsc[:, :], EPS))
            link(dve.memset(kz[:, :, :], 0.0))
            link(dve.memset(xrp[:, :, 0:3], 0.0))
            link(dve.memset(posb[:, :, :], -1.0))
            link(dve.memset(gateb[:, :, :], 0.0))
            dve.memset(ones[:, :], 1.0).then_inc(ones_ready, 1)
            dve.wait_ge(par_turned, 2)
            dve.tensor_copy(par[:, :], bank[5][:, 0:80]).then_inc(par_ready, 1)
            dve.tensor_copy(stat[:, :, :], bank[6][:, 0:320].rearrange("p (n c) -> p n c", n=RT)).then_inc(par_ready, 1)
            dve.wait_ge(par_ready, 2)
            lam = par[:, 70:80]
            L = lambda i: lamt[:, i, :]
            link(dve.tensor_scalar(L(0), lam, -1.0, None, ALU.mult))
            dve.tensor_tensor(L(1), lam, L(0), ALU.max).then_inc(lam_in, 1)
            dve.wait_ge(lam_exp, 1)
            link(dve.tensor_scalar(L(3), L(2), 2.0, None, ALU.add))
            link(dve.reciprocal(L(3), L(3)))
            link(dve.tensor_tensor(L(3), L(2), L(3), ALU.mult))
            link(dve.tensor_tensor(L(4), L(3), L(3), ALU.mult))
            link(dve.memset(L(5), 1.0 / 19.0))
            for k in range(17, 0, -2):
                link(dve.tensor_tensor(L(5), L(5), L(4), ALU.mult))
                link(dve.tensor_scalar(L(5), L(5), 1.0 / k, None, ALU.add))
            link(dve.tensor_tensor(L(5), L(5), L(3), ALU.mult))
            link(dve.tensor_scalar(L(0), L(0), 0.0, None, ALU.max))
            link(dve.scalar_tensor_tensor(out=L(5), in0=L(5), scalar=2.0, in1=L(0), op0=ALU.mult, op1=ALU.add))
            link(dve.tensor_scalar(L(6), L(5), -8.0, None, ALU.mult))
            dve.tensor_scalar(L(7), L(5), 8.0, None, ALU.mult).then_inc(lam_ready, 1)

            dve.wait_ge(tile_evac, 2)
            for g in range(2):
                for q in range(2):
                    last = dve.tensor_copy(kz[q * 64:q * 64 + 64, 2 * g + q, P:P + SEQ], kT[g * 64:g * 64 + 64, 0:SEQ])
            last.then_inc(kz_ready, 1)
            dve.wait_ge(s_misc, 32)

            def softmax_head(h):
                dve.wait_ge(scored, h + 1)
                if h >= 2:
                    dve.wait_ge(probs_turned, h - 1)
                link(dve.scalar_tensor_tensor(out=lg[:, h % 2, :, :].rearrange("p b n -> p (b n)"),
                                              in0=const[:, C_DIST:C_DIST + 512], scalar=-slope(h),
                                              in1=bank[4 + h % 2][:, :], op0=ALU.mult, op1=ALU.add)
                     )
                dve.tensor_reduce(rmax[:, h % 2, :], lg[:, h % 2, :, :], AX.X, ALU.max).then_inc(scores_taken, 1)
                dve.wait_ge(scores_taken, h + 1)
                dve.tensor_scalar(negm[:, :, h], rmax[:, h % 2, :], sink[:, h:h + 1], -1.0, ALU.max, ALU.mult)\
                    .then_inc(max_ready, 1)

            def conv(n):
                xr_tile = 10 + n
                dve.wait_ge(tile_evac, xr_tile + 1)
                w = lambda j: par[:, j * RT + n:j * RT + n + 1]
                cb = par[:, 40 + n:41 + n]
                o, os_ = xc[:, n, 0:SEQ], xc[:, n, SEQ:T]
                dve.tensor_scalar(o, xrp[:, n, 0:SEQ], w(0), cb, ALU.mult, ALU.add)
                link(dve.tensor_scalar(os_, stat[:, n, 0:24:3], w(0), cb, ALU.mult, ALU.add))
                for j in range(1, CONV):
                    dve.scalar_tensor_tensor(out=o, in0=xrp[:, n, j:j + SEQ], scalar=w(j), in1=o,
                                             op0=ALU.mult, op1=ALU.add)
                    src = stat[:, n, j:24:3] if j < 3 else xrs[:, n, :]
                    ins = dve.scalar_tensor_tensor(out=os_, in0=src, scalar=w(j), in1=os_, op0=ALU.mult, op1=ALU.add)
                    if j < CONV - 1:
                        link(ins)
                    else:
                        ins.then_inc(conv_ready, 1)

            for what, n in order:
                if what == "step" and n < NH:
                    softmax_head(n)
                    if n < RT:
                        conv(n)
                elif what == "sample" and n == 0:
                    link(dve.memset(qz, 0.0))
                    for g in range(2):
                        for q in range(2):
                            src = qT[q * 64:q * 64 + 64, 4 * g:4 * g + 4, SEQ:T].rearrange("p f b -> p b f")
                            last = dve.tensor_copy(qz[g * 64:g * 64 + 64, :, 8 * g + q:8 * g + 8:2], src)
                    last.then_inc(s_qz, 1)
                elif what == "sample" and n == 1:
                    dve.wait_ge(s_sc, 1)
                    dist = const[0:NH, C_TDIST:C_TDIST + P].unsqueeze(1).broadcast_to([NH, 4, P])
                    for j in range(2):
                        ins = dve.scalar_tensor_tensor(out=slog[:, 4 * j:4 * j + 4, :], in0=dist,
                                                       scalar=const[0:NH, C_SLOPE:C_SLOPE + 1],
                                                       in1=bank[6 + j][0:NH, :].rearrange("p (b n) -> p b n", b=4),
                                                       op0=ALU.mult, op1=ALU.add)
                    link(ins)
                    link(dve.tensor_reduce(srow[:, 0, :], slog, AX.X, ALU.max))
                    link(dve.tensor_scalar(srow[:, 0, :], srow[:, 0, :], sinkc[:, 0:1], None, ALU.max))
                    dve.tensor_scalar(srow[:, 1, :], srow[:, 0, :], -1.0, sinkc[:, 0:1], ALU.mult, ALU.add)
                    dve.tensor_tensor(slog, slog, srow[:, 0, :].unsqueeze(2).broadcast_to([NH, DECB, P]),
                                      ALU.subtract).then_inc(s_sm, 1)
                    dve.wait_ge(s_ex, 2)
                    link(dve.tensor_reduce(srow[:, 2, :], slog, AX.X, ALU.add))
                    link(dve.tensor_tensor(srow[:, 2, :], srow[:, 2, :], srow[:, 1, :], ALU.add))
                    link(dve.reciprocal(srow[:, 3, :], srow[:, 2, :]))
                    dve.tensor_tensor(slog, slog, srow[:, 3, :].unsqueeze(2).broadcast_to([NH, DECB, P]),
                                      ALU.mult).then_inc(s_pn, 1)
                elif what == "sample" and n == 3:
                    dve.wait_ge(s_pv, 1)
                    ps = bank[5][:, 0:P].rearrange("p (b h) -> p b h", b=DECB)
                    for g in range(2):
                        for q in range(2):
                            dst = oT[q * 64:q * 64 + 64, 4 * g:4 * g + 4, SEQ:T].rearrange("p f b -> p b f")
                            last = dve.tensor_copy(dst, ps[g * 64:g * 64 + 64, :, 8 * g + q:8 * g + 8:2])
                    last.then_inc(s_os, 1)
                if what == "step" and n == NH + 1:
                    dve.wait_ge(probs_ready, NH)
                    dve.wait_ge(max_ready, NH)
                    dve.tensor_tensor(esk[:, :, :], negm[:, :, :],
                                      sink[:, :].unsqueeze(1).broadcast_to([P, 2, NH]), ALU.add).then_inc(den_in, 1)
                    dve.wait_ge(sinkexp, 1)
                    link(dve.tensor_tensor(esk[:, :, :], esk[:, :, :], rsum[:, :, :], ALU.add))
                    link(dve.reciprocal(esk[:, :, :], esk[:, :, :]))
                    dve.wait_ge(o_ready, NH)
                    for blk in range(2):
                        o = otok[:, blk, :].rearrange("p (h d) -> p h d", h=NH)
                        dve.tensor_tensor(o, o, esk[:, blk, :].unsqueeze(2).broadcast_to([P, NH, HD]), ALU.mult)\
                            .then_inc(o_norm, 1)

            dve.wait_ge(tanh_done, RT)
            link(dve.tensor_copy(pack[:, :, 0:3], xrp[:, :, SEQ:SEQ + 3]))
            link(dve.tensor_scalar(den[:, :, :], sg[:, :, :], 1.0, None, ALU.add))
            link(dve.reciprocal(den[:, :, :], den[:, :, :]))
            dve.tensor_tensor(sg[:, :, :], sg[:, :, :], den[:, :, :], ALU.mult).then_inc(ratio_ready, 1)
            dve.wait_ge(gates_done, 2)
            link(dve.tensor_tensor(ig[:, :, :], ig[:, :, :], xc[:, :, :], ALU.mult))
            dve.wait_ge(root_done, 1)
            link(dve.tensor_tensor(ig[:, :, :], ig[:, :, :], sg[:, :, :], ALU.mult))
            dve.wait_ge(decay_done, RT)
            for n in range(RT):
                dve.tensor_tensor_scan(hrec[:, n, 0:SEQ], rg[:, n, 0:SEQ], ig[:, n, 0:SEQ], 0.0, ALU.mult, ALU.add)
            link(dve.tensor_tensor(hrec[:, :, SEQ:T], rg[:, :, SEQ:T], stat[:, :, 24:32], ALU.mult))
            link(dve.tensor_tensor(hrec[:, :, SEQ:T], hrec[:, :, SEQ:T], ig[:, :, SEQ:T], ALU.add))
            dve.wait_ge(gelu_done, 1)
            dve.tensor_tensor(yr[:, :, :], yr[:, :, :], hrec[:, :, :], ALU.mult).then_inc(y_rnn_ready, 1)
            dve.tensor_copy(pack[:, :, 3:4], hrec[:, :, SEQ - 1:SEQ])
            dve.tensor_copy(pack[:, :, 4:12], xrs[:, :, :])
            dve.tensor_copy(pack[:, :, 12:20], hrec[:, :, SEQ:T]).then_inc(pack_ready, 1)

            dve.wait_ge(gates_done, 4)
            for m in range(16):
                dve.wait_ge(out_done, m + 1)
                ps = bank[m % 4][:, 0:T]
                if m < 8:
                    dve.tensor_tensor(ga[:, m, :], ga[:, m, :], ps, ALU.mult).then_inc(out_evac, 1)
                else:
                    f = m - 8
                    dve.tensor_tensor(gb[:, f, :], gb[:, f, :], ps, ALU.mult).then_inc(out_evac, 1)
                    dve.wait_ge(out_evac, m + 1)
                    dve.tensor_tensor(ga[:, f, :], ga[:, f, :], gb[:, f, :], ALU.add).then_inc(merged_ready, 1)

            def norm(psums, var_sem, sd_sem, g_row, b_row, done):
                for t, (_, n) in enumerate(TILES):
                    for h in range(2):
                        x = xtok[0:n, t, h * 512:(h + 1) * 512]
                        link(dve.scalar_tensor_tensor(out=x, in0=x, scalar=ALPHA, in1=psums[t][h][0:n, :],
                                                      op0=ALU.mult, op1=ALU.add))
                        link(dve.bn_stats(stats[0:n, t, h * 6:h * 6 + 6], x))
                    dve.bn_aggr(mv[0:n, t, :], stats[0:n, t, :]).then_inc(var_sem, 1)
                for t, (_, n) in enumerate(TILES):
                    x = xtok[0:n, t, :]
                    dve.wait_ge(sd_sem, t + 1)
                    link(dve.reciprocal(rstd[0:n, t:t + 1], sd[0:n, t:t + 1]))
                    link(dve.tensor_scalar(x, x, mv[0:n, t, 0:1], rstd[0:n, t:t + 1], ALU.subtract, ALU.mult))
                    link(dve.tensor_tensor(x, x, g_row[0:n, :], ALU.mult))
                    dve.tensor_tensor(x, x, b_row[0:n, :], ALU.add).then_inc(done, 1)

            dve.wait_ge(mix_done, 4)
            chunk_ready(dve, CH_LN)
            norm([(bank[4], bank[5]), (bank[6], bank[7]), (bank[0], bank[1])], var_ready, sd_ready,
                 slot(CH_LN)[:, 0:D], slot(CH_LN)[:, D:2 * D], x1_ready)

            dve.wait_ge(logits_done, 1)
            dve.wait_ge(s_bd, 32)
            R = lambda i, t, n: rt[0:n, i, t, :]
            for t, (_, n) in enumerate(TILES):
                l = lgt[0:n, t, :]
                v4 = m8[0:n, t, TOPK - 1:TOPK]
                link(dve.tensor_tensor(l, bank[5][0:n, t * NE:(t + 1) * NE], brb[0:n, :], ALU.add))
                link(dve.max(m8[0:n, t, :], l))
                dve.tensor_scalar(rsm[0:n, 0, t:t + 1], m8[0:n, t, 0:1], -1.0, None, ALU.mult).then_inc(top_ready, 1)
                dve.tensor_scalar(R(1, t, n), l, v4, None, ALU.is_equal)
                link(dve.tensor_scalar(R(0, t, n), l, v4, None, ALU.is_gt))
                link(dve.tensor_reduce(rsm[0:n, 1, t:t + 1], R(0, t, n), AX.X, ALU.add))
                link(dve.tensor_scalar(rsm[0:n, 1, t:t + 1], rsm[0:n, 1, t:t + 1], -1.0, float(TOPK),
                                       ALU.mult, ALU.add))
                link(dve.tensor_tensor_scan(R(2, t, n), ones[0:n, 0:NE], R(1, t, n), 0.0, ALU.mult, ALU.add))
                link(dve.scalar_tensor_tensor(out=R(3, t, n), in0=R(2, t, n), scalar=rsm[0:n, 1, t:t + 1],
                                              in1=R(1, t, n), op0=ALU.is_le, op1=ALU.mult))
                dve.tensor_tensor(R(4, t, n), R(0, t, n), R(3, t, n), ALU.add).then_inc(mask_ready, 1)
            dve.wait_ge(mask_ready, 3)
            for t, (_, n) in enumerate(TILES):
                dve.wait_ge(exp_ready, t + 1)
                link(dve.tensor_tensor(R(5, t, n), R(5, t, n), R(4, t, n), ALU.mult))
                link(dve.tensor_reduce(rsm[0:n, 2, t:t + 1], R(5, t, n), AX.X, ALU.add))
                link(dve.reciprocal(rsm[0:n, 3, t:t + 1], rsm[0:n, 2, t:t + 1]))
                link(dve.tensor_scalar(R(7, t, n), R(5, t, n), rsm[0:n, 3, t:t + 1], None, ALU.mult))
            dve.wait_ge(count_done, 1)
            for t, (_, n) in enumerate(TILES):
                link(dve.scalar_tensor_tensor(out=R(6, t, n), in0=bank[6][0:n, t * NE:(t + 1) * NE], scalar=BIG,
                                              in1=R(4, t, n), op0=ALU.add, op1=ALU.mult))
                dve.tensor_scalar(R(6, t, n), R(6, t, n), BIG, None, ALU.subtract).then_inc(route_ready, 1)
            count = bank[7][0:NE, 0:1]
            link(dve.tensor_scalar(ov[:, 2:3], count, float(CAP), None, ALU.is_gt))
            for j in range(2, 5):
                src, dst = (j, j + 1) if j < 4 else (4, 1)
                ins = dve.scalar_tensor_tensor(out=ov[:, dst:dst + 1], in0=count, scalar=float(j * CAP),
                                               in1=ov[:, src:src + 1], op0=ALU.is_gt, op1=ALU.add)
                if j < 4:
                    link(ins)
                else:
                    ins.then_inc(over_ready, 1)
            dve.wait_ge(start_done, 1)
            dve.wait_ge(over_ready, 1)
            oi = const[0:NE, C_OV:C_OV + MAXOVER]
            link(dve.tensor_copy(ov[:, 5:6], bank[7][0:NE, 8:9]))
            link(dve.tensor_tensor(ov[:, 6:7], ov[:, 5:6], ov[:, 1:2], ALU.add))
            link(dve.tensor_scalar(ohw[:, 0, :], oi, ov[:, 5:6], None, ALU.is_ge))
            link(dve.scalar_tensor_tensor(out=ohw[:, 1, :], in0=oi, scalar=ov[:, 6:7], in1=ohw[:, 0, :],
                                          op0=ALU.is_lt, op1=ALU.mult))
            link(dve.tensor_scalar(ohw[:, 2, :], oi, ov[:, 5:6], None, ALU.subtract))
            link(dve.tensor_scalar(ohw[:, 2, :], ohw[:, 2, :], -float(CAP), -float(CAP), ALU.mult, ALU.add))
            dve.memset(negj[:, 0:NE], 0.0)
            dve.tensor_tensor(negj[:, NE:NB], ohw[:, 2, :], ohw[:, 1, :], ALU.mult)
            dve.tensor_copy(selm[:, 0:NE], ident[0:NE, 0:NE])
            dve.tensor_copy(selm[:, NE:NB], ohw[:, 1, :])
            dve.wait_ge(route_turned, 1)
            dve.tensor_copy(posmT[:, :], bank[0][0:NE, 0:T])
            dve.tensor_copy(gateT[:, :], bank[1][0:NE, 0:T]).then_inc(routeT_ready, 1)
            dve.wait_ge(table_done, 1)
            for t, (_, n) in enumerate(TILES):
                dve.tensor_copy(posb[0:n, 1:1 + NB, t], bank[2][0:n, t * NB:(t + 1) * NB])
                dve.tensor_copy(gateb[0:n, 1:1 + NB, t], bank[3][0:n, t * NB:(t + 1) * NB])
            for half in range(2):
                dst = bup[:, :, :].rearrange("p (j h f) n -> p j h f n", j=NG, h=2)[:, :, half, :, :]
                dve.tensor_scalar(dst, bank[5 + half][:, 0:8 * NB].rearrange("p (j f n) -> p j f n", j=NG, f=2),
                                  float(half), None, ALU.add)
            dve.tensor_copy(tablei[0:1, 0:NB], bank[7][0:1, 32:32 + NB])
            link(dve.tensor_scalar(tablei[0:1, NB:NB + 1], bank[7][0:1, 16:17], float(NE), None, ALU.add))
            dve.wait_ge(s_out, 16 * N_OUT)
            link(dve.memset(yT[:, :, :], 0.0))
            link(dve.memset(onehot[:, :, :].bitcast(F32), 0.0))
            link(dve.memset(bank[4][:, :], 0.0))
            dve.memset(bank[5][:, :], 0.0).then_inc(y_cleared, 1)
            dve.wait_ge(y_cleared, 1)

            def one_hot(col, done):
                for t, (_, n) in enumerate(TILES):
                    ins = dve.tensor_scalar(onehot[0:n, t, CAP:2 * CAP], iota[0:n, 0:CAP], posb[0:n, col, t], None, ALU.is_equal)
                ins.then_inc(done, 1)

            def gates(col, done):
                for t, (_, n) in enumerate(TILES):
                    ins = dve.tensor_scalar(gated[0:n, t, :], iota[0:n, :], posb[0:n, col, t], gateb[0:n, col, t],
                                            ALU.is_equal, ALU.mult)
                ins.then_inc(done, 1)

            def add(d, count):
                dve.wait_ge(combined, count)
                dve.tensor_tensor(yT[:, d, :], yT[:, d, :], bank[CBANK[d % 2]][:, 0:T], ALU.add)\
                    .then_inc(added, 1)

            one_hot(bass.ds(1, 1), onehot_ready)
            dve.sem_inc(hT_taken, 2)
            dve.sem_inc(table_ready, 1)
            blocks = dve.value_load(tablei[0:1, NB:NB + 1], min_val=NE, max_val=NB)
            dve.wait_ge(xh_ready, 3)
            for t, (_, n) in enumerate(TILES):
                dve.tensor_tensor(xl[0:n, t, :], xtok[0:n, t, :], xh[0:n, t, :].bitcast(F32), ALU.subtract)\
                    .then_inc(xl_ready, 1)
            with dve.Fori(0, blocks) as b:
                inner = [0]

                def chain(ins):
                    inner[0] += 1
                    ins.then_inc(vm, 1)
                    dve.wait_ge(vm, b * CHAIN + inner[0])

                def split(i):
                    dve.wait_ge(hi_ready, b * 12 + (i + 1))
                    dve.tensor_tensor(lo[:, i % SPLITS, :], slot(NCH + i), hi[:, i % SPLITS, :].bitcast(F32),
                                      ALU.subtract).then_inc(lo_ready, 1)

                def clamp(j):
                    dve.wait_ge(hT_done, b * NG + (j + 1))
                    ps = bank[2 + j % 2][:, :].rearrange("p (f n) -> p f n", f=4)
                    o = glin[:, j % 2, :, :]
                    chain(dve.tensor_tensor(o, ps[:, :, 0:CAP],
                                            bup[:, 4 * j:4 * j + 4, bass.ds(b, 1)].broadcast_to([P, 4, CAP]), ALU.add))
                    dve.tensor_tensor(o, o, ps[:, :, CAP:P], ALU.add).then_inc(hT_taken, 1)
                    dve.wait_ge(hT_taken, b * NG + (j + 3))
                    dve.tensor_scalar(o[:, 0:2, :], o[:, 0:2, :], LIMIT, None, ALU.min).then_inc(glu_ready, 1)
                    dve.tensor_scalar(o[:, 2:4, :], o[:, 2:4, :], LIMIT + 1, None, ALU.min).then_inc(lin_ready, 1)

                def activate(j):
                    dve.wait_ge(sig_ready, b * NG + (j + 1))
                    dve.wait_ge(lin_ready, b * NG + (j + 1))
                    o = act_[:, j % 2, :, :]
                    high, low = at[:, 2 * j:2 * j + 2, 0:CAP], at[:, 2 * j:2 * j + 2, CAP:P]
                    chain(dve.tensor_tensor(o, glin[:, j % 2, 0:2, :], sig[:, j % 2, :, :], ALU.mult))
                    chain(dve.scalar_tensor_tensor(out=o, in0=glin[:, j % 2, 2:4, :], scalar=1.0 - LIMIT, in1=o,
                                                   op0=ALU.max, op1=ALU.mult))
                    chain(dve.tensor_copy(high, o))
                    dve.tensor_tensor(low, o, high.bitcast(F32), ALU.subtract).then_inc(at_ready, 1)

                def adds(*tiles_):
                    for d in tiles_:
                        add(d, b * 8 + (d + 1))

                split(0)
                split(1)
                dve.wait_ge(gated_turned, b + 1)
                gates(bass.ds(b, 1), gated_ready)
                split(3)
                split(4)
                dve.wait_ge(gathered, b + 1)
                one_hot(bass.ds(b + 2, 1), onehot_ready)
                split(5)
                clamp(0)
                adds(0, 1)
                adds(2)
                split(7)
                activate(0)
                clamp(1)
                adds(3, 4)
                split(8)
                adds(5)
                activate(1)
                adds(6)
                split(9)
                clamp(2)
                adds(7)
                activate(2)
                clamp(3)
                split(11)
                activate(3)
                assert inner[0] == CHAIN
            dve.wait_ge(gated_turned, blocks + 1)
            gates(bass.ds(blocks, 1), gated_ready)
            for d in range(KD):
                add(d, blocks * 8 + (d + 1))
            dve.wait_ge(final_done, 3)
            dve.wait_ge(ln2_loaded, 48)
            norm([(bank[0], bank[1]), (bank[2], bank[3]), (bank[4], bank[5])], var2_ready, sd2_ready,
                 raw[:, 0, 0:D], raw[:, 0, D:2 * D], fin_ready)


INS = ["x_prompt", "x_sample", "cache_k", "cache_v", "state_conv", "state_h", "w_in", "attn_sinks", "conv_w", "conv_b",
       "rg_wa", "rg_ba", "rg_wx", "rg_bx", "rg_lambda", "w_attn_out", "w_rnn_out", "w_out", "ln1_g", "ln1_b",
       "w_router", "b_router", "w_up", "b_up", "w_down", "b_down", "ln2_g", "ln2_b"]
OUTS = [("o_yp", (1, SEQ, D)), ("o_ys", (DECB, 1, D)), ("o_kp", (1, 1, WIN, NKV, HD)), ("o_vp", (1, 1, WIN, NKV, HD)),
        ("o_cp", (1, 1, CONV - 1, DR)), ("o_hp", (1, 1, DR)), ("o_ks", (1, DECB, WIN, NKV, HD)),
        ("o_vs", (1, DECB, WIN, NKV, HD)), ("o_cs", (1, DECB, CONV - 1, DR)), ("o_hs", (1, DECB, DR))]


def kernel(**inputs):
    import concourse.bacc as bacc
    from concourse.bass_utils import run_bass_kernel_spmd

    nc = bacc.Bacc("TRN2", target_bir_lowering=False, num_devices=1)
    arrays, aps = {}, {}
    for name in INS + ["consts"]:
        x = constants() if name == "consts" else np.ascontiguousarray(inputs[name])
        arrays["in_" + name] = x
        aps[name] = nc.dram_tensor("in_" + name, x.shape, mybir.dt.from_np(x.dtype), kind="ExternalInput").ap()
    for name, shape in OUTS:
        aps[name] = nc.dram_tensor("out_" + name, shape, F32, kind="ExternalOutput").ap()
    build(nc, aps)
    r = run_bass_kernel_spmd(nc, [arrays], core_ids=[0])
    return tuple(r.results[0]["out_" + name] for name, _ in OUTS)
```

```python
from contextlib import ExitStack

import numpy as np

import concourse.bass as bass
from concourse import mybir

F32 = mybir.dt.float32
F32R = mybir.dt.float32r
I32 = mybir.dt.int32
ALU = mybir.AluOpType
ACT = mybir.ActivationFunctionType
AX = mybir.AxisListType

P = 128
D = 1024
SEQ, DECB = 256, 8
T = SEQ + DECB
KD = D // P
TILES = [(0, 128), (128, 128), (256, 8)]
NH, NKV, HD = 16, 2, 64
GROUP = NH // NKV
WIN = 128
KVW = NKV * HD
DR = 1280
RT = DR // P
CONV = 4
NE, TOPK, DFF = 32, 4, 1024
FT = 2 * DFF // P
LIMIT, SALPHA = 7.0, 1.702
ALPHA = 2.0 ** 0.25
EPS = 1e-5
PROJ = D + 2 * KVW + 2 * DR + 2 * D
CAP = 64
N_OUT = 11
CHAIN = 16
MAXOVER = 16
NB = NE + MAXOVER
NCOL = NB + 2
BIG = 4096.0
INVALID = 1e30

RING = 6
SLOT = 2048
SPLITS = 4
UPC = 8
NG = 4
ON_POOL = (2, 6, 10)
ON_DVE = tuple(i for i in range(12) if i not in ON_POOL)

C_ID, C_STACK, C_TRI, C_IOTA, C_DIST = 0, 128, 192, 320, 448
C_TDIST = C_DIST + 512
C_SLOPE = C_TDIST + 128
C_OV = C_SLOPE + 1
C_EIDX = C_OV + MAXOVER
C_W = C_EIDX + 1


def constants():
    c = np.zeros((P, C_W), np.float32)
    p = np.arange(P)[:, None]
    j = np.arange(P)[None, :]
    c[:, C_ID:C_ID + P] = p == j
    c[:, C_STACK:C_STACK + CAP] = (p % CAP) == np.arange(CAP)[None, :]
    c[:, C_TRI:C_TRI + P] = p < j
    c[:, C_IOTA:C_IOTA + P] = j % CAP
    for blk in range(2):
        prev = p + WIN - j
        cur = p - j
        c[:, C_DIST + 256 * blk:C_DIST + 256 * blk + 128] = np.where((prev < WIN) & (blk > 0), prev, INVALID)
        c[:, C_DIST + 256 * blk + 128:C_DIST + 256 * blk + 256] = np.where(cur >= 0, cur, INVALID)
    c[:, C_TDIST:C_TDIST + P] = WIN - 1 - j
    c[:NH, C_SLOPE] = [-slope(h) for h in range(NH)]
    c[:, C_OV:C_OV + MAXOVER] = np.arange(MAXOVER)[None, :]
    c[:, C_EIDX] = np.arange(P)
    return c


def slope(h):
    return float(np.float32(2.0) ** np.float32(-8.0 * (h + 1) / NH))


def plan():
    def cols(base, width):
        return [("win", base + 256 * i) for i in range(width // 256)]
    off_k, off_xr = D, D + 2 * KVW
    off_yr, off_ga, off_gb = off_xr + DR, off_xr + 2 * DR, off_xr + 2 * DR + D
    chunks, tiles = [], []

    def section(names, base, width):
        for i, c in enumerate(cols(base, width)):
            chunks.append(c)
            for half in range(2):
                tiles.append((names, 2 * i + half, len(chunks) - 1, half))

    section("kv", off_k, 2 * KVW)
    section("q", 0, D)
    section("xr", off_xr, DR)
    section("yr", off_yr, DR)
    for name, what in (("r", "wa"), ("i", "wx")):
        chunks.append((what, 0))
        tiles.extend((name, n, len(chunks) - 1, 0) for n in range(RT))
    section("ga", off_ga, D)
    section("gb", off_gb, D)
    placed = {("yr", 8): ("sample", 0), ("yr", 9): ("sample", 1), ("i", 9): ("sample", 2), ("ga", 0): ("sample", 3),
              ("ga", 1): ("gate", 0), ("ga", 3): ("oturn", 0), ("ga", 5): ("gate", 1)}
    order = []
    step = 0
    for n, (name, idx, _, _) in enumerate(tiles):
        order.append(("tile", n))
        if n in (3, 5):
            order.append(("parturn", 0) if n == 3 else ("kvturn", 0))
        if name in ("xr", "yr") and step < NH + 2:
            order.append(("step", step))
            step += 1
        if (name, idx) in placed:
            order.append(placed[name, idx])
    assert step == NH + 2
    n_tiles_chunks = len(chunks)
    chunks += [("wao", 256 * i) for i in range(4)] + [("wro", P * i) for i in range(8)]
    chunks += [("wout", 2 * i) for i in range(4)] + [("ln1", 0), ("bup", 0)]
    return chunks, tiles, order, n_tiles_chunks


def build(nc, a):
    chunks, tiles, order, NPC = plan()
    NCH = len(chunks)
    CH_AO, CH_RO, CH_OUT, CH_LN, CH_BUP = NPC, NPC + 4, NPC + 12, NPC + 16, NPC + 17
    NT1 = len(tiles)
    N_GATES = max(n for n in range(NT1) if tiles[n][0] == "i") + 1

    def flat(name):
        ap = a[name]
        return ap[0]

    with ExitStack() as whole:
        def sb(name, shape, dt=F32, scope=whole):
            return scope.enter_context(nc.sbuf_tensor(name, shape, dt))

        def sem(name):
            return whole.enter_context(nc.semaphore(name))

        bank = [whole.enter_context(nc.psum_tensor(f"bank{i}", [P, 512], F32)) for i in range(8)]

        const = sb("const", [P, C_W])
        ident = const[:, C_ID:C_ID + P]
        stack = const[:, C_STACK:C_STACK + CAP]
        iota = const[:, C_IOTA:C_IOTA + P]
        raw = sb("raw", [P, RING, SLOT])
        xtok = sb("xtok", [P, 3, D])
        ln2 = raw[:, NCH % RING, :]
        bdown = raw[0:NE, (NCH + 1) % RING, 0:D]
        gateT = sb("gateT", [NE, T])
        posb = sb("posb", [P, NCOL, 3])
        gateb = sb("gateb", [P, NCOL, 3])
        bup = sb("bup", [P, FT, NB])
        tablei = sb("tablei", [1, NB + 2], I32)
        ones = sb("ones", [P, P])
        stats = sb("stats", [P, 3, 12])
        mv = sb("mv", [P, 3, 2])
        sd = sb("sd", [P, 3])
        rstd = sb("rstd", [P, 3])
        warm = sb("warm", [P, 1])
        epsc = sb("epsc", [P, 1])

        early = ExitStack()
        xT = sb("xT", [P, KD, T], scope=early)
        first = ExitStack()
        parr = sb("parr", [80, P], scope=first)
        statr = sb("statr", [32, DR], scope=first)
        first.close()
        lg = sb("lg", [P, 2, 2, 256], scope=early)
        rmax = sb("rmax", [P, 2, 2], scope=early)
        sb("rows_rest", [P, 384], scope=early)
        par = sb("par", [P, 80], scope=early)
        stat = sb("stat", [P, RT, 32], scope=early)
        sink = sb("sink", [P, NH], scope=early)
        sinkc = sb("sinkc", [NH, 1], scope=early)
        wr = sb("wr", [P, KD, NE], scope=early)
        brb = sb("brb", [P, NE], scope=early)
        kT = sb("kT", [P, T], scope=early)
        vT = sb("vT", [P, T], scope=early)
        kz = sb("kz", [P, 4, 384], scope=early)
        vtok = sb("vtok", [P, 2, P], scope=early)
        ktok = sb("ktok", [P, P], scope=early)
        kv8 = sb("kv8", [DECB, 2, P], scope=early)
        qT = sb("qT", [P, KD, T], scope=early)
        pT = sb("pT", [P, 2, 384], scope=early)
        negm = sb("negm", [P, 2, NH], scope=early)
        rsum = sb("rsum", [P, 2, NH], scope=early)
        esk = sb("esk", [P, 2, NH], scope=early)
        otok = sb("otok", [P, 2, D], scope=early)
        oT = qT
        kc = sb("kc", [P, DECB, KVW], scope=early)
        vc = sb("vc", [P, DECB, KVW], scope=early)
        xrp = sb("xrp", [P, RT, T], scope=early)
        xrs = sb("xrs", [P, RT, DECB], scope=early)
        xc = sb("xc", [P, RT, T], scope=early)
        yr = sb("yr", [P, RT, T], scope=early)
        rg = sb("rg", [P, RT, T], scope=early)
        ig = sb("ig", [P, RT, T], scope=early)
        ga = sb("ga", [P, KD, T], scope=early)
        gb = sb("gb", [P, KD, T], scope=early)
        sg = sb("sg", [P, RT, T], scope=early)
        den = xrp
        hrec = xc
        sgf = sg[:, :, :].rearrange("p a b -> p (a b)")
        kcT = sgf[:, 0:1024].rearrange("p (b k) -> p b k", b=DECB)
        slog = sgf[0:NH, 1024:2048].rearrange("p (b k) -> p b k", b=DECB)
        qz = sgf[:, 2048:2176].rearrange("p (b h) -> p b h", b=DECB)
        pTs = sgf[:, 2176:2304].rearrange("p (b h) -> p b h", b=DECB)
        srow = sb("srow", [NH, 4, DECB], scope=early)
        pack = sb("pack", [P, RT, 20], scope=early)
        lamt = sb("lamt", [P, 8, RT], scope=early)
        rgf = sgf[:, 1024:RT * T]
        rt = rgf[:, 0:768].rearrange("p (i t e) -> p i t e", i=8, t=3)
        lgt = rgf[:, 768:864].rearrange("p (t e) -> p t e", t=3)
        m8 = rgf[:, 864:888].rearrange("p (t e) -> p t e", t=3)
        rsm = rgf[:, 888:900].rearrange("p (i t) -> p i t", i=4)
        posmT = rgf[0:NE, 900:900 + T]
        ov = rgf[0:NE, 1164:1172]
        selm = rgf[0:NE, 1172:1172 + NB]
        negj = rgf[0:NE, 1220:1220 + NB]
        ohw = rgf[0:NE, 1268:1268 + 3 * MAXOVER].rearrange("p (i o) -> p i o", i=3)
        rows = otok[0:20, :, :].rearrange("p a b -> p (a b)")[:, 0:DR]
        early.close()

        late = ExitStack()
        hi = sb("hi", [P, SPLITS, SLOT], F32R, scope=late)
        lo = sb("lo", [P, SPLITS, SLOT], F32R, scope=late)
        xg = sb("xg", [P, KD, P], F32R, scope=late)
        at = sb("at", [P, KD, P], F32R, scope=late)
        hsb = sb("hsb", [P, 2, 512], scope=late)
        xh = sb("xh", [P, 3, D], F32R, scope=late)
        xl = sb("xl", [P, 3, D], F32R, scope=late)
        ysb = sb("ysb", [P, D], scope=late)
        gt = sb("gt", [P, T], scope=late)
        onehot = sb("onehot", [P, 3, 3 * CAP], F32R, scope=late)
        gx = sb("gx", [P, D], scope=late)
        gated = sb("gated", [P, 3, P], scope=late)
        glin = sb("glin", [P, 2, 4, CAP], scope=late)
        sig = sb("sig", [P, 2, 2, CAP], scope=late)
        act_ = sb("act_", [P, 2, 2, CAP], scope=late)
        yT = sb("yT", [P, KD, T], scope=late)
        late.close()

        s_const = sem("s_const")
        s_x = sem("s_x")
        s_par = sem("s_par")
        s_misc = sem("s_misc")
        s_cache = sem("s_cache")
        s_new = sem("s_new")
        s_bd = sem("s_bd")
        s_out = sem("s_out")
        y_out = sem("y_out")
        loaded = [sem(f"loaded{i}") for i in range(RING)]
        x_turned = sem("x_turned")
        xT_ready = sem("xT_ready")
        par_turned = sem("par_turned")
        par_ready = sem("par_ready")
        tile_done = sem("tile_done")
        tile_evac = sem("tile_evac")
        kv_turned = sem("kv_turned")
        kv_ready = sem("kv_ready")
        kz_ready = sem("kz_ready")
        scored = sem("scored")
        scores_taken = sem("scores_taken")
        max_ready = sem("max_ready")
        probs_ready = sem("probs_ready")
        probs_turned = sem("probs_turned")
        pT_ready = sem("pT_ready")
        pv_done = sem("pv_done")
        o_ready = sem("o_ready")
        den_in = sem("den_in")
        sinkexp = sem("sinkexp")
        o_norm = sem("o_norm")
        o_turned = sem("o_turned")
        oT_ready = sem("oT_ready")
        conv_ready = sem("conv_ready")
        lam_in = sem("lam_in")
        lam_exp = sem("lam_exp")
        lam_ready = sem("lam_ready")
        gates_done = sem("gates_done")
        tanh_done = sem("tanh_done")
        ratio_ready = sem("ratio_ready")
        root_done = sem("root_done")
        decay_done = sem("decay_done")
        gelu_done = sem("gelu_done")
        y_rnn_ready = sem("y_rnn_ready")
        s_kt = sem("s_kt")
        s_kte = sem("s_kte")
        s_qz = sem("s_qz")
        s_sc = sem("s_sc")
        s_sm = sem("s_sm")
        s_ex = sem("s_ex")
        s_pn = sem("s_pn")
        s_ptt = sem("s_ptt")
        s_pte = sem("s_pte")
        s_pv = sem("s_pv")
        s_os = sem("s_os")
        out_done = sem("out_done")
        out_evac = sem("out_evac")
        merged_ready = sem("merged_ready")
        mix_done = sem("mix_done")
        pack_ready = sem("pack_ready")
        pack_turned = sem("pack_turned")
        rows_ready = sem("rows_ready")
        var_ready = sem("var_ready")
        sd_ready = sem("sd_ready")
        x1_ready = sem("x1_ready")
        x1_turned = sem("x1_turned")
        x1T_ready = sem("x1T_ready")
        logits_done = sem("logits_done")
        top_ready = sem("top_ready")
        exp_ready = sem("exp_ready")
        mask_ready = sem("mask_ready")
        count_done = sem("count_done")
        over_ready = sem("over_ready")
        start_done = sem("start_done")
        route_ready = sem("route_ready")
        route_turned = sem("route_turned")
        routeT_ready = sem("routeT_ready")
        table_done = sem("table_done")
        table_ready = sem("table_ready")
        bup_ready = sem("bup_ready")
        v = sem("v")
        vm = sem("vm")
        onehot_ready = sem("onehot_ready")
        gated_ready = sem("gated_ready")
        gathered = sem("gathered")
        gx_ready = sem("gx_ready")
        gx_turned = sem("gx_turned")
        gated_turned = sem("gated_turned")
        gt_ready = sem("gt_ready")
        xh_ready = sem("xh_ready")
        xl_ready = sem("xl_ready")
        xg_ready = sem("xg_ready")
        split_free = sem("split_free")
        hi_ready = sem("hi_ready")
        lo_ready = sem("lo_ready")
        lo_pool_ready = sem("lo_pool_ready")
        up_taken = sem("up_taken")
        hT_done = sem("hT_done")
        hT_taken = sem("hT_taken")
        glu_ready = sem("glu_ready")
        lin_ready = sem("lin_ready")
        sig_ready = sem("sig_ready")
        at_ready = sem("at_ready")
        y_ready = sem("y_ready")
        combined = sem("combined")
        added = sem("added")
        y_cleared = sem("y_cleared")
        final_done = sem("final_done")
        var2_ready = sem("var2_ready")
        sd2_ready = sem("sd2_ready")
        biases_loaded = sem("biases_loaded")
        normal_ready = sem("normal_ready")
        scaled = sem("scaled")
        fin_pool_ready = sem("fin_pool_ready")
        fin_ready = sem("fin_ready")

        def slot(c):
            return raw[:, c % RING, :]

        def loads(c):
            return sum(2 if chunks[x][0] == "ln1" else 1 for x in range(c % RING, min(c + 1, NCH), RING)) \
                + sum(2 if (x - NCH) % 12 < UPC else 1 for x in range(NCH, c + 1) if x % RING == c % RING)

        def chunk_ready(e, c):
            e.wait_ge(loaded[c % RING], 16 * loads(c))

        def low_ready(e, i, b):
            if i in ON_POOL:
                e.wait_ge(lo_pool_ready, b * len(ON_POOL) + (ON_POOL.index(i) + 1))
            else:
                e.wait_ge(lo_ready, b * len(ON_DVE) + (ON_DVE.index(i) + 1))

        TURN_TO = (0, 1, 6, 7, 0)
        LOGITS = (5, 4, 1)
        CBANK = (6, 7)
        LOADED0 = [16 * loads(NCH + i) for i in range(12)]
        PER_BLOCK = [16 * (loads(NCH + i + 12) - loads(NCH + i)) for i in range(12)]

        block = whole.enter_context(nc.Block())

        @block.sync
        def _(sp):
            win = flat("w_in").rearrange("(k p) n -> p k n", p=P)
            wao = flat("w_attn_out").rearrange("(k p) n -> p k n", p=P)
            wro = flat("w_rnn_out").rearrange("(k p) n -> p k n", p=P)
            wout = flat("w_out").rearrange("(k p) n -> p k n", p=P)
            w_up = a["w_up"].rearrange("l e d (h j n) -> (l e d) h j n", h=2, j=NG)
            w_down = a["w_down"].rearrange("l e d n -> (l e d) n")

            def used(c):
                if c < NPC:
                    sp.wait_ge(tile_done, max(n for n in range(NT1) if tiles[n][2] == c) + 1)
                elif c < CH_RO:
                    sp.wait_ge(out_done, 2 * (c - CH_AO) + 2)
                elif c < CH_OUT:
                    sp.wait_ge(out_done, 8 + c - CH_RO + 1)
                elif c < CH_LN:
                    sp.wait_ge(mix_done, 3)
                elif c == CH_LN:
                    sp.wait_ge(x1_ready, 3)
                else:
                    sp.wait_ge(table_done, 3)

            sp.dma_start(const[:, :], a["consts"]).then_inc(s_const, 16)
            for t in range(2):
                sp.dma_start(xtok[:, t, :], a["x_prompt"][0, t * P:(t + 1) * P, :]).then_inc(s_x, 16)
            sp.dma_start(xtok[0:DECB, 2, :], a["x_sample"][:, 0, :]).then_inc(s_x, 16)
            for c, (kind, at0) in enumerate(chunks):
                if c >= RING:
                    used(c - RING)
                if kind == "win":
                    pieces = [(slot(c).rearrange("p (k n) -> p k n", k=KD), win[:, :, at0:at0 + 256])]
                elif kind in ("wa", "wx"):
                    pieces = [(slot(c)[:, 0:DR].rearrange("p (n d) -> p n d", n=RT),
                               flat("rg_" + kind).rearrange("n c d -> c n d"))]
                elif kind == "wao":
                    pieces = [(slot(c).rearrange("p (k n) -> p k n", k=KD), wao[:, :, at0:at0 + 256])]
                elif kind == "wro":
                    pieces = [(slot(c)[:, 0:DR].rearrange("p (k n) -> p k n", k=RT), wro[:, :, at0:at0 + P])]
                elif kind == "wout":
                    pieces = [(slot(c).rearrange("p (k n) -> p k n", k=2), wout[:, at0:at0 + 2, :])]
                elif kind == "ln1":
                    pieces = [(slot(c)[:, 0:D], a["ln1_g"].partition_broadcast(P)),
                              (slot(c)[:, D:2 * D], a["ln1_b"].partition_broadcast(P))]
                else:
                    pieces = [(slot(c)[0:NE, :], flat("b_up"))]
                for dst, src in pieces:
                    sp.dma_start(dst, src).then_inc(loaded[c % RING], 16)

            def moe_chunk(i, row0):
                c = NCH + i
                if i < UPC:
                    j, half = i // 2, i % 2
                    for h in range(2):
                        src = w_up[bass.ds(row0 + half * 512, 512), h, j, :].rearrange("(k p) n -> p k n", p=P)
                        dst = slot(c).rearrange("p (k h n) -> p k h n", k=4, h=2)[:, :, h, :]
                        sp.dma_start(dst, src).then_inc(loaded[c % RING], 16)
                    return
                src = w_down[bass.ds(row0 + (i - UPC) * 256, 256), :].rearrange("(k p) n -> p k n", p=P)
                dst = slot(c).rearrange("p (k n) -> p k n", k=2)
                sp.dma_start(dst, src).then_inc(loaded[c % RING], 16)

            for i in range(12):
                if i < RING:
                    used(NCH + i - RING)
                else:
                    low_ready(sp, i - RING, 0)
                moe_chunk(i, 0)
            sp.wait_ge(table_ready, 1)
            blocks = sp.value_load(tablei[0:1, NB:NB + 1], min_val=NE, max_val=NB)
            with sp.Fori(1, blocks) as b:
                e = sp.value_load(tablei[0:1, bass.ds(b, 1)], min_val=0, max_val=NE - 1)
                row0 = e * D
                before = b - 1
                for i in range(12):
                    if i < RING:
                        low_ready(sp, 12 + i - RING, before)
                    else:
                        low_ready(sp, i - RING, b)
                    moe_chunk(i, row0)
            sp.wait_ge(split_free, blocks * 12 + (SPLITS + UPC - 12))
            sp.dma_start(ln2[:, 0:D], a["ln2_g"].partition_broadcast(P)).then_inc(loaded[NCH % RING], 16)
            sp.dma_start(ln2[:, D:2 * D], a["ln2_b"].partition_broadcast(P)).then_inc(loaded[NCH % RING], 16)
            sp.dma_start(bdown, flat("b_down")).then_inc(biases_loaded, 16)
            for t, (t0, n) in enumerate(TILES):
                if t < 2:
                    sp.wait_ge(fin_pool_ready, t + 1)
                else:
                    sp.wait_ge(fin_ready, 1)
                dst = a["o_yp"][0, t0:t0 + n, :] if t < 2 else a["o_ys"][:, 0, :]
                sp.dma_start(dst, xtok[0:n, t, :]).then_inc(y_out, 16)
            sp.wait_ge(y_out, 48)

        @block.gpsimd
        def _(pool):
            pool.dma_start(a["o_ks"][0, :, 0:WIN - 1], a["cache_k"][0, :, 1:WIN]).then_inc(s_out, 16)
            pool.dma_start(a["o_vs"][0, :, 0:WIN - 1], a["cache_v"][0, :, 1:WIN]).then_inc(s_out, 16)
            pool.dma_start(a["o_cs"][0, :, 0:2], a["state_conv"][0, :, 1:3]).then_inc(s_out, 16)
            pool.wait_ge(kv_ready, 3)
            pool.wait_ge(s_cache, 32)
            pool.dma_start(kc[P - 1:P, :, :], kv8[:, 0:1, :]).then_inc(s_new, 16)
            pool.dma_start(vc[P - 1:P, :, :], kv8[:, 1:2, :]).then_inc(s_new, 16)
            kvo = lambda name: a[name][0, :, WIN - 1, :, :].rearrange("b g d -> b (g d)")
            pool.dma_start(kvo("o_ks"), kv8[:, 0, :]).then_inc(s_out, 16)
            pool.dma_start(kvo("o_vs"), kv8[:, 1, :]).then_inc(s_out, 16)
            pool.dma_start(a["o_kp"][0, 0].rearrange("s g d -> s (g d)"), ktok[:, :]).then_inc(s_out, 16)
            pool.dma_start(a["o_vp"][0, 0].rearrange("s g d -> s (g d)"), vtok[:, 1, :]).then_inc(s_out, 16)
            pool.wait_ge(rows_ready, 3)
            pool.dma_start(a["o_cp"][0, 0], rows[0:3, :]).then_inc(s_out, 16)
            pool.dma_start(a["o_hp"][0], rows[3:4, :]).then_inc(s_out, 16)
            pool.dma_start(a["o_cs"][0, :, 2, :], rows[4:12, :]).then_inc(s_out, 16)
            pool.dma_start(a["o_hs"][0], rows[12:20, :]).then_inc(s_out, 16)
            pool.wait_ge(s_out, 16 * N_OUT)
            pool.wait_ge(table_ready, 1)
            blocks = pool.value_load(tablei[0:1, NB:NB + 1], min_val=NE, max_val=NB)
            with pool.Fori(0, blocks) as b:
                for i in ON_POOL:
                    pool.wait_ge(hi_ready, b * 12 + (i + 1))
                    pool.tensor_tensor(lo[:, i % SPLITS, :], slot(NCH + i), hi[:, i % SPLITS, :].bitcast(F32),
                                       ALU.subtract).then_inc(lo_pool_ready, 1)
            for t in range(2):
                pool.wait_ge(normal_ready, t + 1)
                pool.tensor_tensor(xtok[:, t, :], xtok[:, t, :], ln2[:, 0:D], ALU.mult).then_inc(scaled, 1)
                pool.wait_ge(scaled, t + 1)
                pool.tensor_tensor(xtok[:, t, :], xtok[:, t, :], ln2[:, D:2 * D], ALU.add).then_inc(fin_pool_ready, 1)

        @block.scalar
        def _(act):
            r0 = 0
            for name in ("conv_w", "conv_b", "rg_ba", "rg_bx", "rg_lambda"):
                src = a[name][0].rearrange("j (t p) -> (j t) p", p=P) if name == "conv_w" \
                    else a[name][0].rearrange("(t p) -> t p", p=P)
                n = 40 if name == "conv_w" else RT
                act.dma_start(parr[r0:r0 + n, :], src).then_inc(s_par, 16)
                r0 += n
            act.dma_start(statr[0:24, :], a["state_conv"][0].rearrange("b j c -> (b j) c")).then_inc(s_par, 16)
            act.dma_start(statr[24:32, :], a["state_h"][0]).then_inc(s_par, 16)
            act.dma_start(sink[:, :], a["attn_sinks"].partition_broadcast(P)).then_inc(s_misc, 16)
            act.dma_start(sinkc[:, :], a["attn_sinks"].rearrange("l h -> h l")).then_inc(s_misc, 16)
            act.dma_start(kc[0:P - 1, :, :], a["cache_k"][0, :, 1:WIN].rearrange("b w g d -> w b (g d)"))\
                .then_inc(s_cache, 16)
            act.dma_start(vc[0:P - 1, :, :], a["cache_v"][0, :, 1:WIN].rearrange("b w g d -> w b (g d)"))\
                .then_inc(s_cache, 16)
            act.dma_start(wr[:, :, :], flat("w_router").rearrange("(k p) e -> p k e", p=P)).then_inc(s_bd, 16)
            act.dma_start(brb[:, :], a["b_router"].partition_broadcast(P)).then_inc(s_bd, 16)

            def turned_x(g, frm, ready, done):
                act.wait_ge(ready, g + 1)
                if g < 4:
                    t, d0 = g // 2, 4 * (g % 2)
                    act.activation(xT[:, d0:d0 + 4, t * P:(t + 1) * P],
                                   bank[frm][:, :].rearrange("p (d n) -> p d n", d=4), ACT.Copy).then_inc(done, 1)
                else:
                    act.activation(xT[:, :, SEQ:T], bank[frm][:, 0:64].rearrange("p (d n) -> p d n", d=KD),
                                   ACT.Copy).then_inc(done, 1)

            for g in range(5):
                turned_x(g, g, x_turned, xT_ready)

            def exps(h):
                act.wait_ge(max_ready, h + 1)
                for blk in range(2):
                    last = act.activation(lg[:, h % 2, blk, :], lg[:, h % 2, blk, :], ACT.Exp,
                                          bias=negm[:, blk, h:h + 1], accum_out=rsum[:, blk, h:h + 1])
                last.then_inc(probs_ready, 1)

            for what, n in order:
                if what == "tile":
                    name, idx, _, _ = tiles[n]
                    ps = bank[n % 4][:, 0:T]
                    act.wait_ge(tile_done, n + 1)
                    if name == "kv":
                        ins = act.activation((kT if idx == 0 else vT)[:, :], ps, ACT.Copy)
                    elif name == "q":
                        ins = act.activation(qT[:, idx, :], ps, ACT.Copy, scale=HD ** -0.5)
                    elif name == "xr":
                        act.activation(xrp[:, idx, 3:3 + SEQ], ps[:, 0:SEQ], ACT.Copy)
                        ins = act.activation(xrs[:, idx, :], ps[:, SEQ:T], ACT.Copy)
                    elif name in ("r", "i"):
                        if name == "r" and idx == 0:
                            act.wait_ge(par_ready, 2)
                        col = (50 if name == "r" else 60) + idx
                        ins = act.activation((rg if name == "r" else ig)[:, idx, :], ps, ACT.Identity,
                                             bias=par[:, col:col + 1])
                    else:
                        ins = act.activation({"yr": yr, "ga": ga, "gb": gb}[name][:, idx, :], ps, ACT.Copy)
                    ins.then_inc(tile_evac, 1)
                elif what == "kvturn":
                    act.wait_ge(lam_in, 1)
                    act.activation(lamt[:, 2, :], lamt[:, 1, :], ACT.Exp, scale=-1.0).then_inc(lam_exp, 1)
                    act.wait_ge(kv_turned, 1)
                    act.activation(vtok[:, :, :], bank[6][:, 0:256].rearrange("p (b n) -> p b n", b=2), ACT.Copy)\
                        .then_inc(kv_ready, 1)
                    act.activation(ktok[:, :], bank[6][:, 256:384], ACT.Copy).then_inc(kv_ready, 1)
                    act.activation(kv8[:, :, :], bank[7][0:DECB, 0:256].rearrange("p (b n) -> p b n", b=2), ACT.Copy)\
                        .then_inc(kv_ready, 1)
                elif what == "step":
                    h = n - 1
                    if 0 <= h < NH:
                        if h >= 2:
                            act.wait_ge(pv_done, h - 1)
                        act.wait_ge(probs_turned, h + 1)
                        act.activation(pT[:, h % 2, :], bank[6][:, 0:384], ACT.Copy).then_inc(pT_ready, 1)
                    h = n - 2
                    if 0 <= h < NH:
                        act.wait_ge(pv_done, h + 1)
                        act.activation(otok[:, :, h * HD:(h + 1) * HD],
                                       bank[7][:, (h % 4) * P:(h % 4 + 1) * P].rearrange("p (b n) -> p b n", b=2),
                                       ACT.Copy).then_inc(o_ready, 1)
                    if n < NH:
                        exps(n)
                    if n == NH + 1:
                        act.wait_ge(den_in, 1)
                        act.activation(esk[:, :, :], esk[:, :, :], ACT.Exp).then_inc(sinkexp, 1)
                elif what == "gate" and n == 0:
                    act.wait_ge(tile_evac, N_GATES)
                    act.activation(rg[:, :, :], rg[:, :, :], ACT.Sigmoid).then_inc(gates_done, 1)
                    act.wait_ge(gates_done, 1)
                    act.wait_ge(lam_ready, 1)
                    act.wait_ge(s_os, 1)
                    for n_ in range(RT):
                        act.activation(sg[:, n_, :], rg[:, n_, :], ACT.Tanh, scale=lamt[:, 7, n_:n_ + 1])\
                            .then_inc(tanh_done, 1)
                    act.activation(ig[:, :, :], ig[:, :, :], ACT.Sigmoid).then_inc(gates_done, 1)
                elif what == "gate":
                    act.wait_ge(tanh_done, RT)
                    for n_ in range(RT):
                        act.activation(rg[:, n_, :], rg[:, n_, :], ACT.Exp, scale=lamt[:, 6, n_:n_ + 1])\
                            .then_inc(decay_done, 1)
                    act.activation(yr[:, :, :], yr[:, :, :], ACT.Gelu_apprx_tanh).then_inc(gelu_done, 1)
                    act.wait_ge(ratio_ready, 1)
                    act.activation(sg[:, :, :], sg[:, :, :], ACT.Sqrt, scale=2.0).then_inc(root_done, 1)
                elif what == "oturn":
                    for g in range(4):
                        act.wait_ge(o_turned, g + 1)
                        if g == 0:
                            act.wait_ge(s_qz, 1)
                        blk, d0 = g // 2, 4 * (g % 2)
                        act.activation(oT[:, d0:d0 + 4, blk * P:(blk + 1) * P],
                                       bank[4 + g][:, :].rearrange("p (d n) -> p d n", d=4), ACT.Copy)\
                            .then_inc(oT_ready, 1)
                elif what == "sample":
                    if n == 0:
                        for j in range(2):
                            act.wait_ge(s_kt, j + 1)
                            act.activation(kcT[:, 4 * j:4 * j + 4, :],
                                           bank[4 + j][:, :].rearrange("p (b n) -> p b n", b=4), ACT.Copy)\
                                .then_inc(s_kte, 1)
                    elif n == 1:
                        act.wait_ge(s_sm, 1)
                        act.activation(slog, slog, ACT.Exp).then_inc(s_ex, 1)
                        act.activation(srow[:, 1, :], srow[:, 1, :], ACT.Exp).then_inc(s_ex, 1)
                    elif n == 2:
                        act.wait_ge(s_ptt, 1)
                        act.activation(pTs, bank[4][:, 0:P].rearrange("p (b h) -> p b h", b=DECB), ACT.Copy)\
                            .then_inc(s_pte, 1)

            act.wait_ge(tile_evac, NT1)
            act.activation(ga[:, :, :], ga[:, :, :], ACT.Sigmoid).then_inc(gates_done, 1)
            act.activation(gb[:, :, :], gb[:, :, :], ACT.Sigmoid).then_inc(gates_done, 1)

            for g, (c0, w) in enumerate(((0, 512), (512, 512), (1024, 256))):
                act.wait_ge(pack_turned, g + 1)
                act.activation(rows[:, c0:c0 + w], bank[5 + g][0:20, 0:w], ACT.Copy).then_inc(rows_ready, 1)

            def root(t, ready, done):
                n = TILES[t][1]
                act.wait_ge(ready, t + 1)
                act.activation(sd[0:n, t:t + 1], mv[0:n, t, 1:2], ACT.Sqrt, bias=epsc[0:n, :]).then_inc(done, 1)

            def exponentials(t):
                n = TILES[t][1]
                act.wait_ge(top_ready, t + 1)
                act.activation(rt[0:n, 5, t, :], lgt[0:n, t, :], ACT.Exp, bias=rsm[0:n, 0, t:t + 1])\
                    .then_inc(exp_ready, 1)

            for t, (_, n) in enumerate(TILES):
                root(t, var_ready, sd_ready)
                for g in ((0, 1), (2, 3), (4,))[t]:
                    turned_x(g, TURN_TO[g], x1_turned, x1T_ready)
                act.activation(xh[0:n, t, :], xtok[0:n, t, :], ACT.Copy).then_inc(xh_ready, 1)
                if t == 1:
                    exponentials(0)
                    exponentials(1)
            exponentials(2)
            act.activation(warm[:, :], warm[:, :], ACT.Sigmoid)
            def split(i, b):
                c = NCH + i
                act.wait_ge(split_free, b * 12 + (i + 1))
                act.wait_ge(loaded[c % RING], b * PER_BLOCK[i] + LOADED0[i])
                act.activation(hi[:, i % SPLITS, :], slot(c), ACT.Copy).then_inc(hi_ready, 1)

            split(0, 0)
            act.wait_ge(table_ready, 1)
            blocks = act.value_load(tablei[0:1, NB:NB + 1], min_val=NE, max_val=NB)

            def take_gather(count):
                act.wait_ge(gathered, count)
                for h in range(2):
                    ins = act.activation(gx[:, h * 512:(h + 1) * 512], bank[6 + h][:, :], ACT.Copy)
                ins.then_inc(gx_ready, 1)

            def take_turned(count):
                act.wait_ge(gx_turned, count)
                for h in range(2):
                    ins = act.activation(xg[:, 4 * h:4 * h + 4, :],
                                         bank[6 + h][:, :].rearrange("p (d n) -> p d n", d=4), ACT.Copy)
                ins.then_inc(xg_ready, 1)

            def take_gt(count):
                act.wait_ge(gated_turned, count)
                act.activation(gt[:, :], bank[7][:, 0:T], ACT.Copy).then_inc(gt_ready, 1)

            def take_y(before):
                act.wait_ge(split_free, before * 12 + SPLITS)
                for j in range(2):
                    act.activation(ysb[:, j * 512:(j + 1) * 512], bank[4 + j][:, :], ACT.Copy).then_inc(y_ready, 1)

            take_gather(1)
            take_turned(1)
            with act.Fori(0, blocks) as b:

                def take_up(j):
                    act.wait_ge(split_free, b * 12 + (SPLITS + 2 * j + 2))
                    if j >= 2:
                        act.wait_ge(hT_done, b * NG + (j - 1))
                    act.activation(hsb[:, j % 2, :], bank[j % 2][:, :], ACT.Copy).then_inc(up_taken, 1)

                def sigmoid(j):
                    act.wait_ge(glu_ready, b * NG + (j + 1))
                    act.activation(sig[:, j % 2, :, :], glin[:, j % 2, 0:2, :], ACT.Sigmoid, scale=SALPHA)\
                        .then_inc(sig_ready, 1)

                split(1, b)
                split(2, b)
                split(3, b)
                take_y(b)
                split(4, b)
                take_up(0)
                split(5, b)
                take_gt(b + 2)
                split(6, b)
                take_up(1)
                split(7, b)
                sigmoid(0)
                split(8, b)
                take_up(2)
                split(9, b)
                sigmoid(1)
                split(10, b)
                sigmoid(2)
                take_up(3)
                split(11, b)
                take_gather(b + 2)
                sigmoid(3)
                split(0, b + 1)
                take_turned(b + 2)
            take_y(blocks)
            take_gt(blocks + 2)
            for t in range(3):
                root(t, var2_ready, sd2_ready)

        @block.tensor
        def _(pe):
            pe.wait_ge(s_const, 16)
            pe.wait_ge(s_x, 48)

            def turn_x(g, to, done):
                if g < 4:
                    t, d0 = g // 2, 4 * (g % 2)
                    for j in range(4):
                        last = pe.transpose(bank[to][:, j * P:(j + 1) * P], xtok[:, t, (d0 + j) * P:(d0 + j + 1) * P],
                                            ident)
                else:
                    for d in range(KD):
                        last = pe.transpose(bank[to][:, d * 8:d * 8 + 8], xtok[0:DECB, 2, d * P:(d + 1) * P],
                                            ident[0:DECB, 0:DECB])
                last.then_inc(done, 1)

            for g in range(5):
                turn_x(g, g, x_turned)
            pe.wait_ge(xT_ready, 5)

            def scores(h):
                g, par_ = h // GROUP, h % 2
                if h == 0:
                    pe.wait_ge(kz_ready, 1)
                    pe.wait_ge(tile_evac, 10)
                if h >= 2:
                    pe.wait_ge(scores_taken, h - 1)
                for blk in range(2):
                    last = pe.matmul(bank[4 + h % 2][:, blk * 256:(blk + 1) * 256],
                                     qT[:, h // 2, blk * P:(blk + 1) * P],
                                     kz[:, 2 * g + par_, blk * P:blk * P + 256], start=True, stop=True)
                last.then_inc(scored, 1)

            def turn_probs(h):
                pe.wait_ge(probs_ready, h + 1)
                if h >= 1:
                    pe.wait_ge(pT_ready, h)
                for j, (blk, part) in enumerate(((0, 1), (1, 0), (1, 1))):
                    last = pe.transpose(bank[6][:, j * P:(j + 1) * P], lg[:, h % 2, blk, part * P:(part + 1) * P],
                                        ident)
                last.then_inc(probs_turned, 1)

            def weigh(h):
                g = h // GROUP
                pe.wait_ge(pT_ready, h + 1)
                if h >= 1:
                    pe.wait_ge(o_ready, h)
                o = bank[7][:, (h % 4) * P:(h % 4 + 1) * P]
                vv = lambda blk: vtok[:, blk, g * HD:(g + 1) * HD]
                pe.matmul(o[:, 0:HD], pT[:, h % 2, 0:P], vv(0), start=True, stop=True)
                pe.matmul(o[:, HD:P], pT[:, h % 2, P:2 * P], vv(0), start=True, stop=False)
                pe.matmul(o[:, HD:P], pT[:, h % 2, 2 * P:3 * P], vv(1), start=False, stop=True).then_inc(pv_done, 1)

            seen = set()
            for what, n in order:
                if what == "tile":
                    name, idx, c, half = tiles[n]
                    if c not in seen:
                        chunk_ready(pe, c)
                        seen.add(c)
                    if n >= 4:
                        pe.wait_ge(tile_evac, n - 3)
                    if name in ("r", "i"):
                        pe.wait_ge(conv_ready, idx + 1 if name == "r" else RT)
                        last = pe.matmul(bank[n % 4][:, 0:T], slot(c)[:, idx * P:(idx + 1) * P], xc[:, idx, :],
                                         start=True, stop=True)
                    else:
                        w = slot(c).rearrange("p (k n) -> p k n", k=KD)
                        for k in range(KD):
                            last = pe.matmul(bank[n % 4][:, 0:T], w[:, k, half * P:(half + 1) * P], xT[:, k, :],
                                             start=k == 0, stop=k == KD - 1)
                    last.then_inc(tile_done, 1)
                elif what == "parturn":
                    pe.wait_ge(s_par, 16 * 7)
                    pe.transpose(bank[5][:, 0:80], parr[:, :], ident[0:80, 0:80]).then_inc(par_turned, 1)
                    for k in range(RT):
                        last = pe.transpose(bank[6][:, k * 32:(k + 1) * 32], statr[:, k * P:(k + 1) * P],
                                            ident[0:32, 0:32])
                    last.then_inc(par_turned, 1)
                elif what == "kvturn":
                    pe.wait_ge(tile_evac, 2)
                    pe.wait_ge(par_ready, 2)
                    for blk in range(2):
                        pe.transpose(bank[6][:, blk * P:(blk + 1) * P], vT[:, blk * P:(blk + 1) * P], ident)
                    pe.transpose(bank[6][:, 256:384], kT[:, P:2 * P], ident)
                    pe.transpose(bank[7][0:DECB, 0:P], kT[:, SEQ:T], ident)
                    pe.transpose(bank[7][0:DECB, P:2 * P], vT[:, SEQ:T], ident).then_inc(kv_turned, 1)
                elif what == "step":
                    if n == 0:
                        pe.wait_ge(kv_ready, 3)
                    if n < NH:
                        scores(n)
                    if 0 <= n - 1 < NH:
                        turn_probs(n - 1)
                    if 0 <= n - 2 < NH:
                        weigh(n - 2)
                elif what == "oturn":
                    pe.wait_ge(o_norm, 2)
                    pe.wait_ge(s_os, 1)
                    for g in range(4):
                        blk, d0 = g // 2, 4 * (g % 2)
                        for j in range(4):
                            last = pe.transpose(bank[4 + g][:, j * P:(j + 1) * P], otok[:, blk, (d0 + j) * P:(d0 + j + 1) * P],
                                                ident)
                        last.then_inc(o_turned, 1)
                elif what == "sample":
                    if n == 0:
                        pe.wait_ge(s_new, 32)
                        pe.wait_ge(scores_taken, NH)
                        for j in range(2):
                            for b in range(4):
                                last = pe.transpose(bank[4 + j][:, b * P:(b + 1) * P], kc[:, 4 * j + b, :], ident)
                            last.then_inc(s_kt, 1)
                    elif n == 1:
                        pe.wait_ge(s_kte, 2)
                        pe.wait_ge(s_qz, 1)
                        pe.wait_ge(o_ready, NH)
                        for b in range(DECB):
                            last = pe.matmul(bank[6 + b // 4][0:NH, (b % 4) * P:(b % 4 + 1) * P], qz[:, b, :],
                                             kcT[:, b, :], start=True, stop=True)
                        last.then_inc(s_sc, 1)
                    elif n == 2:
                        pe.wait_ge(s_pn, 1)
                        for b in range(DECB):
                            last = pe.transpose(bank[4][:, b * NH:(b + 1) * NH], slog[:, b, :], ident[0:NH, 0:NH])
                        last.then_inc(s_ptt, 1)
                    else:
                        pe.wait_ge(s_pte, 1)
                        for b in range(DECB):
                            last = pe.matmul(bank[5][:, b * NH:(b + 1) * NH], vc[:, b, :], pTs[:, b, :],
                                             start=True, stop=True)
                        last.then_inc(s_pv, 1)

            pe.wait_ge(oT_ready, 4)
            for m in range(16):
                if m < 4:
                    pe.wait_ge(tile_evac, NT1)
                else:
                    pe.wait_ge(out_evac, m - 3)
                if m < 8:
                    c, half = CH_AO + m // 2, m % 2
                    w, src, kk = slot(c).rearrange("p (k n) -> p k n", k=KD), oT, KD
                else:
                    c, half = CH_RO + m - 8, 0
                    w, src, kk = slot(c)[:, 0:DR].rearrange("p (k n) -> p k n", k=RT), yr, RT
                    pe.wait_ge(y_rnn_ready, 1)
                chunk_ready(pe, c)
                for k in range(kk):
                    last = pe.matmul(bank[m % 4][:, 0:T], w[:, k, half * P:(half + 1) * P], src[:, k, :],
                                     start=k == 0, stop=k == kk - 1)
                last.then_inc(out_done, 1)
            pe.wait_ge(pack_ready, 1)
            pe.wait_ge(oT_ready, 4)
            for g, (n0, n1) in enumerate(((0, 4), (4, 8), (8, 10))):
                for n in range(n0, n1):
                    last = pe.transpose(bank[5 + g][0:20, (n - n0) * P:(n - n0 + 1) * P], pack[:, n, :], ident)
                last.then_inc(pack_turned, 1)
            mix = [(bank[4], bank[5]), (bank[6], bank[7]), (bank[2], bank[3])]
            pe.wait_ge(merged_ready, 8)
            pe.wait_ge(rows_ready, 3)

            def mix_tile(t, k0, k1):
                t0, n = TILES[t]
                for k in range(k0, k1):
                    chunk_ready(pe, CH_OUT + k // 2)
                    w = slot(CH_OUT + k // 2).rearrange("p (k n) -> p k n", k=2)
                    for h in range(2):
                        last = pe.matmul(mix[t][h][0:n, :], ga[:, k, t0:t0 + n],
                                         w[:, k % 2, h * 512:(h + 1) * 512], start=k == 0, stop=k == KD - 1)
                if k1 == KD:
                    last.then_inc(mix_done, 1)

            def logits(t):
                t0, n = TILES[t]
                pe.wait_ge(x1T_ready, (2, 4, 5)[t])
                for k in range(KD):
                    last = pe.matmul(bank[LOGITS[t]][0:n, 0:NE], xT[:, k, t0:t0 + n], wr[:, k, :],
                                     start=k == 0, stop=k == KD - 1)
                last.then_inc(logits_done, 1)

            mix_tile(0, 0, KD)
            mix_tile(1, 0, KD)
            pe.wait_ge(x1_ready, 1)
            turn_x(0, TURN_TO[0], x1_turned)
            turn_x(1, TURN_TO[1], x1_turned)
            mix_tile(2, 0, KD // 2)
            pe.wait_ge(s_bd, 32)
            logits(0)
            pe.wait_ge(x1_ready, 2)
            turn_x(2, TURN_TO[2], x1_turned)
            turn_x(3, TURN_TO[3], x1_turned)
            mix_tile(2, KD // 2, KD - 2)
            logits(1)
            mix_tile(2, KD - 2, KD)
            pe.wait_ge(x1_ready, 3)
            turn_x(4, TURN_TO[4], x1_turned)
            logits(2)
            pe.sem_inc(split_free, SPLITS)
            pe.wait_ge(mask_ready, 3)
            mask = lambda t, n: rt[0:n, 4, t, :]
            for t, (t0, n) in enumerate(TILES):
                for u in range(t):
                    pe.matmul(bank[6][0:n, t * NE:(t + 1) * NE], ones[:, 0:n], mask(u, P), start=u == 0, stop=False)
                pe.matmul(bank[6][0:n, t * NE:(t + 1) * NE], const[0:n, C_TRI:C_TRI + n], mask(t, n),
                          start=t == 0, stop=True)
            for t, (t0, n) in enumerate(TILES):
                last = pe.matmul(bank[7][0:NE, 0:1], mask(t, n), ones[0:n, 0:1], start=t == 0, stop=t == 2)
            last.then_inc(count_done, 1)
            pe.wait_ge(over_ready, 1)
            pe.matmul(bank[7][0:NE, 8:9], const[0:NE, C_TRI:C_TRI + NE], ov[:, 1:2], start=True, stop=True)
            pe.matmul(bank[7][0:1, 16:17], ov[:, 1:2], ones[0:NE, 0:1], start=True, stop=True).then_inc(start_done, 1)
            pe.wait_ge(route_ready, 3)
            for t, (t0, n) in enumerate(TILES):
                pe.transpose(bank[0][0:NE, t0:t0 + n], rt[0:n, 6, t, :], ident[0:n, 0:n])
                last = pe.transpose(bank[1][0:NE, t0:t0 + n], rt[0:n, 7, t, :], ident[0:n, 0:n])
            last.then_inc(route_turned, 1)
            pe.wait_ge(routeT_ready, 1)
            for t, (t0, n) in enumerate(TILES):
                pe.matmul(bank[2][0:n, t * NB:(t + 1) * NB], posmT[:, t0:t0 + n], selm[:, :], start=True, stop=False)
                pe.matmul(bank[2][0:n, t * NB:(t + 1) * NB], ones[0:NE, 0:n], negj[:, :], start=False, stop=True)
                pe.matmul(bank[3][0:n, t * NB:(t + 1) * NB], gateT[:, t0:t0 + n], selm[:, :], start=True, stop=True)
            last = pe.matmul(bank[7][0:1, 32:32 + NB], const[0:NE, C_EIDX:C_EIDX + 1], selm[:, :], start=True, stop=True)
            last.then_inc(table_done, 1)

            def biases(half):
                chunk_ready(pe, CH_BUP)
                for f in range(8):
                    last = pe.matmul(bank[2 + half][:, f * NB:(f + 1) * NB],
                                     slot(CH_BUP)[0:NE, (8 * half + f) * P:(8 * half + f + 1) * P], selm[:, :],
                                     start=True, stop=True)
                last.then_inc(table_done, 1)

            pe.wait_ge(table_ready, 1)
            blocks = pe.value_load(tablei[0:1, NB:NB + 1], min_val=NE, max_val=NB)

            def gather(h):
                for part, x in ((0, xh), (1, xl)):
                    for t, (_, n) in enumerate(TILES):
                        last = pe.matmul(bank[6 + h][:, :],
                                         onehot[0:n, t, (1 - part) * CAP:(1 - part) * CAP + P],
                                         x[0:n, t, h * 512:(h + 1) * 512],
                                         start=part == 0 and t == 0, stop=part == 1 and t == 2)
                if h == 1:
                    last.then_inc(gathered, 1)

            def turn_gathered(count):
                pe.wait_ge(gx_ready, count)
                for d in range(KD):
                    last = pe.transpose(bank[6 + d // 4][:, (d % 4) * P:(d % 4 + 1) * P], gx[:, d * P:(d + 1) * P],
                                        ident)
                last.then_inc(gx_turned, 1)

            def turn_gates():
                for t, (t0, n) in enumerate(TILES):
                    last = pe.transpose(bank[7][:, t0:t0 + n], gated[0:n, t, :], ident[0:n, 0:n])
                last.then_inc(gated_turned, 1)

            def combine(tiles_, added_before):
                for d in tiles_:
                    if d >= 2:
                        pe.wait_ge(added, added_before + (d - 1))
                    pe.matmul(bank[CBANK[d % 2]][:, 0:T], ysb[:, d * P:(d + 1) * P], gt[:, :], start=True, stop=True)\
                        .then_inc(combined, 1)

            pe.sem_inc(gated_turned, 1)
            pe.wait_ge(onehot_ready, 1)
            pe.wait_ge(xh_ready, 3)
            pe.wait_ge(xl_ready, 3)
            gather(0)
            gather(1)
            biases(0)
            turn_gathered(1)
            biases(1)
            pe.wait_ge(y_cleared, 2)
            pe.wait_ge(bup_ready, 2)
            with pe.Fori(0, blocks) as b:
                def up(i):
                    j, half = i // 2, i % 2
                    if j >= 2 and half == 0:
                        pe.wait_ge(up_taken, b * NG + (j - 1))
                    h_ = hi[:, i % SPLITS, :].rearrange("p (k n) -> p k n", k=4)
                    l_ = lo[:, i % SPLITS, :].rearrange("p (k n) -> p k n", k=4)
                    pe.wait_ge(hi_ready, b * 12 + (i + 1))
                    for k in range(4):
                        pe.matmul(bank[j % 2][:, :], xg[:, 4 * half + k, :], h_[:, k, :],
                                  start=half == 0 and k == 0, stop=False)
                    low_ready(pe, i, b)
                    for k in range(4):
                        last = pe.matmul(bank[j % 2][:, :], xg[:, 4 * half + k, :], l_[:, k, :],
                                         start=False, stop=half == 1 and k == 3)
                    last.then_inc(split_free, 1)

                def down(i):
                    pe.wait_ge(at_ready, b * NG + (i - UPC + 1))
                    for part, src in ((0, hi), (1, lo)):
                        if part == 0:
                            pe.wait_ge(hi_ready, b * 12 + (i + 1))
                        else:
                            low_ready(pe, i, b)
                        for kk in range(2):
                            k = 2 * (i - UPC) + kk
                            for n in range(2):
                                last = pe.matmul(bank[4 + n][:, :], at[:, k, :],
                                                 src[:, i % SPLITS, kk * D + n * 512:kk * D + (n + 1) * 512],
                                                 start=part == 0 and k == 0, stop=part == 1 and k == KD - 1)
                    last.then_inc(split_free, 1)

                def turn_up(j):
                    pe.wait_ge(up_taken, b * NG + (j + 1))
                    pe.wait_ge(hT_taken, b * NG + (j + 1))
                    for f in range(4):
                        last = pe.transpose(bank[2 + j % 2][:, f * P:(f + 1) * P], hsb[:, j % 2, f * P:(f + 1) * P],
                                            ident)
                    last.then_inc(hT_done, 1)

                pe.wait_ge(xg_ready, b + 1)
                up(0)
                up(1)
                pe.wait_ge(gated_ready, b + 1)
                turn_gates()
                up(2)
                turn_up(0)
                pe.wait_ge(gt_ready, b + 1)
                pe.wait_ge(y_ready, b * 2 + 2)
                combine((0, 1), b * 8)
                up(3)
                combine((2,), b * 8)
                up(4)
                turn_up(1)
                combine((3, 4), b * 8)
                up(5)
                combine((5, 6), b * 8)
                up(6)
                turn_up(2)
                combine((7,), b * 8)
                pe.wait_ge(onehot_ready, b + 2)
                pe.wait_ge(added, b * 8 + 7)
                gather(0)
                up(7)
                pe.wait_ge(added, b * 8 + 8)
                gather(1)
                turn_up(3)
                down(8)
                turn_gathered(b + 2)
                down(9)
                down(10)
                down(11)

            pe.wait_ge(gated_ready, blocks + 1)
            pe.wait_ge(xg_ready, blocks + 1)
            turn_gates()
            pe.wait_ge(biases_loaded, 16)
            pe.wait_ge(added, blocks * 8)

            def final(t, h):
                return bank[2 * t + h][0:TILES[t][1], :]

            def sums(t):
                t0, n = TILES[t]
                for h in range(2):
                    pe.matmul(final(t, h), gateT[:, t0:t0 + n], bdown[:, h * 512:(h + 1) * 512], start=True, stop=False)
                    for j in range(4):
                        pe.matmul(final(t, h)[:, j * P:(j + 1) * P], yT[:, 4 * h + j, t0:t0 + n], ident,
                                  start=False, stop=False)

            def last_block(t):
                t0, n = TILES[t]
                for h in range(2):
                    last = pe.matmul(final(t, h), gt[:, t0:t0 + n], ysb[:, h * 512:(h + 1) * 512],
                                     start=False, stop=True)
                last.then_inc(final_done, 1)

            sums(0)
            pe.wait_ge(gt_ready, blocks + 1)
            pe.wait_ge(y_ready, blocks * 2 + 2)
            last_block(0)
            sums(1)
            last_block(1)
            sums(2)
            last_block(2)

        @block.vector
        def _(dve):
            steps = [0]

            def link(ins):
                steps[0] += 1
                ins.then_inc(v, 1)
                dve.wait_ge(v, steps[0])

            link(dve.memset(warm[:, :], 0.0))
            link(dve.memset(epsc[:, :], EPS))
            link(dve.memset(kz[:, :, :], 0.0))
            link(dve.memset(xrp[:, :, 0:3], 0.0))
            link(dve.memset(posb[:, :, :], -1.0))
            link(dve.memset(gateb[:, :, :], 0.0))
            link(dve.memset(ones[:, :], 1.0))
            dve.wait_ge(par_turned, 2)
            dve.tensor_copy(par[:, :], bank[5][:, 0:80]).then_inc(par_ready, 1)
            dve.tensor_copy(stat[:, :, :], bank[6][:, 0:320].rearrange("p (n c) -> p n c", n=RT)).then_inc(par_ready, 1)
            dve.wait_ge(par_ready, 2)
            lam = par[:, 70:80]
            L = lambda i: lamt[:, i, :]
            link(dve.tensor_scalar(L(0), lam, -1.0, None, ALU.mult))
            dve.tensor_tensor(L(1), lam, L(0), ALU.max).then_inc(lam_in, 1)
            dve.wait_ge(lam_exp, 1)
            link(dve.tensor_scalar(L(3), L(2), 2.0, None, ALU.add))
            link(dve.reciprocal(L(3), L(3)))
            link(dve.tensor_tensor(L(3), L(2), L(3), ALU.mult))
            link(dve.tensor_tensor(L(4), L(3), L(3), ALU.mult))
            link(dve.memset(L(5), 1.0 / 19.0))
            for k in range(17, 0, -2):
                link(dve.tensor_tensor(L(5), L(5), L(4), ALU.mult))
                link(dve.tensor_scalar(L(5), L(5), 1.0 / k, None, ALU.add))
            link(dve.tensor_tensor(L(5), L(5), L(3), ALU.mult))
            link(dve.tensor_scalar(L(0), L(0), 0.0, None, ALU.max))
            link(dve.scalar_tensor_tensor(out=L(5), in0=L(5), scalar=2.0, in1=L(0), op0=ALU.mult, op1=ALU.add))
            link(dve.tensor_scalar(L(6), L(5), -8.0, None, ALU.mult))
            dve.tensor_scalar(L(7), L(5), 8.0, None, ALU.mult).then_inc(lam_ready, 1)

            dve.wait_ge(tile_evac, 2)
            for g in range(2):
                for q in range(2):
                    last = dve.tensor_copy(kz[q * 64:q * 64 + 64, 2 * g + q, P:P + SEQ], kT[g * 64:g * 64 + 64, 0:SEQ])
            last.then_inc(kz_ready, 1)
            dve.wait_ge(s_misc, 32)

            def softmax_head(h):
                dve.wait_ge(scored, h + 1)
                if h >= 2:
                    dve.wait_ge(probs_turned, h - 1)
                link(dve.scalar_tensor_tensor(out=lg[:, h % 2, :, :].rearrange("p b n -> p (b n)"),
                                              in0=const[:, C_DIST:C_DIST + 512], scalar=-slope(h),
                                              in1=bank[4 + h % 2][:, :], op0=ALU.mult, op1=ALU.add))
                dve.tensor_reduce(rmax[:, h % 2, :], lg[:, h % 2, :, :], AX.X, ALU.max).then_inc(scores_taken, 1)
                dve.wait_ge(scores_taken, h + 1)
                dve.tensor_scalar(negm[:, :, h], rmax[:, h % 2, :], sink[:, h:h + 1], -1.0, ALU.max, ALU.mult)\
                    .then_inc(max_ready, 1)

            def conv(n):
                xr_tile = 10 + n
                dve.wait_ge(tile_evac, xr_tile + 1)
                w = lambda j: par[:, j * RT + n:j * RT + n + 1]
                cb = par[:, 40 + n:41 + n]
                o, os_ = xc[:, n, 0:SEQ], xc[:, n, SEQ:T]
                dve.tensor_scalar(o, xrp[:, n, 0:SEQ], w(0), cb, ALU.mult, ALU.add)
                link(dve.tensor_scalar(os_, stat[:, n, 0:24:3], w(0), cb, ALU.mult, ALU.add))
                for j in range(1, CONV):
                    dve.scalar_tensor_tensor(out=o, in0=xrp[:, n, j:j + SEQ], scalar=w(j), in1=o,
                                             op0=ALU.mult, op1=ALU.add)
                    src = stat[:, n, j:24:3] if j < 3 else xrs[:, n, :]
                    ins = dve.scalar_tensor_tensor(out=os_, in0=src, scalar=w(j), in1=os_, op0=ALU.mult, op1=ALU.add)
                    if j < CONV - 1:
                        link(ins)
                    else:
                        ins.then_inc(conv_ready, 1)

            def recurrence():
                dve.wait_ge(tanh_done, RT)
                link(dve.tensor_copy(pack[:, :, 0:3], xrp[:, :, SEQ:SEQ + 3]))
                link(dve.tensor_scalar(den[:, :, :], sg[:, :, :], 1.0, None, ALU.add))
                link(dve.reciprocal(den[:, :, :], den[:, :, :]))
                dve.tensor_tensor(sg[:, :, :], sg[:, :, :], den[:, :, :], ALU.mult).then_inc(ratio_ready, 1)
                dve.wait_ge(gates_done, 2)
                link(dve.tensor_tensor(ig[:, :, :], ig[:, :, :], xc[:, :, :], ALU.mult))
                dve.wait_ge(root_done, 1)
                link(dve.tensor_tensor(ig[:, :, :], ig[:, :, :], sg[:, :, :], ALU.mult))
                dve.wait_ge(decay_done, RT)
                for n in range(RT):
                    dve.tensor_tensor_scan(hrec[:, n, 0:SEQ], rg[:, n, 0:SEQ], ig[:, n, 0:SEQ], 0.0, ALU.mult, ALU.add)
                link(dve.tensor_tensor(hrec[:, :, SEQ:T], rg[:, :, SEQ:T], stat[:, :, 24:32], ALU.mult))
                link(dve.tensor_tensor(hrec[:, :, SEQ:T], hrec[:, :, SEQ:T], ig[:, :, SEQ:T], ALU.add))
                dve.wait_ge(gelu_done, 1)
                dve.tensor_tensor(yr[:, :, :], yr[:, :, :], hrec[:, :, :], ALU.mult).then_inc(y_rnn_ready, 1)
                dve.tensor_copy(pack[:, :, 3:4], hrec[:, :, SEQ - 1:SEQ])
                dve.tensor_copy(pack[:, :, 4:12], xrs[:, :, :])
                dve.tensor_copy(pack[:, :, 12:20], hrec[:, :, SEQ:T]).then_inc(pack_ready, 1)

            for what, n in order:
                if what == "step" and n < NH:
                    softmax_head(n)
                    if n < RT:
                        conv(n)
                elif what == "sample" and n == 0:
                    link(dve.memset(qz, 0.0))
                    for g in range(2):
                        for q in range(2):
                            src = qT[q * 64:q * 64 + 64, 4 * g:4 * g + 4, SEQ:T].rearrange("p f b -> p b f")
                            last = dve.tensor_copy(qz[g * 64:g * 64 + 64, :, 8 * g + q:8 * g + 8:2], src)
                    last.then_inc(s_qz, 1)
                elif what == "sample" and n == 1:
                    dve.wait_ge(s_sc, 1)
                    dist = const[0:NH, C_TDIST:C_TDIST + P].unsqueeze(1).broadcast_to([NH, 4, P])
                    for j in range(2):
                        ins = dve.scalar_tensor_tensor(out=slog[:, 4 * j:4 * j + 4, :], in0=dist,
                                                       scalar=const[0:NH, C_SLOPE:C_SLOPE + 1],
                                                       in1=bank[6 + j][0:NH, :].rearrange("p (b n) -> p b n", b=4),
                                                       op0=ALU.mult, op1=ALU.add)
                    link(ins)
                    link(dve.tensor_reduce(srow[:, 0, :], slog, AX.X, ALU.max))
                    link(dve.tensor_scalar(srow[:, 0, :], srow[:, 0, :], sinkc[:, 0:1], None, ALU.max))
                    dve.tensor_scalar(srow[:, 1, :], srow[:, 0, :], -1.0, sinkc[:, 0:1], ALU.mult, ALU.add)
                    dve.tensor_tensor(slog, slog, srow[:, 0, :].unsqueeze(2).broadcast_to([NH, DECB, P]),
                                      ALU.subtract).then_inc(s_sm, 1)
                    dve.wait_ge(s_ex, 2)
                    link(dve.tensor_reduce(srow[:, 2, :], slog, AX.X, ALU.add))
                    link(dve.tensor_tensor(srow[:, 2, :], srow[:, 2, :], srow[:, 1, :], ALU.add))
                    link(dve.reciprocal(srow[:, 3, :], srow[:, 2, :]))
                    dve.tensor_tensor(slog, slog, srow[:, 3, :].unsqueeze(2).broadcast_to([NH, DECB, P]),
                                      ALU.mult).then_inc(s_pn, 1)
                elif what == "sample" and n == 3:
                    dve.wait_ge(s_pv, 1)
                    ps = bank[5][:, 0:P].rearrange("p (b h) -> p b h", b=DECB)
                    for g in range(2):
                        for q in range(2):
                            dst = oT[q * 64:q * 64 + 64, 4 * g:4 * g + 4, SEQ:T].rearrange("p f b -> p b f")
                            last = dve.tensor_copy(dst, ps[g * 64:g * 64 + 64, :, 8 * g + q:8 * g + 8:2])
                    last.then_inc(s_os, 1)
                elif what == "gate" and n == 1:
                    recurrence()
                if what == "step" and n == NH + 1:
                    dve.wait_ge(probs_ready, NH)
                    dve.wait_ge(max_ready, NH)
                    dve.tensor_tensor(esk[:, :, :], negm[:, :, :],
                                      sink[:, :].unsqueeze(1).broadcast_to([P, 2, NH]), ALU.add).then_inc(den_in, 1)
                    dve.wait_ge(sinkexp, 1)
                    link(dve.tensor_tensor(esk[:, :, :], esk[:, :, :], rsum[:, :, :], ALU.add))
                    link(dve.reciprocal(esk[:, :, :], esk[:, :, :]))
                    dve.wait_ge(o_ready, NH)
                    for blk in range(2):
                        o = otok[:, blk, :].rearrange("p (h d) -> p h d", h=NH)
                        dve.tensor_tensor(o, o, esk[:, blk, :].unsqueeze(2).broadcast_to([P, NH, HD]), ALU.mult)\
                            .then_inc(o_norm, 1)

            dve.wait_ge(gates_done, 4)
            for m in range(16):
                dve.wait_ge(out_done, m + 1)
                ps = bank[m % 4][:, 0:T]
                if m < 8:
                    dve.tensor_tensor(ga[:, m, :], ga[:, m, :], ps, ALU.mult).then_inc(out_evac, 1)
                else:
                    f = m - 8
                    dve.tensor_tensor(gb[:, f, :], gb[:, f, :], ps, ALU.mult).then_inc(out_evac, 1)
                    dve.wait_ge(out_evac, m + 1)
                    dve.tensor_tensor(ga[:, f, :], ga[:, f, :], gb[:, f, :], ALU.add).then_inc(merged_ready, 1)

            def moments(t, psums, var_sem):
                n = TILES[t][1]
                for h in range(2):
                    x = xtok[0:n, t, h * 512:(h + 1) * 512]
                    link(dve.scalar_tensor_tensor(out=x, in0=x, scalar=ALPHA, in1=psums[h][0:n, :],
                                                  op0=ALU.mult, op1=ALU.add))
                    link(dve.bn_stats(stats[0:n, t, h * 6:h * 6 + 6], x))
                dve.bn_aggr(mv[0:n, t, :], stats[0:n, t, :]).then_inc(var_sem, 1)

            def normalise(t, sd_sem, g_row, b_row, done):
                n = TILES[t][1]
                x = xtok[0:n, t, :]
                dve.wait_ge(sd_sem, t + 1)
                link(dve.reciprocal(rstd[0:n, t:t + 1], sd[0:n, t:t + 1]))
                ins = dve.tensor_scalar(x, x, mv[0:n, t, 0:1], rstd[0:n, t:t + 1], ALU.subtract, ALU.mult)
                if g_row is None:
                    ins.then_inc(done, 1)
                    return
                link(ins)
                link(dve.tensor_tensor(x, x, g_row[0:n, :], ALU.mult))
                dve.tensor_tensor(x, x, b_row[0:n, :], ALU.add).then_inc(done, 1)

            R = lambda i, t, n: rt[0:n, i, t, :]

            def select(t):
                n = TILES[t][1]
                dve.wait_ge(logits_done, t + 1)
                l = lgt[0:n, t, :]
                v4 = m8[0:n, t, TOPK - 1:TOPK]
                link(dve.tensor_tensor(l, bank[LOGITS[t]][0:n, 0:NE], brb[0:n, :], ALU.add))
                link(dve.max(m8[0:n, t, :], l))
                dve.tensor_scalar(rsm[0:n, 0, t:t + 1], m8[0:n, t, 0:1], -1.0, None, ALU.mult).then_inc(top_ready, 1)
                dve.tensor_scalar(R(1, t, n), l, v4, None, ALU.is_equal)
                link(dve.tensor_scalar(R(0, t, n), l, v4, None, ALU.is_gt))
                link(dve.tensor_reduce(rsm[0:n, 1, t:t + 1], R(0, t, n), AX.X, ALU.add))
                link(dve.tensor_scalar(rsm[0:n, 1, t:t + 1], rsm[0:n, 1, t:t + 1], -1.0, float(TOPK),
                                       ALU.mult, ALU.add))
                link(dve.tensor_tensor_scan(R(2, t, n), ones[0:n, 0:NE], R(1, t, n), 0.0, ALU.mult, ALU.add))
                link(dve.scalar_tensor_tensor(out=R(3, t, n), in0=R(2, t, n), scalar=rsm[0:n, 1, t:t + 1],
                                              in1=R(1, t, n), op0=ALU.is_le, op1=ALU.mult))
                dve.tensor_tensor(R(4, t, n), R(0, t, n), R(3, t, n), ALU.add).then_inc(mask_ready, 1)

            def softmax(t):
                n = TILES[t][1]
                dve.wait_ge(mask_ready, t + 1)
                dve.wait_ge(exp_ready, t + 1)
                link(dve.tensor_tensor(R(5, t, n), R(5, t, n), R(4, t, n), ALU.mult))
                link(dve.tensor_reduce(rsm[0:n, 2, t:t + 1], R(5, t, n), AX.X, ALU.add))
                link(dve.reciprocal(rsm[0:n, 3, t:t + 1], rsm[0:n, 2, t:t + 1]))
                link(dve.tensor_scalar(R(7, t, n), R(5, t, n), rsm[0:n, 3, t:t + 1], None, ALU.mult))

            def low_tokens(t):
                n = TILES[t][1]
                dve.wait_ge(xh_ready, t + 1)
                dve.tensor_tensor(xl[0:n, t, :], xtok[0:n, t, :], xh[0:n, t, :].bitcast(F32), ALU.subtract)\
                    .then_inc(xl_ready, 1)

            chunk_ready(dve, CH_LN)
            dve.wait_ge(s_bd, 32)
            mixed = [(bank[4], bank[5]), (bank[6], bank[7]), (bank[2], bank[3])]
            for t in range(3):
                dve.wait_ge(mix_done, t + 1)
                moments(t, mixed[t], var_ready)
                normalise(t, sd_ready, slot(CH_LN)[:, 0:D], slot(CH_LN)[:, D:2 * D], x1_ready)
                if t == 1:
                    select(0)
                    dve.memset(onehot[:, :, :].bitcast(F32), 0.0)
                    low_tokens(0)
                    select(1)
            softmax(0)
            softmax(1)
            select(2)
            softmax(2)
            dve.wait_ge(count_done, 1)
            count = bank[7][0:NE, 0:1]
            link(dve.tensor_scalar(ov[:, 2:3], count, float(CAP), None, ALU.is_gt))
            for j in range(2, 5):
                src, dst = (j, j + 1) if j < 4 else (4, 1)
                ins = dve.scalar_tensor_tensor(out=ov[:, dst:dst + 1], in0=count, scalar=float(j * CAP),
                                               in1=ov[:, src:src + 1], op0=ALU.is_gt, op1=ALU.add)
                if j < 4:
                    link(ins)
                else:
                    ins.then_inc(over_ready, 1)
            for t, (_, n) in enumerate(TILES):
                link(dve.scalar_tensor_tensor(out=R(6, t, n), in0=bank[6][0:n, t * NE:(t + 1) * NE], scalar=BIG,
                                              in1=R(4, t, n), op0=ALU.add, op1=ALU.mult))
                dve.tensor_scalar(R(6, t, n), R(6, t, n), BIG, None, ALU.subtract).then_inc(route_ready, 1)
            dve.wait_ge(start_done, 1)
            dve.wait_ge(over_ready, 1)
            oi = const[0:NE, C_OV:C_OV + MAXOVER]
            link(dve.tensor_copy(ov[:, 5:6], bank[7][0:NE, 8:9]))
            link(dve.tensor_tensor(ov[:, 6:7], ov[:, 5:6], ov[:, 1:2], ALU.add))
            link(dve.tensor_scalar(ohw[:, 0, :], oi, ov[:, 5:6], None, ALU.is_ge))
            link(dve.scalar_tensor_tensor(out=ohw[:, 1, :], in0=oi, scalar=ov[:, 6:7], in1=ohw[:, 0, :],
                                          op0=ALU.is_lt, op1=ALU.mult))
            link(dve.tensor_scalar(ohw[:, 2, :], oi, ov[:, 5:6], None, ALU.subtract))
            link(dve.tensor_scalar(ohw[:, 2, :], ohw[:, 2, :], -float(CAP), -float(CAP), ALU.mult, ALU.add))
            dve.memset(negj[:, 0:NE], 0.0)
            dve.tensor_tensor(negj[:, NE:NB], ohw[:, 2, :], ohw[:, 1, :], ALU.mult)
            dve.tensor_copy(selm[:, 0:NE], ident[0:NE, 0:NE])
            dve.tensor_copy(selm[:, NE:NB], ohw[:, 1, :])
            dve.wait_ge(route_turned, 1)
            dve.tensor_copy(posmT[:, :], bank[0][0:NE, 0:T])
            dve.tensor_copy(gateT[:, :], bank[1][0:NE, 0:T]).then_inc(routeT_ready, 1)
            low_tokens(1)
            low_tokens(2)
            for y in range(2):
                dve.memset(bank[4 + y][:, :], 0.0).then_inc(y_cleared, 1)
            dve.wait_ge(table_done, 1)
            for t, (_, n) in enumerate(TILES):
                dve.tensor_copy(posb[0:n, 1:1 + NB, t], bank[2][0:n, t * NB:(t + 1) * NB])
                dve.tensor_copy(gateb[0:n, 1:1 + NB, t], bank[3][0:n, t * NB:(t + 1) * NB])
            dve.tensor_copy(tablei[0:1, 0:NB], bank[7][0:1, 32:32 + NB])
            link(dve.tensor_scalar(tablei[0:1, NB:NB + 1], bank[7][0:1, 16:17], float(NE), None, ALU.add))
            dve.wait_ge(s_out, 16 * N_OUT)

            def one_hot(col, done):
                for t, (_, n) in enumerate(TILES):
                    ins = dve.tensor_scalar(onehot[0:n, t, CAP:2 * CAP], iota[0:n, 0:CAP], posb[0:n, col, t], None, ALU.is_equal)
                ins.then_inc(done, 1)

            def gates(col, done):
                for t, (_, n) in enumerate(TILES):
                    ins = dve.tensor_scalar(gated[0:n, t, :], iota[0:n, :], posb[0:n, col, t], gateb[0:n, col, t],
                                            ALU.is_equal, ALU.mult)
                ins.then_inc(done, 1)

            def add(d, count):
                dve.wait_ge(combined, count)
                dve.tensor_tensor(yT[:, d, :], yT[:, d, :], bank[CBANK[d % 2]][:, 0:T], ALU.add)\
                    .then_inc(added, 1)

            one_hot(bass.ds(1, 1), onehot_ready)
            gates(bass.ds(0, 1), gated_ready)
            dve.sem_inc(hT_taken, 2)
            dve.sem_inc(table_ready, 1)
            dve.memset(yT[:, :, :], 0.0).then_inc(y_cleared, 1)
            dve.wait_ge(y_cleared, 3)
            dve.wait_ge(table_done, 3)
            for half in range(2):
                dst = bup[:, :, :].rearrange("p (j h f) n -> p j h f n", j=NG, h=2)[:, :, half, :, :]
                dve.tensor_scalar(dst, bank[2 + half][:, 0:8 * NB].rearrange("p (j f n) -> p j f n", j=NG, f=2),
                                  float(half), None, ALU.add)\
                    .then_inc(bup_ready, 1)
            dve.wait_ge(bup_ready, 2)
            blocks = dve.value_load(tablei[0:1, NB:NB + 1], min_val=NE, max_val=NB)

            def split(i, b):
                dve.wait_ge(hi_ready, b * 12 + (i + 1))
                dve.tensor_tensor(lo[:, i % SPLITS, :], slot(NCH + i), hi[:, i % SPLITS, :].bitcast(F32),
                                  ALU.subtract).then_inc(lo_ready, 1)

            split(0, 0)
            with dve.Fori(0, blocks) as b:
                inner = [0]

                def chain(ins):
                    inner[0] += 1
                    ins.then_inc(vm, 1)
                    dve.wait_ge(vm, b * CHAIN + inner[0])

                def clamp(j):
                    dve.wait_ge(hT_done, b * NG + (j + 1))
                    ps = bank[2 + j % 2][:, :].rearrange("p (f n) -> p f n", f=4)
                    o = glin[:, j % 2, :, :]
                    chain(dve.tensor_tensor(o, ps[:, :, 0:CAP],
                                            bup[:, 4 * j:4 * j + 4, bass.ds(b, 1)].broadcast_to([P, 4, CAP]), ALU.add))
                    dve.tensor_tensor(o, o, ps[:, :, CAP:P], ALU.add).then_inc(hT_taken, 1)
                    dve.wait_ge(hT_taken, b * NG + (j + 3))
                    dve.tensor_scalar(o[:, 0:2, :], o[:, 0:2, :], LIMIT, None, ALU.min).then_inc(glu_ready, 1)
                    dve.tensor_scalar(o[:, 2:4, :], o[:, 2:4, :], LIMIT + 1, None, ALU.min).then_inc(lin_ready, 1)

                def activate(j):
                    dve.wait_ge(sig_ready, b * NG + (j + 1))
                    dve.wait_ge(lin_ready, b * NG + (j + 1))
                    o = act_[:, j % 2, :, :]
                    high, low = at[:, 2 * j:2 * j + 2, 0:CAP], at[:, 2 * j:2 * j + 2, CAP:P]
                    chain(dve.tensor_tensor(o, glin[:, j % 2, 0:2, :], sig[:, j % 2, :, :], ALU.mult))
                    chain(dve.scalar_tensor_tensor(out=o, in0=glin[:, j % 2, 2:4, :], scalar=1.0 - LIMIT, in1=o,
                                                   op0=ALU.max, op1=ALU.mult))
                    chain(dve.tensor_copy(high, o))
                    dve.tensor_tensor(low, o, high.bitcast(F32), ALU.subtract).then_inc(at_ready, 1)

                def adds(*tiles_):
                    for d in tiles_:
                        add(d, b * 8 + (d + 1))

                split(1, b)
                split(3, b)
                split(4, b)
                split(5, b)
                clamp(0)
                adds(0, 1)
                dve.wait_ge(gathered, b + 1)
                one_hot(bass.ds(b + 2, 1), onehot_ready)
                adds(2)
                split(7, b)
                activate(0)
                clamp(1)
                adds(3, 4)
                split(8, b)
                adds(5)
                activate(1)
                adds(6)
                split(9, b)
                clamp(2)
                adds(7)
                activate(2)
                clamp(3)
                split(11, b)
                activate(3)
                split(0, b + 1)
                dve.wait_ge(gated_turned, b + 2)
                gates(bass.ds(b + 1, 1), gated_ready)
                assert inner[0] == CHAIN
            dve.wait_ge(loaded[NCH % RING], blocks * PER_BLOCK[0] + LOADED0[0])
            for t in range(3):
                dve.wait_ge(final_done, t + 1)
                moments(t, (bank[2 * t], bank[2 * t + 1]), var2_ready)
                if t < 2:
                    normalise(t, sd2_ready, None, None, normal_ready)
                else:
                    normalise(t, sd2_ready, ln2[:, 0:D], ln2[:, D:2 * D], fin_ready)


INS = ["x_prompt", "x_sample", "cache_k", "cache_v", "state_conv", "state_h", "w_in", "attn_sinks", "conv_w", "conv_b",
       "rg_wa", "rg_ba", "rg_wx", "rg_bx", "rg_lambda", "w_attn_out", "w_rnn_out", "w_out", "ln1_g", "ln1_b",
       "w_router", "b_router", "w_up", "b_up", "w_down", "b_down", "ln2_g", "ln2_b"]
OUTS = [("o_yp", (1, SEQ, D)), ("o_ys", (DECB, 1, D)), ("o_kp", (1, 1, WIN, NKV, HD)), ("o_vp", (1, 1, WIN, NKV, HD)),
        ("o_cp", (1, 1, CONV - 1, DR)), ("o_hp", (1, 1, DR)), ("o_ks", (1, DECB, WIN, NKV, HD)),
        ("o_vs", (1, DECB, WIN, NKV, HD)), ("o_cs", (1, DECB, CONV - 1, DR)), ("o_hs", (1, DECB, DR))]


def kernel(**inputs):
    import concourse.bacc as bacc
    from concourse.bass_utils import run_bass_kernel_spmd

    nc = bacc.Bacc("TRN2", target_bir_lowering=False, num_devices=1)
    arrays, aps = {}, {}
    for name in INS + ["consts"]:
        x = constants() if name == "consts" else np.ascontiguousarray(inputs[name])
        arrays["in_" + name] = x
        aps[name] = nc.dram_tensor("in_" + name, x.shape, mybir.dt.from_np(x.dtype), kind="ExternalInput").ap()
    for name, shape in OUTS:
        aps[name] = nc.dram_tensor("out_" + name, shape, F32, kind="ExternalOutput").ap()
    build(nc, aps)
    r = run_bass_kernel_spmd(nc, [arrays], core_ids=[0])
    return tuple(r.results[0]["out_" + name] for name, _ in OUTS)
```
